# Optimizing a Trainium2 kernel written in Bass

```python
import math
import jax
import jax.numpy as jnp
from jax import lax
import numpy as np
import jax, jax.numpy as jnp

D_MODEL = 1024
BATCH = 1
SEQ = 256
DEPTH = 2

NORM_EPS = 1e-6
D_FF = 2816
CONV_CH = 1024
CONV_WIDTH = 31
SSM_D_INNER = 1024
SSM_HEAD_DIM = 64
SSM_HEADS = SSM_D_INNER // SSM_HEAD_DIM
SSM_GROUPS = 2
SSM_STATE = 128
SSM_CONV_WIDTH = 4
SSM_CHUNK = 128
SSM_XBC = SSM_D_INNER + 2 * SSM_GROUPS * SSM_STATE
HYB_IN_COLS = 2 * CONV_CH + SSM_D_INNER + SSM_XBC + SSM_HEADS
HYB_MIX_WIDTH = CONV_CH + SSM_D_INNER
ATTN_HEAD_DIM = 64
ATTN_HEADS = 8
DILATED_PATTERNS = ((128, 1), (512, 4), (2048, 16))
ATTN_GROUPS = len(DILATED_PATTERNS)
ATTN_BLOCK = 128
ATTN_QKV_COLS = 3 * ATTN_GROUPS * ATTN_HEADS * ATTN_HEAD_DIM
ATTN_OUT_WIDTH = ATTN_HEADS * ATTN_HEAD_DIM
N_EVEN = (DEPTH + 1) // 2
N_ODD = DEPTH // 2


def rms_norm(x, g):
    xf = x.astype(jnp.float32)
    y = xf * lax.rsqrt(jnp.mean(xf * xf, axis=-1, keepdims=True) + NORM_EPS)
    return (y * g.astype(jnp.float32)).astype(x.dtype)

def layer_norm(x, g, b):
    xf = x.astype(jnp.float32)
    xc = xf - jnp.mean(xf, axis=-1, keepdims=True)
    y = xc * lax.rsqrt(jnp.mean(xc * xc, axis=-1, keepdims=True) + NORM_EPS)
    return (y * g.astype(jnp.float32) + b.astype(jnp.float32)).astype(x.dtype)

def swiglu(u, w1, w2):
    gate, up = jnp.split(u @ w1, 2, axis=-1)
    return (jax.nn.silu(gate) * up) @ w2

def causal_depthwise_conv(x, w, b):
    k = w.shape[0]
    y = lax.conv_general_dilated(x, w[:, None, :].astype(x.dtype), window_strides=(1,), padding=[(k - 1, 0)], dimension_numbers=('NWC', 'WIO', 'NWC'), feature_group_count=x.shape[-1])
    return y + b.astype(x.dtype)

def conformer_conv(u, w_dw, b_dw, ln_g, ln_b):
    val, gate = jnp.split(u, 2, axis=-1)
    hid = causal_depthwise_conv(val * jax.nn.sigmoid(gate), w_dw, b_dw)
    return jax.nn.silu(layer_norm(hid, ln_g, ln_b))

def segsum(a):
    t = a.shape[-1]
    strict = jnp.tril(jnp.ones((t, t), dtype=bool), -1)
    incl = jnp.tril(jnp.ones((t, t), dtype=bool), 0)
    ss = jnp.cumsum(jnp.where(strict, a[..., :, None], 0.0), axis=-2)
    return jnp.where(incl, ss, -jnp.inf)

def ssd_chunked(x, a, bm, cm):
    bsz, seq, heads, hd = x.shape
    groups, nst = bm.shape[2], bm.shape[3]
    rep = heads // groups
    nc = seq // SSM_CHUNK
    x = x.reshape(bsz, nc, SSM_CHUNK, groups, rep, hd)
    a = a.reshape(bsz, nc, SSM_CHUNK, groups, rep).transpose(0, 3, 4, 1, 2)
    bm = bm.reshape(bsz, nc, SSM_CHUNK, groups, nst)
    cm = cm.reshape(bsz, nc, SSM_CHUNK, groups, nst)
    a_cum = jnp.cumsum(a, axis=-1)
    decay_in = jnp.exp(segsum(a))
    cb = jnp.einsum('bclgn,bcsgn->bgcls', cm, bm)
    y_diag = jnp.einsum('bgrcls,bcsgrp->bclgrp', cb[:, :, None] * decay_in, x)
    decay_states = jnp.exp(a_cum[..., -1:] - a_cum)
    states = jnp.einsum('bcsgn,bgrcs,bcsgrp->bcgrpn', bm, decay_states, x)
    states = jnp.concatenate([jnp.zeros_like(states[:, :1]), states], axis=1)
    chunk_tot = jnp.pad(a_cum[..., -1], ((0, 0), (0, 0), (0, 0), (1, 0)))
    decay_chunk = jnp.exp(segsum(chunk_tot))
    states = jnp.einsum('bgrzc,bcgrpn->bzgrpn', decay_chunk, states)[:, :-1]
    y_off = jnp.einsum('bclgn,bcgrpn,bgrcl->bclgrp', cm, states, jnp.exp(a_cum))
    return (y_diag + y_off).reshape(bsz, seq, heads, hd)

def mamba2_ssd(z, xbc, dt_raw, conv_w, conv_b, dt_bias, a_log, d_skip, norm_g):
    bsz, seq, _ = z.shape
    xbc = jax.nn.silu(causal_depthwise_conv(xbc, conv_w, conv_b)).astype(jnp.float32)
    xs, bm, cm = jnp.split(xbc, [SSM_D_INNER, SSM_D_INNER + SSM_GROUPS * SSM_STATE], axis=-1)
    xs = xs.reshape(bsz, seq, SSM_HEADS, SSM_HEAD_DIM)
    bm = bm.reshape(bsz, seq, SSM_GROUPS, SSM_STATE)
    cm = cm.reshape(bsz, seq, SSM_GROUPS, SSM_STATE)
    dt = jax.nn.softplus(dt_raw.astype(jnp.float32) + dt_bias.astype(jnp.float32))
    a = -jnp.exp(a_log.astype(jnp.float32))
    y = ssd_chunked(xs * dt[..., None], dt * a, bm, cm) + d_skip.astype(jnp.float32)[:, None] * xs
    y = y.reshape(bsz, seq, SSM_D_INNER) * jax.nn.silu(z.astype(jnp.float32))
    return rms_norm(y, norm_g).astype(z.dtype)

def conv_ssd_mixer(u, w_in, conv_dw_w, conv_dw_b, conv_ln_g, conv_ln_b, ssm_conv_w, ssm_conv_b, ssm_dt_bias, ssm_a_log, ssm_d, ssm_norm_g, w_out):
    proj = u @ w_in
    s0 = 2 * CONV_CH
    s1 = s0 + SSM_D_INNER
    s2 = s1 + SSM_XBC
    conv_in, z, xbc, dt_raw = jnp.split(proj, [s0, s1, s2], axis=-1)
    ya = conformer_conv(conv_in, conv_dw_w, conv_dw_b, conv_ln_g, conv_ln_b)
    yb = mamba2_ssd(z, xbc, dt_raw, ssm_conv_w, ssm_conv_b, ssm_dt_bias, ssm_a_log, ssm_d, ssm_norm_g)
    return jnp.concatenate([ya.astype(u.dtype), yb.astype(u.dtype)], axis=-1) @ w_out

def dilated_window_attention(q, k, v, slopes, window, dilation):
    bsz, seq, heads, dh = q.shape
    n = seq // dilation
    steps = window // dilation
    nb = -(-n // ATTN_BLOCK)
    pad = nb * ATTN_BLOCK - n

    def strided(t):
        t = t.reshape(bsz, n, dilation, heads, dh).transpose(0, 2, 1, 3, 4)
        t = t.reshape(bsz * dilation, n, heads, dh)
        t = jnp.pad(t, ((0, 0), (0, pad), (0, 0), (0, 0)))
        return t.reshape(bsz * dilation, nb, ATTN_BLOCK, heads, dh)

    def with_previous_block(t):
        prev = jnp.pad(t[:, :-1], ((0, 0), (1, 0), (0, 0), (0, 0), (0, 0)))
        return jnp.concatenate([prev, t], axis=2)

    qb = strided(q)
    kb = with_previous_block(strided(k))
    vb = with_previous_block(strided(v))
    scores = jnp.einsum('znqhd,znkhd->znhqk', qb.astype(jnp.float32), kb.astype(jnp.float32)) * (dh ** -0.5)
    qi = jnp.arange(ATTN_BLOCK)[:, None]
    kj = jnp.arange(2 * ATTN_BLOCK)[None, :] - ATTN_BLOCK
    rel = qi - kj
    blk0 = (jnp.arange(nb) * ATTN_BLOCK)[:, None, None]
    valid = (rel >= 0) & (rel <= steps) & (blk0 + kj >= 0)
    bias = -slopes[:, None, None] * (rel * dilation).astype(jnp.float32)
    scores = jnp.where(valid[None, :, None], scores + bias[None, None], -jnp.inf)
    lse = jax.nn.logsumexp(scores, axis=-1)
    probs = jnp.exp(scores - lse[..., None]).astype(v.dtype)
    out = jnp.einsum('znhqk,znkhd->znqhd', probs, vb)
    out = out.reshape(bsz, dilation, nb * ATTN_BLOCK, heads, dh)[:, :, :n]
    out = out.transpose(0, 2, 1, 3, 4).reshape(bsz, seq, heads, dh)
    lse = lse.transpose(0, 1, 3, 2).reshape(bsz, dilation, nb * ATTN_BLOCK, heads)[:, :, :n]
    lse = lse.transpose(0, 2, 1, 3).reshape(bsz, seq, heads)
    return out, lse

def dilated_attention_mixer(u, w_qkv, w_o):
    bsz, seq, _ = u.shape
    qkv = (u @ w_qkv).reshape(bsz, seq, 3, ATTN_GROUPS, ATTN_HEADS, ATTN_HEAD_DIM)
    slopes = jnp.exp2(-8.0 * jnp.arange(1, ATTN_HEADS + 1, dtype=jnp.float32) / ATTN_HEADS)
    outs = []
    lses = []
    for g, (window, dilation) in enumerate(DILATED_PATTERNS):
        o, l = dilated_window_attention(qkv[:, :, 0, g], qkv[:, :, 1, g], qkv[:, :, 2, g], slopes, window, dilation)
        outs.append(o)
        lses.append(l)
    weights = jax.nn.softmax(jnp.stack(lses, axis=0), axis=0)
    merged = jnp.einsum('gblh,gblhd->blhd', weights, jnp.stack(outs, axis=0).astype(jnp.float32))
    return merged.reshape(bsz, seq, ATTN_OUT_WIDTH).astype(u.dtype) @ w_o

def first_inputs(seed: int = 0) -> dict:
    key = jax.random.key(seed)
    ks = jax.random.split(key, 20)

    def normal(k, shape, scale):
        return jax.random.normal(k, shape, jnp.float32) * scale

    x = normal(ks[0], (BATCH, SEQ, D_MODEL), 1.0)
    norm_g = 1.0 + normal(ks[1], (DEPTH, 6, D_MODEL), 0.05)
    ffn_w1 = normal(ks[2], (DEPTH, 2, D_MODEL, 2 * D_FF), D_MODEL ** -0.5)
    ffn_w2 = normal(ks[3], (DEPTH, 2, D_FF, D_MODEL), D_FF ** -0.5)
    hyb_w_in = normal(ks[4], (N_EVEN, D_MODEL, HYB_IN_COLS), D_MODEL ** -0.5)
    conv_dw_w = normal(ks[5], (N_EVEN, CONV_WIDTH, CONV_CH), CONV_WIDTH ** -0.5)
    conv_dw_b = normal(ks[6], (N_EVEN, CONV_CH), 0.02)
    conv_ln_g = 1.0 + normal(ks[7], (N_EVEN, CONV_CH), 0.05)
    conv_ln_b = normal(ks[8], (N_EVEN, CONV_CH), 0.02)
    ssm_conv_w = normal(ks[9], (N_EVEN, SSM_CONV_WIDTH, SSM_XBC), SSM_CONV_WIDTH ** -0.5)
    ssm_conv_b = normal(ks[10], (N_EVEN, SSM_XBC), 0.02)
    dt0 = jnp.exp(jax.random.uniform(ks[11], (N_EVEN, SSM_HEADS), jnp.float32, math.log(1e-3), math.log(1e-1)))
    ssm_dt_bias = dt0 + jnp.log(-jnp.expm1(-dt0))
    ssm_a_log = jnp.log(jax.random.uniform(ks[12], (N_EVEN, SSM_HEADS), jnp.float32, 1.0, 16.0))
    ssm_d = 1.0 + normal(ks[13], (N_EVEN, SSM_HEADS), 0.1)
    ssm_norm_g = 1.0 + normal(ks[14], (N_EVEN, SSM_D_INNER), 0.05)
    hyb_w_out = normal(ks[15], (N_EVEN, HYB_MIX_WIDTH, D_MODEL), HYB_MIX_WIDTH ** -0.5)
    attn_w_qkv = normal(ks[16], (N_ODD, D_MODEL, ATTN_QKV_COLS), D_MODEL ** -0.5)
    attn_w_o = normal(ks[17], (N_ODD, ATTN_OUT_WIDTH, D_MODEL), ATTN_OUT_WIDTH ** -0.5)
    return {'x': x, 'norm_g': norm_g, 'ffn_w1': ffn_w1, 'ffn_w2': ffn_w2, 'hyb_w_in': hyb_w_in, 'conv_dw_w': conv_dw_w, 'conv_dw_b': conv_dw_b, 'conv_ln_g': conv_ln_g, 'conv_ln_b': conv_ln_b, 'ssm_conv_w': ssm_conv_w, 'ssm_conv_b': ssm_conv_b, 'ssm_dt_bias': ssm_dt_bias, 'ssm_a_log': ssm_a_log, 'ssm_d': ssm_d, 'ssm_norm_g': ssm_norm_g, 'hyb_w_out': hyb_w_out, 'attn_w_qkv': attn_w_qkv, 'attn_w_o': attn_w_o}

def first_block(x, norm_g, ffn_w1, ffn_w2, hyb_w_in, conv_dw_w, conv_dw_b, conv_ln_g, conv_ln_b, ssm_conv_w, ssm_conv_b, ssm_dt_bias, ssm_a_log, ssm_d, ssm_norm_g, hyb_w_out, attn_w_qkv, attn_w_o):
    h = x
    for i in range(DEPTH):
        g = norm_g[i]
        h = h + 0.5 * rms_norm(swiglu(rms_norm(h, g[0]), ffn_w1[i, 0], ffn_w2[i, 0]), g[1])
        u = rms_norm(h, g[2])
        j = i // 2
        if i % 2 == 0:
            m = conv_ssd_mixer(u, hyb_w_in[j], conv_dw_w[j], conv_dw_b[j], conv_ln_g[j], conv_ln_b[j], ssm_conv_w[j], ssm_conv_b[j], ssm_dt_bias[j], ssm_a_log[j], ssm_d[j], ssm_norm_g[j], hyb_w_out[j])
        else:
            m = dilated_attention_mixer(u, attn_w_qkv[j], attn_w_o[j])
        h = h + rms_norm(m, g[3])
        h = h + 0.5 * rms_norm(swiglu(rms_norm(h, g[4]), ffn_w1[i, 1], ffn_w2[i, 1]), g[5])
    return h


CHUNK = 64
RET_HEADS = 4
RET_DK = 128
RET_DV = 256
RET_QK = RET_HEADS * RET_DK
RET_V = RET_HEADS * RET_DV
ROPE_BASE = 10000.0
HG_HEADS = 8
HG_DK = 128
HG_DV = 128
HG_K = HG_HEADS * HG_DK
HG_V = HG_HEADS * HG_DV
HG_BLOCK = 16
SWA_HQ = 16
SWA_HKV = 4
SWA_HD = 64
SWA_Q = SWA_HQ * SWA_HD
SWA_KV = SWA_HKV * SWA_HD
SWA_WINDOW = 128
SWA_WIN_CHUNKS = SWA_WINDOW // CHUNK
N_EXPERTS = 8
TOP_K = 2
D_EXP = 3584
N_DENSE = (DEPTH + 1) // 2
N_MOE = DEPTH // 2
LN_EPS = 1e-5
RMS_EPS = 1e-6
DN_ALPHA = (2.0 * DEPTH) ** 0.25
DN_BETA = (8.0 * DEPTH) ** -0.25
IN_SPLITS = (RET_QK, RET_QK, RET_V, RET_V,
             HG_K, HG_K, HG_V, HG_V,
             SWA_Q, SWA_KV, SWA_KV,
             D_MODEL, D_MODEL, D_MODEL)
N_IN = sum(IN_SPLITS)


def layer_norm_2(x, g, b):
    xf = x.astype(jnp.float32)
    mu = jnp.mean(xf, -1, keepdims=True)
    var = jnp.mean(jnp.square(xf - mu), -1, keepdims=True)
    return ((xf - mu) * lax.rsqrt(var + LN_EPS) * g + b).astype(x.dtype)

def rms_norm_2(x):
    xf = x.astype(jnp.float32)
    return xf * lax.rsqrt(jnp.mean(xf * xf, -1, keepdims=True) + RMS_EPS)

def rotary(x, pos):
    half = x.shape[-1] // 2
    inv = 1.0 / (ROPE_BASE ** jnp.linspace(0.0, 1.0, half, dtype=jnp.float32))
    ang = pos[:, None] * inv[None, :]
    cos = jnp.cos(ang)[None, :, None, :]
    sin = jnp.sin(ang)[None, :, None, :]
    x1, x2 = x[..., :half], x[..., half:]
    return jnp.concatenate([x1 * cos - x2 * sin, x1 * sin + x2 * cos], axis=-1)

def retention(q, k, v):
    B, S, H, DK = q.shape
    DV = v.shape[-1]
    n = S // CHUNK
    log_gamma = jnp.log(1.0 - 2.0 ** (-5.0 - jnp.arange(H, dtype=jnp.float32)))
    k = k * DK ** -0.5
    qc = q.reshape(B, n, CHUNK, H, DK)
    kc = k.reshape(B, n, CHUNK, H, DK)
    vc = v.reshape(B, n, CHUNK, H, DV)
    idx = jnp.arange(CHUNK, dtype=jnp.float32)
    diff = idx[:, None] - idx[None, :]
    decay = jnp.where(diff[None] >= 0,
                      jnp.exp(jnp.maximum(diff, 0.0)[None] * log_gamma[:, None, None]), 0.0)
    scores = jnp.einsum('bnthd,bnshd->bnhts', qc, kc) * decay
    o_intra = jnp.einsum('bnhts,bnshv->bnthv', scores, vc)
    k_decay = jnp.exp((CHUNK - 1.0 - idx)[:, None] * log_gamma[None, :])
    q_decay = jnp.exp((idx + 1.0)[:, None] * log_gamma[None, :])
    chunk_decay = jnp.exp(CHUNK * log_gamma)[None, :, None, None]

    def step(state, inp):
        q_n, k_n, v_n = inp
        o = jnp.einsum('bthd,th,bhdv->bthv', q_n, q_decay, state)
        state = chunk_decay * state + jnp.einsum('bshd,sh,bshv->bhdv', k_n, k_decay, v_n)
        return state, o

    init = jnp.zeros((B, H, DK, DV), jnp.float32)
    _, o_inter = lax.scan(step, init, (jnp.moveaxis(qc, 1, 0), jnp.moveaxis(kc, 1, 0),
                                       jnp.moveaxis(vc, 1, 0)))
    return (o_intra + jnp.moveaxis(o_inter, 0, 1)).reshape(B, S, H, DV)

def hgrn2_scan(q, log_f, k, v):
    B, S, H, DK = q.shape
    DV = v.shape[-1]
    n = S // HG_BLOCK
    L = HG_BLOCK
    qc = q.reshape(B, n, L, H, DK)
    kc = k.reshape(B, n, L, H, DK)
    vc = v.reshape(B, n, L, H, DV)
    bcum = jnp.cumsum(log_f.reshape(B, n, L, H, DK), axis=2)
    q_t = qc * jnp.exp(bcum)
    k_t = kc * jnp.exp(-bcum)
    causal = jnp.tril(jnp.ones((L, L), dtype=bool))
    a = jnp.where(causal, jnp.einsum('bnthd,bnshd->bnhts', q_t, k_t), 0.0)
    o_intra = jnp.einsum('bnhts,bnshv->bnthv', a, vc)
    b_last = bcum[:, :, -1]
    k_state = kc * jnp.exp(b_last[:, :, None] - bcum)
    blk_decay = jnp.exp(b_last)

    def step(state, inp):
        q_n, ks_n, v_n, d_n = inp
        o = jnp.einsum('bthd,bhdv->bthv', q_n, state)
        state = d_n[..., None] * state + jnp.einsum('bshd,bshv->bhdv', ks_n, v_n)
        return state, o

    init = jnp.zeros((B, H, DK, DV), jnp.float32)
    _, o_inter = lax.scan(step, init, (jnp.moveaxis(q_t, 1, 0), jnp.moveaxis(k_state, 1, 0),
                                       jnp.moveaxis(vc, 1, 0), jnp.moveaxis(blk_decay, 1, 0)))
    return (o_intra + jnp.moveaxis(o_inter, 0, 1)).reshape(B, S, H, DV)

def swa_with_sinks(q, k, v, sinks):
    B, S, HQ, HD = q.shape
    HKV = k.shape[2]
    G = HQ // HKV
    W = SWA_WIN_CHUNKS
    n = S // CHUNK
    qc = q.astype(jnp.float32).reshape(B, n, CHUNK, HKV, G, HD)
    kc = k.astype(jnp.float32).reshape(B, n, CHUNK, HKV, HD)
    vc = v.astype(jnp.float32).reshape(B, n, CHUNK, HKV, HD)
    padw = ((0, 0), (W, 0), (0, 0), (0, 0), (0, 0))
    kp = jnp.pad(kc, padw)
    vp = jnp.pad(vc, padw)
    kb = jnp.concatenate([kp[:, j:j + n] for j in range(W + 1)], axis=2)
    vb = jnp.concatenate([vp[:, j:j + n] for j in range(W + 1)], axis=2)
    chunk_ids = jnp.arange(n)[:, None] - W + jnp.arange(W + 1)[None, :]
    valid = jnp.repeat(chunk_ids >= 0, CHUNK, axis=1)
    s = jnp.einsum('bntkgd,bnskd->bnkgts', qc, kb) * HD ** -0.5
    s = jnp.where(valid[None, :, None, None, None, :], s, -jnp.inf)
    sink = sinks.astype(jnp.float32).reshape(HKV, G)[None, None, :, :, None, None]
    m = jnp.maximum(jnp.max(s, -1, keepdims=True), sink)
    p = jnp.exp(s - m)
    p = p / (jnp.sum(p, -1, keepdims=True) + jnp.exp(sink - m))
    o = jnp.einsum('bnkgts,bnskd->bntkgd', p, vb)
    return o.reshape(B, S, HQ * HD)

def swiglu_2(h, w_gate, w_up, w_down):
    return (jax.nn.silu(h @ w_gate) * (h @ w_up)) @ w_down

def moe_swiglu(h2, w_router, w_gate, w_up, w_down):
    logits = (h2 @ w_router).astype(jnp.float32)
    top_logits, top_idx = lax.top_k(logits, TOP_K)
    top_w = jax.nn.softmax(top_logits, axis=-1)
    flat_e = top_idx.reshape(-1)
    order = jnp.argsort(flat_e)
    tok = order // TOP_K
    xs = h2[tok]
    sizes = jnp.bincount(flat_e, length=N_EXPERTS).astype(jnp.int32)
    hid = jax.nn.silu(lax.ragged_dot(xs, w_gate, sizes)) * lax.ragged_dot(xs, w_up, sizes)
    y = lax.ragged_dot(hid, w_down, sizes)
    y = y * top_w.reshape(-1)[order][:, None].astype(y.dtype)
    return jnp.zeros_like(h2).at[tok].add(y.astype(h2.dtype))

def second_inputs(seed: int = 0) -> dict:
    key = jax.random.key(seed)
    ks = jax.random.split(key, 24)
    f32 = jnp.float32
    D = D_MODEL

    def nrm(k, shape, scale):
        return jax.random.normal(k, shape, f32) * scale

    return {
        'x': nrm(ks[0], (BATCH, SEQ, D), 1.0),
        'ln_in_g': 1.0 + nrm(ks[1], (D,), 0.02),
        'ln_in_b': nrm(ks[2], (D,), 0.02),
        'w_in': nrm(ks[3], (DEPTH, D, N_IN), D ** -0.5),
        'ret_w_out': nrm(ks[4], (DEPTH, RET_V, D), DN_BETA * RET_V ** -0.5),
        'hgrn_lower_bounds': 1.0 + nrm(ks[5], (DEPTH, HG_K), 0.5),
        'hgrn_norm_g': 1.0 + nrm(ks[6], (DEPTH, HG_DV), 0.02),
        'hgrn_w_out': nrm(ks[7], (DEPTH, HG_V, D), DN_BETA * HG_V ** -0.5),
        'swa_sinks': nrm(ks[8], (DEPTH, SWA_HQ), 0.5),
        'swa_w_out': nrm(ks[9], (DEPTH, SWA_Q, D), DN_BETA * SWA_Q ** -0.5),
        'w_o': nrm(ks[10], (DEPTH, D, D), DN_BETA * D ** -0.5),
        'ln_mix_g': 1.0 + nrm(ks[11], (DEPTH, D), 0.02),
        'ln_mix_b': nrm(ks[12], (DEPTH, D), 0.02),
        'ffn_w_gate': nrm(ks[13], (N_DENSE, D, D_FF), D ** -0.5),
        'ffn_w_up': nrm(ks[14], (N_DENSE, D, D_FF), D ** -0.5),
        'ffn_w_down': nrm(ks[15], (N_DENSE, D_FF, D), DN_BETA * D_FF ** -0.5),
        'moe_router': nrm(ks[16], (N_MOE, D, N_EXPERTS), D ** -0.5),
        'moe_w_gate': nrm(ks[17], (N_MOE, N_EXPERTS, D, D_EXP), D ** -0.5),
        'moe_w_up': nrm(ks[18], (N_MOE, N_EXPERTS, D, D_EXP), D ** -0.5),
        'moe_w_down': nrm(ks[19], (N_MOE, N_EXPERTS, D_EXP, D), DN_BETA * D_EXP ** -0.5),
        'ln_ffn_g': 1.0 + nrm(ks[20], (DEPTH, D), 0.02),
        'ln_ffn_b': nrm(ks[21], (DEPTH, D), 0.02),
    }

def second_block(x, ln_in_g, ln_in_b, w_in, ret_w_out, hgrn_lower_bounds, hgrn_norm_g, hgrn_w_out,
              swa_sinks, swa_w_out, w_o, ln_mix_g, ln_mix_b, ffn_w_gate, ffn_w_up, ffn_w_down,
              moe_router, moe_w_gate, moe_w_up, moe_w_down, ln_ffn_g, ln_ffn_b):
    B, S, D = x.shape
    f32 = jnp.float32
    pos = jnp.arange(S, dtype=f32)
    split_points = np.cumsum(np.array(IN_SPLITS))[:-1].tolist()
    lb_all = jnp.cumsum(jax.nn.softmax(hgrn_lower_bounds.astype(f32), axis=0), axis=0)
    lb_all = lb_all - lb_all[0]

    h = layer_norm_2(x, ln_in_g, ln_in_b)
    for layer in range(DEPTH):
        proj = jnp.einsum('bsd,dc->bsc', h, w_in[layer])
        (rq, rk, rv, rg, hq, hf, hi, hg, sq, sk, sv, ga, gb, gc) = jnp.split(proj, split_points, axis=-1)

        r_q = rotary(rq.astype(f32).reshape(B, S, RET_HEADS, RET_DK), pos)
        r_k = rotary(rk.astype(f32).reshape(B, S, RET_HEADS, RET_DK), pos)
        r_v = rv.astype(f32).reshape(B, S, RET_HEADS, RET_DV)
        r_o = rms_norm_2(retention(r_q, r_k, r_v)).reshape(B, S, RET_V)
        y_a = (jax.nn.silu(rg.astype(f32)) * r_o) @ ret_w_out[layer]

        lb = lb_all[layer].reshape(HG_HEADS, HG_DK)
        z = hf.astype(f32).reshape(B, S, HG_HEADS, HG_DK)
        log_f = jnp.logaddexp(jnp.log(lb), jnp.log1p(-lb) + jax.nn.log_sigmoid(z))
        h_k = -jnp.expm1(log_f)
        h_q = hq.astype(f32).reshape(B, S, HG_HEADS, HG_DK)
        h_v = hi.astype(f32).reshape(B, S, HG_HEADS, HG_DV)
        h_o = rms_norm_2(hgrn2_scan(h_q, log_f, h_k, h_v)) * hgrn_norm_g[layer]
        y_b = (jax.nn.silu(hg.astype(f32)) * h_o.reshape(B, S, HG_V)) @ hgrn_w_out[layer]

        s_o = swa_with_sinks(sq.reshape(B, S, SWA_HQ, SWA_HD), sk.reshape(B, S, SWA_HKV, SWA_HD),
                             sv.reshape(B, S, SWA_HKV, SWA_HD), swa_sinks[layer])
        y_c = s_o @ swa_w_out[layer]

        merged = (jax.nn.sigmoid(ga.astype(f32)) * y_a + jax.nn.sigmoid(gb.astype(f32)) * y_b
                  + jax.nn.sigmoid(gc.astype(f32)) * y_c)
        mix = merged @ w_o[layer]
        h = layer_norm_2((DN_ALPHA * h + mix).astype(h.dtype), ln_mix_g[layer], ln_mix_b[layer])

        j = layer // 2
        if layer % 2 == 0:
            ff = swiglu_2(h, ffn_w_gate[j], ffn_w_up[j], ffn_w_down[j])
        else:
            ff = moe_swiglu(h.reshape(B * S, D), moe_router[j], moe_w_gate[j], moe_w_up[j],
                            moe_w_down[j]).reshape(B, S, D)
        h = layer_norm_2((DN_ALPHA * h + ff).astype(h.dtype), ln_ffn_g[layer], ln_ffn_b[layer])
    return h


def setup_inputs(seed=0):
    out = dict(first_inputs(seed))
    for name, value in second_inputs(seed + 1).items():
        if name != "x":
            out[name + "_2"] = value
    return out


def reference(
    x, norm_g, ffn_w1, ffn_w2, hyb_w_in, conv_dw_w, conv_dw_b, conv_ln_g, conv_ln_b, ssm_conv_w,
    ssm_conv_b, ssm_dt_bias, ssm_a_log, ssm_d, ssm_norm_g, hyb_w_out, attn_w_qkv, attn_w_o,
    ln_in_g_2, ln_in_b_2, w_in_2, ret_w_out_2, hgrn_lower_bounds_2, hgrn_norm_g_2, hgrn_w_out_2,
    swa_sinks_2, swa_w_out_2, w_o_2, ln_mix_g_2, ln_mix_b_2, ffn_w_gate_2, ffn_w_up_2,
    ffn_w_down_2, moe_router_2, moe_w_gate_2, moe_w_up_2, moe_w_down_2, ln_ffn_g_2, ln_ffn_b_2,
):
    x = first_block(
        x, norm_g, ffn_w1, ffn_w2, hyb_w_in, conv_dw_w, conv_dw_b, conv_ln_g, conv_ln_b,
        ssm_conv_w, ssm_conv_b, ssm_dt_bias, ssm_a_log, ssm_d, ssm_norm_g, hyb_w_out,
        attn_w_qkv, attn_w_o,
    )
    return second_block(
        x, ln_in_g_2, ln_in_b_2, w_in_2, ret_w_out_2, hgrn_lower_bounds_2, hgrn_norm_g_2,
        hgrn_w_out_2, swa_sinks_2, swa_w_out_2, w_o_2, ln_mix_g_2, ln_mix_b_2, ffn_w_gate_2,
        ffn_w_up_2, ffn_w_down_2, moe_router_2, moe_w_gate_2, moe_w_up_2, moe_w_down_2,
        ln_ffn_g_2, ln_ffn_b_2,
    )


_drawn_inputs = setup_inputs


def setup_inputs(seed=0):
    import zlib

    import numpy as np

    out = dict(_drawn_inputs(seed))
    spreads = {}
    factors = {'conv_ln_b': 3.483, 'hgrn_norm_g_2': 22.355, 'swa_sinks_2': 44.22}
    for name, (base, spread) in spreads.items():
        noise = np.random.default_rng([zlib.crc32(name.encode()), seed]).standard_normal(out[name].shape)
        drawn = base * np.exp(spread * noise) if base else spread * noise
        out[name] = jnp.asarray(drawn.astype(out[name].dtype))
    for name, factor in factors.items():
        out[name] = (out[name] * factor).astype(out[name].dtype)
    return out
```

```python
from contextlib import ExitStack

import numpy as np

import concourse.bass as bass
from concourse import mybir

F32 = mybir.dt.float32
U32 = mybir.dt.uint32
ACT = mybir.ActivationFunctionType
ALU = mybir.AluOpType
AX = mybir.AxisListType

P = 128
T = 256
NT = T // P
D = 1024
KC = D // P
COLS = 512
FF = 2816
FFB = FF // 256
NE = 8
DE = 3584
MOEB = DE // 256
SLOTS = P
RING = 4
RING2 = 2
TAPS = 31
SCONV = 4
HEADS_SSM = 16
ALPHA = 4.0 ** 0.25
NEG = -1.0e30



def shape_constants():
    f = np.float32
    p = np.arange(P)
    c = {}
    c["ident"] = np.eye(P, dtype=f)
    c["ones"] = np.ones((P, P), f)
    c["upper"] = (p[:, None] <= p[None, :]).astype(f)
    inv = (1.0 / (np.float32(10000.0) ** np.linspace(0.0, 1.0, 64, dtype=f))).astype(f)
    ang = (np.arange(T, dtype=f)[None, :] * inv[:, None]).astype(f)
    c["cos"] = np.tile(np.cos(ang), (2, 1)).astype(f)
    c["sin"] = np.concatenate([np.sin(ang), -np.sin(ang)], 0).astype(f)
    diff = np.arange(T)[None, :] - p[:, None]
    for h in range(4):
        lg = np.log(f(1.0) - f(2.0) ** f(-5.0 - h)).astype(f)
        dec = np.where(diff >= 0, np.exp(np.maximum(diff, 0).astype(f) * lg), 0.0)
        c[f"decay{h}"] = (dec * 128.0 ** -0.5).astype(f)
    for qt in range(2):
        q = qt * P + p[:, None]
        k = np.arange((qt + 1) * P)[None, :]
        rel = q - k
        for g, dil in enumerate((1, 4, 16)):
            ok = (rel >= 0) & (rel % dil == 0) & (rel // dil <= P)
            c[f"dist{qt}{g}"] = np.where(ok, rel, 1e30).astype(f)
        cd = q // 64 - k // 64
        c[f"window{qt}"] = np.where((cd >= 0) & (cd <= 2), 0.0, NEG).astype(f)
    c["block"] = (p[:, None] // 16 == np.arange(8)[None, :]).astype(f)
    c["blockcausal"] = ((p[:, None] // 16 == p[None, :] // 16) & (p[:, None] <= p[None, :])).astype(f)
    c["iota128"] = np.tile(np.arange(P, dtype=f), (P, 1))
    c["iota8"] = np.tile(np.arange(8, dtype=f), (P, 1))
    return c


def const_layout():
    at, off = {}, 0
    for name, v in shape_constants().items():
        at[name] = (off, v.shape[1])
        off += v.shape[1]
    return at, off


STACK = [("norm_g", 96), ("conv_dw_w", TAPS * 8), ("conv_dw_b", 8), ("conv_ln_g", 8), ("conv_ln_b", 8),
         ("ssm_conv_w", SCONV * 12), ("ssm_conv_b", 12), ("ssm_norm_g", 8), ("hgrn_lower_bounds_2", 16),
         ("hgrn_norm_g_2", 2)]
STACK_ROWS = sum(n for _, n in STACK)
STACKS = -(-STACK_ROWS // P)


def stack_at(name):
    off = 0
    for n, r in STACK:
        if n == name:
            return off
        off += r
    raise KeyError(name)


class Events:

    def __init__(self, nc, ctx, known):
        self.nc, self.ctx, self.known = nc, ctx, known
        self.seen, self.count, self.sems = {}, {}, {}

    def sem(self, name):
        if name not in self.sems:
            self.sems[name] = self.ctx.enter_context(self.nc.semaphore(name))
            self.count.setdefault(name, 0)
        return self.sems[name]

    def value(self, name, key):
        assert not self.known or (name, key) in self.known, (name, key)
        return self.known.get((name, key), 1)

    def mark(self, name, key, inc=1):
        self.sem(name)
        self.count[name] += inc
        assert (name, key) not in self.seen, (name, key)
        self.seen[(name, key)] = self.count[name]
        return inc

    def start(self, name, stage):
        self.sem(name)
        self.seen[(name, ("start", stage))] = self.count[name]

    def base(self, name, stage):
        assert not self.known or (name, ("start", stage)) in self.known, (name, stage)
        return self.known.get((name, ("start", stage)), 1)


def build(nc, a, out, consts, known):
    ctx = ExitStack()
    with ctx:
        ev = Events(nc, ctx, known)
        cat, ccols = const_layout()

        def sb(name, shape, dt=F32):
            return ctx.enter_context(nc.sbuf_tensor(name, shape, dt))

        w1 = sb("w1", [P, RING, 4096])
        w2 = sb("w2", [P, RING2, 2, D])
        con = sb("con", [P, ccols])
        h = sb("h", [P, NT, D])
        u = sb("u", [P, KC, T])
        rows = sb("rows", [P, 2, D])
        par = sb("par", [P, STACKS * P])
        small = sb("small", [P, 512])
        ARENA = 21760
        arena = sb("arena", [P, ARENA])
        acc = ctx.enter_context(nc.psum_tensor("acc", [P, 4, 512], F32))
        duo = ctx.enter_context(nc.psum_tensor("duo", [P, 2, 512], F32))
        aux = ctx.enter_context(nc.psum_tensor("aux", [P, 2, 512], F32))

        def cst(name):
            o, n = cat[name]
            return con[:, o:o + n]

        def view(off, *shape):
            n = int(np.prod(shape))
            assert off + n <= ARENA, (off, shape)
            v = arena[:, off:off + n]
            if len(shape) == 2:
                v = v.rearrange("p (a b) -> p a b", b=shape[1])
            if len(shape) == 3:
                v = v.rearrange("p (a b c) -> p a b c", b=shape[1], c=shape[2])
            return v

        def bc(x, axis, shape):
            return x.unsqueeze(axis).broadcast_to(shape)

        def split(x, n):
            return x.rearrange("p (a b) -> p a b", a=n)

        def pcol(name, row):
            o = stack_at(name) + row
            return par[:, o:o + 1]

        used = [0]

        def cols(n):
            used[0] += n
            assert used[0] <= 512
            return small[:, used[0] - n:used[0]]

        ssq, msq, rot, rsd = cols(8), cols(8), cols(8), cols(8)
        stats, mv = cols(24), cols(4)
        dtb, alog, dskip = cols(16), cols(16), cols(16)
        sinks = cols(32)
        gates, logits, top = cols(16), cols(16), cols(16)
        topi = cols(16).bitcast(U32)
        topf, prob = cols(16), cols(8)
        lbd, lb1, lb2, lb3, lbA, lbC = cols(8), cols(16), cols(16), cols(16), cols(16), cols(16)
        smax, ssum, sinke = cols(16), cols(16), cols(16)
        decay_tot = cols(16)

        pe, act, dve, pool, sp = nc.tensor, nc.scalar, nc.vector, nc.gpsimd, nc.sync

        sem = ev.sem
        at = ev.value
        mark = ev.mark

        def latest(name):
            return ev.count[name]

        orders = {"act_order": 0, "dve_order": 0}

        def A(ins):
            ins.then_inc(sem("act_order"), 1)
            orders["act_order"] += 1
            act.wait_ge(sem("act_order"), orders["act_order"])

        def V(ins):
            ins.then_inc(sem("dve_order"), 1)
            orders["dve_order"] += 1
            dve.wait_ge(sem("dve_order"), orders["dve_order"])

        last_fill = {}

        def bank(b):
            return acc[:, b, :] if b < 4 else (duo, aux)[(b - 4) // 2][:, b % 2, :]

        def bank_full(b):
            return sem(f"bank_full{b}")

        def filled_at(b, key):
            return at(f"bank_full{b}", key)

        def fill(b, key):
            last_fill[b] = key
            return mark(f"bank_full{b}", key)

        def claim(*banks):
            for b in banks:
                if b in last_fill and known:
                    name, count = known[("read", b, last_fill[b])]
                    pe.wait_ge(sem(name), count)

        def was_read(b, key, name):
            ev.seen[("read", b, key)] = (name, ev.count[name])

        def mark_read(name, b, key):
            inc = mark(name, ("read", b, key))
            was_read(b, key, name)
            return inc

        ring_pe, ring_sp = {"w1": 0, "w2": 0}, {"w1": 0, "w2": 0}

        def arrived():
            n = ring_pe["w1"]
            ring_pe["w1"] += 1
            pe.wait_ge(sem(f"w1_landed{n % RING}"), 32 * (n // RING + 1))
            return w1[:, n % RING, :]

        def released(ring, n, name, count=None):
            ev.seen[("release", ring, n)] = (name, ev.count[name] if count is None else count)

        def released_last(name):
            released("w1", ring_pe["w1"] - 1, name)

        def slot_free(ring):
            n = ring_sp[ring] - (RING if ring == "w1" else RING2)
            if n >= 0 and known:
                name, count = known[("release", ring, n)]
                sp.wait_ge(sem(name), count)

        def load(*blocks):
            for parts in blocks:
                slot_free("w1")
                n = ring_sp["w1"]
                ring_sp["w1"] += 1
                for dst, src in parts(w1[:, n % RING, :]):
                    sp.dma_start(dst, src).then_inc(sem(f"w1_landed{n % RING}"), 16)

        def col_block(w, c0):
            def parts(slot):
                s = slot.rearrange("p (t n) -> p t n", n=COLS)
                src = w.rearrange("(t p) n -> p t n", p=P)
                return [(s[:, 4 * i:4 * i + 4, :], src[:, 4 * i:4 * i + 4, c0:c0 + COLS]) for i in range(2)]
            return parts

        def row_block(w, r0):
            def parts(slot):
                s = slot.rearrange("p (t n) -> p t n", n=D)
                src = w[r0:r0 + 4 * P, :].rearrange("(t p) n -> p t n", p=P)
                return [(s[:, 2 * i:2 * i + 2, :], src[:, 2 * i:2 * i + 2, :]) for i in range(2)]
            return parts

        def pe_cols_tm(src, key):
            slot = arrived().rearrange("p (t n) -> p t n", n=COLS)
            for t in range(NT):
                claim(4 + t)
                for k in range(KC):
                    m = pe.matmul(bank(4 + t), src[:, k, t * P:(t + 1) * P], slot[:, k, :],
                                  start=(k == 0), stop=(k == KC - 1))
                m.then_inc(bank_full(4 + t), fill(4 + t, key))
            released_last("bank_full5")

        def pe_cols_fm(src, key):
            slot = arrived().rearrange("p (t n) -> p t n", n=COLS)
            for b in range(2):
                claim(4 + b)
                for c in range(2):
                    for k in range(KC):
                        m = pe.matmul(bank(4 + b)[:, c * T:(c + 1) * T],
                                      slot[:, k, (2 * b + c) * P:(2 * b + c + 1) * P], src[:, k, :],
                                      start=(k == 0), stop=(k == KC - 1))
                m.then_inc(bank_full(4 + b), fill(4 + b, key))
            released_last("bank_full5")

        def pe_rows_acc(src, chunks, key):
            claim(0, 1, 2, 3)
            for blk in range(chunks // 4):
                slot = arrived().rearrange("p (t n) -> p t n", n=D)
                for t in range(NT):
                    for half in range(2):
                        for k in range(4):
                            kk = 4 * blk + k
                            m = pe.matmul(acc[:, 2 * t + half, :], src[:, kk, t * P:(t + 1) * P],
                                          slot[:, k, half * 512:(half + 1) * 512],
                                          start=(kk == 0), stop=(kk == chunks - 1))
                        if kk == chunks - 1:
                            m.then_inc(bank_full(2 * t + half), fill(2 * t + half, key))
                if blk == chunks // 4 - 1:
                    released_last("bank_full3")
                else:
                    m.then_inc(sem("rows_multiplied"), mark("rows_multiplied", (key, blk)))
                    released_last("rows_multiplied")

        def pe_to_fm(src, chunks, key):
            for c in range(chunks):
                b = 6 + (c // 2) % 2
                if c % 2 == 0:
                    claim(b)
                for t in range(NT):
                    m = pe.transpose(bank(b)[:, (c % 2) * T + t * P:(c % 2) * T + (t + 1) * P],
                                     src[:, t, c * P:(c + 1) * P], cst("ident"))
                if c % 2:
                    m.then_inc(bank_full(b), fill(b, (key, c // 2)))

        def act_to_fm(dst, chunks, key, gain=None):
            for c in range(0, chunks, 2):
                b = 6 + (c // 2) % 2
                act.wait_ge(bank_full(b), filled_at(b, (key, c // 2)))
                if gain is None:
                    m = act.activation(dst[:, c:c + 2, :], split(bank(b), 2), ACT.Copy)
                else:
                    act.activation(dst[:, c, :], bank(b)[:, 0:T], ACT.Copy, scale=gain(c))
                    m = act.activation(dst[:, c + 1, :], bank(b)[:, T:2 * T], ACT.Copy, scale=gain(c + 1))
                m.then_inc(sem("fm_ready"), mark("fm_ready", (key, c // 2)))
                was_read(b, (key, c // 2), "fm_ready")

        def pe_fm_wait(key, chunks):
            pe.wait_ge(sem("fm_ready"), at("fm_ready", (key, chunks // 2 - 1)))

        def dve_mean(key, n, scale, eps):
            dve.wait_ge(sem("sumsq"), at("sumsq", key))
            dve.tensor_scalar(msq[:, 0:n], ssq[:, 0:n], scale, eps, ALU.mult, ALU.add)\
                .then_inc(sem("meansq"), mark("meansq", key))

        def act_root(key, n):
            act.wait_ge(sem("meansq"), at("meansq", key))
            act.activation(rot[:, 0:n], msq[:, 0:n], ACT.Sqrt).then_inc(sem("root"), mark("root", key))

        def dve_recip(key, n):
            dve.wait_ge(sem("root"), at("root", key))
            V(dve.reciprocal(rsd[:, 0:n], rot[:, 0:n]))

        hn = view(0, NT, D)
        junk = view(2048, NT, D)

        def pe_prenorm(key):
            pe.wait_ge(sem("normed"), at("normed", (key, 1)))
            pe_to_fm(hn, KC, key)
            pe_fm_wait(key, KC)

        def act_prenorm(key, row):
            act.wait_ge(sem("h_ready"), at("h_ready", key))
            for t in range(NT):
                m = act.activation(junk[:, t, :], h[:, t, :], ACT.Square, accum_out=ssq[:, t:t + 1])
            m.then_inc(sem("sumsq"), mark("sumsq", key))
            act_root(key, 2)
            act_to_fm(u, KC, key, gain=lambda c: pcol("norm_g", row * 8 + c))

        def dve_prenorm(key):
            dve_mean(key, 2, 1.0 / D, 1e-6)
            dve_recip(key, 2)
            for t in range(NT):
                dve.tensor_scalar(hn[:, t, :], h[:, t, :], rsd[:, t:t + 1], None, ALU.mult)\
                    .then_inc(sem("normed"), mark("normed", (key, t)))

        def act_postnorm(key):
            act.wait_ge(bank_full(3), filled_at(3, key))
            for t in range(NT):
                for half in range(2):
                    m = act.activation(junk[:, t, half * 512:(half + 1) * 512], acc[:, 2 * t + half, :],
                                       ACT.Square, accum_out=ssq[:, 2 * t + half:2 * t + half + 1])
            m.then_inc(sem("sumsq"), mark("sumsq", key))
            act_root(key, 2)

        def dve_postnorm(key, factor, next_key):
            dve.wait_ge(sem("sumsq"), at("sumsq", key))
            pair = ssq[:, 0:4].rearrange("p (t x) -> p t x", x=2)
            V(dve.tensor_tensor(msq[:, 0:2], pair[:, :, 0], pair[:, :, 1], ALU.add))
            dve.tensor_scalar(msq[:, 0:2], msq[:, 0:2], 1.0 / D, 1e-6, ALU.mult, ALU.add)\
                .then_inc(sem("meansq"), mark("meansq", key))
            dve_recip(key, 2)
            dve.wait_ge(sem("rows_landed"), at("rows_landed", key))
            for t in range(NT):
                for half in range(2):
                    cut = slice(half * 512, (half + 1) * 512)
                    m = dve.scalar_tensor_tensor(out=hn[:, t, cut], in0=acc[:, 2 * t + half, :],
                                                 scalar=rsd[:, t:t + 1], in1=rows[:, 0, cut],
                                                 op0=ALU.mult, op1=ALU.mult)
                    m.then_inc(sem("acc_scaled"), mark("acc_scaled", (key, t, half)))
                    was_read(2 * t + half, key, "acc_scaled")
            dve.wait_ge(sem("acc_scaled"), latest("acc_scaled"))
            for t in range(NT):
                m = dve.scalar_tensor_tensor(out=h[:, t, :], in0=hn[:, t, :], scalar=factor, in1=h[:, t, :],
                                             op0=ALU.mult, op1=ALU.add)
            m.then_inc(sem("h_ready"), mark("h_ready", next_key))

        def dve_layernorm(key, with_acc, next_key):
            if with_acc == "experts":
                V(dve.scalar_tensor_tensor(out=h[:, :, :], in0=h[:, :, :], scalar=ALPHA, in1=ysum[:, :, :],
                                           op0=ALU.mult, op1=ALU.add))
                with dve.If(overflows(dve)):
                    dve_ffn("over", NE * MOEB, NE, True)
                    for t in range(NT):
                        for half in range(2):
                            dve.wait_ge(bank_full(2 * t + half), filled_at(2 * t + half, "over"))
                            cut = slice(half * 512, (half + 1) * 512)
                            dve.tensor_tensor(h[:, t, cut], h[:, t, cut], acc[:, 2 * t + half, :], ALU.add)\
                               .then_inc(sem("over_added"), 1)
                    dve.wait_ge(sem("over_added"), 4)
            elif with_acc:
                for t in range(NT):
                    for half in range(2):
                        dve.wait_ge(bank_full(2 * t + half), filled_at(2 * t + half, key))
                        cut = slice(half * 512, (half + 1) * 512)
                        m = dve.scalar_tensor_tensor(out=h[:, t, cut], in0=h[:, t, cut], scalar=ALPHA,
                                                     in1=acc[:, 2 * t + half, :], op0=ALU.mult, op1=ALU.add)
                        m.then_inc(sem("acc_scaled"), mark("acc_scaled", (key, t, half)))
                        was_read(2 * t + half, key, "acc_scaled")
                dve.wait_ge(sem("acc_scaled"), latest("acc_scaled"))
            else:
                dve.wait_ge(sem("h_ready"), at("h_ready", key))
            for t in range(NT):
                for half in range(2):
                    i = 2 * t + half
                    V(dve.bn_stats(stats[:, 6 * i:6 * i + 6], h[:, t, half * 512:(half + 1) * 512]))
                V(dve.bn_aggr(mv[:, 2 * t:2 * t + 2], stats[:, 12 * t:12 * t + 12]))
            dve.tensor_scalar(msq[:, 0:2], mv.rearrange("p (t x) -> p t x", x=2)[:, :, 1],
                                        1.0, 1e-5, ALU.mult, ALU.add).then_inc(sem("meansq"), mark("meansq", key))
            dve_recip(key, 2)
            dve.wait_ge(sem("rows_landed"), at("rows_landed", key))
            for t in range(NT):
                V(dve.tensor_scalar(h[:, t, :], h[:, t, :], mv[:, 2 * t:2 * t + 1], rsd[:, t:t + 1],
                                    ALU.subtract, ALU.mult))
                V(dve.tensor_tensor(h[:, t, :], h[:, t, :], rows[:, 0, :], ALU.mult))
                m = dve.tensor_tensor(h[:, t, :], h[:, t, :], rows[:, 1, :], ALU.add)
            m.then_inc(sem("h_ready"), mark("h_ready", next_key))

        def pool_rows(key, previous, gain, bias=None):
            if previous is not None:
                pool.wait_ge(sem("h_ready"), at("h_ready", previous))
            pool.dma_start(rows[:, 0, :], gain.partition_broadcast(P))\
                .then_inc(sem("rows_landed"), mark("rows_landed", key if bias is None else (key, 0), 16))
            if bias is not None:
                pool.dma_start(rows[:, 1, :], bias.partition_broadcast(P))\
                    .then_inc(sem("rows_landed"), mark("rows_landed", key, 16))

        silu = view(4096, NT, 256)
        hid = view(4608, NT, 256)
        hidT = view(5120, 2, T)

        def loop_blocks(engine, total, body, step):
            trips = (total - 2) // body
            step(0, -1)
            step(0, 0)
            with engine.Fori(0, trips) as i:
                for j in range(1, body + 1):
                    step(i, j)
            for n in range(2 + trips * body, total):
                step(trips, n - 1 - trips * body)

        def pe_ffn(key, total, body):
            r1, r2 = ring_pe["w1"], ring_pe["w2"]
            hid0, hidT0 = ev.base("hidden_ready", key), ev.base("hidT_ready", key)
            for b in (4, 5, 6):
                ev.start(f"bank_full{b}", key)
            ev.start("w2_used", key)
            full5, used2 = ev.count["bank_full5"], ev.count["w2_used"]

            def up(i, j):
                n1 = r1 + 1 + j
                pe.wait_ge(sem(f"w1_landed{n1 % RING}"), 32 * (n1 // RING + 1) + 32 * (body // RING) * i)
                slot = w1[:, n1 % RING, :].rearrange("p (t n) -> p t n", n=COLS)
                for t in range(NT):
                    if j < 0:
                        claim(4 + t)
                    else:
                        pe.wait_ge(sem("hidden_ready"), hid0 + 2 * j + t + 1 + 2 * body * i)
                    for k in range(KC):
                        m = pe.matmul(bank(4 + t), u[:, k, t * P:(t + 1) * P], slot[:, k, :],
                                      start=(k == 0), stop=(k == KC - 1))
                    m.then_inc(bank_full(4 + t), 1)

            def turn(i, j):
                if j < 0:
                    claim(6)
                pe.wait_ge(sem("hidden_ready"), hid0 + 2 * (j + 2) + 2 * body * i)
                for c in range(2):
                    for t in range(NT):
                        m = pe.transpose(bank(6)[:, c * T + t * P:c * T + (t + 1) * P],
                                         hid[:, t, c * P:(c + 1) * P], cst("ident"))
                m.then_inc(bank_full(6), 1)

            def down(i, j, first=False, last=False):
                if first:
                    claim(0, 1, 2, 3)
                n2 = r2 + 1 + j
                pe.wait_ge(sem(f"w2_landed{n2 % RING2}"), 16 * (n2 // RING2 + 1) + 16 * (body // RING2) * i)
                pe.wait_ge(sem("hidT_ready"), hidT0 + j + 2 + body * i)
                for t in range(NT):
                    for half in range(2):
                        for c in range(2):
                            m = pe.matmul(acc[:, 2 * t + half, :], hidT[:, c, t * P:(t + 1) * P],
                                          w2[:, n2 % RING2, c, half * 512:(half + 1) * 512],
                                          start=(first and c == 0), stop=(last and c == 1),
                                          skip_group_check=True)
                        if last:
                            m.then_inc(bank_full(2 * t + half), fill(2 * t + half, key))
                if not last:
                    m.then_inc(sem("w2_used"), 1)

            def step(i, j):
                up(i, j)
                if j >= 0:
                    down(i, j - 1, first=(j == 0))
                turn(i, j)

            loop_blocks(pe, total, body, step)
            trips = (total - 2) // body
            down(trips, total - 2 - trips * body, last=True)
            ring_pe["w1"] += total
            ring_pe["w2"] += total
            for b in (4, 5, 6):
                ev.count[f"bank_full{b}"] += total
                last_fill[b] = ("ffn", key)
            ev.count["w2_used"] += total - 1
            for n in range(total):
                released("w1", r1 + n, "bank_full5", full5 + n + 1)
                released("w2", r2 + n, "w2_used", used2 + n + 1)
            released("w2", r2 + total - 1, "bank_full3")

        def act_ffn(key, total, body):
            full0 = [ev.base(f"bank_full{b}", key) for b in (4, 5, 6)]
            ev.start("silu_ready", key)
            ev.start("hidT_ready", key)

            def step(i, j):
                for t in range(NT):
                    act.wait_ge(bank_full(4 + t), full0[t] + 2 + j + body * i)
                    act.activation(silu[:, t, :], bank(4 + t)[:, 0:256], ACT.Silu)\
                       .then_inc(sem("silu_ready"), 1)
                act.wait_ge(bank_full(6), full0[2] + 2 + j + body * i)
                act.activation(hidT[:, :, :], split(bank(6), 2), ACT.Copy).then_inc(sem("hidT_ready"), 1)

            loop_blocks(act, total, body, step)
            ev.count["silu_ready"] += 2 * total
            ev.count["hidT_ready"] += total
            was_read(6, ("ffn", key), "hidT_ready")

        def dve_ffn(key, total, body, moe):
            silu0 = ev.base("silu_ready", key)
            ev.start("hidden_ready", key)

            def step(i, j):
                for t in range(NT):
                    dve.wait_ge(sem("silu_ready"), silu0 + 2 * (1 + j) + t + 1 + 2 * body * i)
                    if moe:
                        e = (1 + j) % NE
                        m = dve.scalar_tensor_tensor(out=hid[:, t, :], in0=silu[:, t, :],
                                                     scalar=gates[:, t * NE + e:t * NE + e + 1],
                                                     in1=bank(4 + t)[:, 256:512], op0=ALU.mult, op1=ALU.mult)
                    else:
                        m = dve.tensor_tensor(hid[:, t, :], silu[:, t, :], bank(4 + t)[:, 256:512], ALU.mult)
                    m.then_inc(sem("hidden_ready"), 1)

            loop_blocks(dve, total, body, step)
            ev.count["hidden_ready"] += 2 * total
            for t in range(NT):
                was_read(4 + t, ("ffn", key), "hidden_ready")

        def sp_ffn(key, total, body, gate, up, down):
            r1, r2 = ring_sp["w1"], ring_sp["w2"]
            full5, used2 = ev.base("bank_full5", key), ev.base("w2_used", key)

            def step(i, n):
                n1, n2 = r1 + n, r2 + n
                if n < RING:
                    slot_free("w1")
                else:
                    sp.wait_ge(bank_full(5), full5 + n - RING + 1 + body * i)
                slot = w1[:, n1 % RING, :].rearrange("p (t n) -> p t n", n=COLS)
                for half, src in enumerate((gate(n, i), up(n, i))):
                    sp.dma_start(slot[:, :, half * 256:(half + 1) * 256], src)\
                      .then_inc(sem(f"w1_landed{n1 % RING}"), 16)
                if n < RING2:
                    slot_free("w2")
                else:
                    sp.wait_ge(sem("w2_used"), used2 + n - RING2 + 1 + body * i)
                sp.dma_start(w2[:, n2 % RING2, :, :], down(n, i)).then_inc(sem(f"w2_landed{n2 % RING2}"), 16)

            for n in range(RING):
                step(0, n)
                ring_sp["w1"] += 1
                ring_sp["w2"] += 1
            trips = (total - RING) // body
            with sp.Fori(0, trips) as i:
                for n in range(RING, RING + body):
                    step(i, n)
            for n in range(RING + trips * body, total):
                step(trips, n - trips * body)
            ring_sp["w1"] = r1 + total
            ring_sp["w2"] = r2 + total

        def dense_sources(wg, wu, wd, body):
            g, uu = (x.rearrange("(t p) n -> p t n", p=P) for x in (wg, wu))
            d = wd.rearrange("(b c p) n -> b p c n", c=2, p=P)
            return (lambda n, i: g[:, :, bass.ds(256 * n + 256 * body * i, 256)],
                    lambda n, i: uu[:, :, bass.ds(256 * n + 256 * body * i, 256)],
                    lambda n, i: d[bass.ds(n + body * i, 1)].rearrange("b p c n -> p (b c) n"))

        def moe_sources(wg, wu, wd):
            def cols_of(w):
                v = w.rearrange("e (t p) n -> e p t n", p=P)
                return lambda n, i: v[n % NE][:, :, bass.ds(256 * (n // NE) + 256 * i, 256)]
            d = wd.rearrange("e (b c p) n -> e b p c n", c=2, p=P)
            return (cols_of(wg), cols_of(wu),
                    lambda n, i: d[n % NE][bass.ds(n // NE + i, 1)].rearrange("b p c n -> p (b c) n"))

        BODY = 2 * MOEB
        msilu, mhid = view(0, 256), view(256, 256)
        mhidT = view(512, 2, P)
        mx = [view(1024 + 1024 * i, KC, P) for i in range(2)]
        mG, mW = view(3072, NT, P), view(3328, NT, P)
        mWT = [view(3584 + 256 * i, T) for i in range(2)]
        mye = view(4096, D)
        ysum = view(5120, NT, D)
        slot_of, gate_of = view(7168, NT, 16), view(7200, NT, 16)

        def pe_moe():
            r1, r2 = ring_pe["w1"], ring_pe["w2"]

            def prepare(i, e):
                pe.wait_ge(sem("moe_picked"), 2 * i + e + 1)
                for half in range(2):
                    if not (isinstance(i, int) and half == 0):
                        pe.wait_ge(sem("moe_moved"), 6 * i + 3 * e + half)
                    for c in range(4):
                        for t in range(NT):
                            k = 4 * half + c
                            m = pe.matmul(bank(7)[:, c * P:(c + 1) * P], h[:, t, k * P:(k + 1) * P], mG[:, t, :],
                                          start=(t == 0), stop=(t == NT - 1))
                    m.then_inc(sem("moe_prepared"), 1)
                pe.wait_ge(sem("moe_moved"), 6 * i + 3 * e + 2)
                for t in range(NT):
                    m = pe.transpose(bank(7)[:, t * P:(t + 1) * P], mW[:, t, :], cst("ident"))
                m.then_inc(sem("moe_prepared"), 1)

            def down(i, b):
                n2 = r2 + b
                pe.wait_ge(sem(f"w2_landed{n2 % RING2}"), 16 * (n2 // RING2 + 1) + 16 * (BODY // RING2) * i)
                pe.wait_ge(sem("moe_hidT"), BODY * i + b + 1)
                if b == MOEB:
                    pe.wait_ge(sem("moe_ye"), 4 * i + 2)
                for half in range(2):
                    for c in range(2):
                        m = pe.matmul(bank(half), mhidT[:, c, :], w2[:, n2 % RING2, c, half * 512:(half + 1) * 512],
                                      start=(b % MOEB == 0 and c == 0), stop=(b % MOEB == MOEB - 1 and c == 1),
                                      skip_group_check=True)
                m.then_inc(sem("moe_down"), 1)

            def scatter(i, e):
                pe.wait_ge(sem("moe_ye"), 4 * i + 2 * e + 2)
                for t in range(NT):
                    pe.wait_ge(sem("moe_added"), 8 * i + 4 * e + 2 * t + 1)
                    for half in range(2):
                        pe.matmul(bank(2 + half), mWT[e][:, t * P:(t + 1) * P], mye[:, half * 512:(half + 1) * 512],
                                  start=True, stop=True).then_inc(sem("moe_scattered"), 1)

            claim(0, 1, 2, 3, 4, 6, 7)
            prepare(0, 0)
            with pe.Fori(0, NE // 2) as i:
                for b in range(BODY):
                    e, c = b // MOEB, b % MOEB
                    n1 = r1 + b
                    pe.wait_ge(sem(f"w1_landed{n1 % RING}"), 32 * (n1 // RING + 1) + 32 * (BODY // RING) * i)
                    if c == 0:
                        pe.wait_ge(sem("moe_moved"), 6 * i + 3 * e + 3)
                    pe.wait_ge(sem("moe_hidden"), BODY * i + b + 1)
                    slot = w1[:, n1 % RING, :].rearrange("p (t n) -> p t n", n=COLS)
                    for k in range(KC):
                        m = pe.matmul(bank(4), mx[e][:, k, :], slot[:, k, :], start=(k == 0), stop=(k == KC - 1))
                    m.then_inc(sem("moe_up"), 1)
                    if b:
                        down(i, b - 1)
                    pe.wait_ge(sem("moe_hidden"), BODY * i + b + 2)
                    for k in range(2):
                        m = pe.transpose(bank(6)[:, k * P:(k + 1) * P], mhid[:, k * P:(k + 1) * P], cst("ident"))
                    m.then_inc(sem("moe_turned"), 1)
                    if b == MOEB + 2:
                        scatter(i, 0)
                    if c == 6:
                        prepare(i, e + 1)
                down(i, BODY - 1)
                scatter(i, 1)
            ring_pe["w1"] += NE * MOEB
            ring_pe["w2"] += NE * MOEB
            for n in range(NE * MOEB):
                released("w1", r1 + n, "moe_up", n + 1)
                released("w2", r2 + n, "moe_down", n + 1)
            for b in (0, 1, 2, 3, 4, 6, 7):
                last_fill[b] = "moe"

        def act_moe():
            def moved(i, e):
                for half in range(2):
                    act.wait_ge(sem("moe_prepared"), 6 * i + 3 * e + half + 1)
                    act.activation(mx[e % 2][:, 4 * half:4 * half + 4, :], split(bank(7), 4), ACT.Copy)\
                       .then_inc(sem("moe_moved"), 1)
                act.wait_ge(sem("moe_prepared"), 6 * i + 3 * e + 3)
                act.activation(mWT[e % 2][:, :], bank(7)[:, 0:T], ACT.Copy).then_inc(sem("moe_moved"), 1)

            def output(i, e):
                act.wait_ge(sem("moe_down"), BODY * i + MOEB * (e + 1))
                for half in range(2):
                    act.activation(mye[:, half * 512:(half + 1) * 512], bank(half), ACT.Copy)\
                       .then_inc(sem("moe_ye"), 1)

            moved(0, 0)
            with act.Fori(0, NE // 2) as i:
                for b in range(BODY):
                    act.wait_ge(sem("moe_up"), BODY * i + b + 1)
                    act.activation(msilu[:, :], bank(4)[:, 0:256], ACT.Silu).then_inc(sem("moe_silu"), 1)
                    if b == MOEB:
                        output(i, 0)
                    act.wait_ge(sem("moe_turned"), BODY * i + b + 1)
                    act.activation(mhidT[:, :, :], split(bank(6)[:, 0:256], 2), ACT.Copy).then_inc(sem("moe_hidT"), 1)
                    if b % MOEB == 6:
                        moved(i, b // MOEB + 1)
                output(i, 1)
            for b, name, count in ((0, "moe_ye", 2 * NE), (1, "moe_ye", 2 * NE), (6, "moe_hidT", NE * MOEB),
                                   (7, "moe_moved", 3 * NE + 3)):
                ev.seen[("read", b, "moe")] = (name, count)

        def dve_moe():
            def pick(i, e):
                if not isinstance(i, int):
                    dve.wait_ge(sem("moe_prepared"), 6 * i + 3 * e)
                for t in range(NT):
                    col = slot_of[:, t, bass.ds(2 * i + e, 1)]
                    dve.tensor_scalar(mG[:, t, :], cst("iota128"), col, None, ALU.is_equal)\
                       .then_inc(sem("moe_matrix"), 1)
                    m = dve.tensor_scalar(mW[:, t, :], cst("iota128"), col, gate_of[:, t, bass.ds(2 * i + e, 1)],
                                          ALU.is_equal, ALU.mult)
                    m.then_inc(sem("moe_picked" if t else "moe_matrix"), 1)

            def add(i, e):
                for t in range(NT):
                    for half in range(2):
                        dve.wait_ge(sem("moe_scattered"), 8 * i + 4 * e + 2 * t + half + 1)
                        cut = slice(half * 512, (half + 1) * 512)
                        dve.tensor_tensor(ysum[:, t, cut], ysum[:, t, cut], bank(2 + half), ALU.add)\
                           .then_inc(sem("moe_added"), 1)

            dve.memset(ysum[:, :, :], 0.0).then_inc(sem("moe_added"), 1)
            dve.memset(mhid[:, :], 0.0).then_inc(sem("moe_hidden"), 1)
            dve.wait_ge(sem("moe_added"), 1)
            dve.wait_ge(sem("moe_hidden"), 1)
            pick(0, 0)
            with dve.Fori(0, NE // 2) as i:
                for b in range(BODY):
                    dve.wait_ge(sem("moe_silu"), BODY * i + b + 1)
                    dve.tensor_tensor(mhid[:, :], msilu[:, :], bank(4)[:, 256:512], ALU.mult)\
                       .then_inc(sem("moe_hidden"), 1)
                    if b == MOEB + 2:
                        add(i, 0)
                    if b % MOEB == 6:
                        pick(i, b // MOEB + 1)
                add(i, 1)
                dve.wait_ge(sem("moe_added"), 8 * i + 9)
            for b, name, count in ((2, "moe_added", 4 * NE + 1), (3, "moe_added", 4 * NE + 1),
                                   (4, "moe_hidden", NE * MOEB + 1)):
                ev.seen[("read", b, "moe")] = (name, count)

        def sp_moe(wg, wu, wd):
            r1, r2 = ring_sp["w1"], ring_sp["w2"]
            g, uu = (x.rearrange("e (t p) n -> e p t n", p=P) for x in (wg, wu))
            d = wd.rearrange("e (b c p) n -> e b p c n", c=2, p=P)

            def step(i, n):
                e, c = n // MOEB, n % MOEB
                n1, n2 = r1 + n, r2 + n
                if n < RING:
                    slot_free("w1")
                else:
                    sp.wait_ge(sem("moe_up"), BODY * i + n - RING + 1)
                slot = w1[:, n1 % RING, :].rearrange("p (t n) -> p t n", n=COLS)
                for half, w in enumerate((g, uu)):
                    src = w[bass.ds(2 * i + e, 1)].rearrange("e p t n -> p (e t) n")[:, :, c * 256:(c + 1) * 256]
                    sp.dma_start(slot[:, :, half * 256:(half + 1) * 256], src)\
                      .then_inc(sem(f"w1_landed{n1 % RING}"), 16)
                if n < RING2:
                    slot_free("w2")
                else:
                    sp.wait_ge(sem("moe_down"), BODY * i + n - RING2 + 1)
                src = d[bass.ds(2 * i + e, 1)].rearrange("e b p c n -> p (e b c) n")[:, 2 * c:2 * c + 2, :]
                sp.dma_start(w2[:, n2 % RING2, :, :], src).then_inc(sem(f"w2_landed{n2 % RING2}"), 16)

            for n in range(RING):
                step(0, n)
                ring_sp["w1"] += 1
                ring_sp["w2"] += 1
            with sp.Fori(0, NE // 2 - 1) as i:
                for n in range(RING, RING + BODY):
                    step(i, n)
            for n in range(RING, BODY):
                step(NE // 2 - 1, n)
            ring_sp["w1"] = r1 + NE * MOEB
            ring_sp["w2"] = r2 + NE * MOEB

        def overflows(engine):
            engine.wait_ge(sem("most_tokens"), at("most_tokens", 0))
            return engine.value_load(most[0:1, 0:1], min_val=0, max_val=T) > SLOTS

        def dve_conv(name, key, dst, src, chunks, taps, weight, bias):
            ev.start(name, key)
            first = ev.count[name]
            for c in range(chunks):
                if bias:
                    m = dve.tensor_scalar(dst[:, c, :], src[:, c, 0:T], pcol(weight, c), pcol(bias, c),
                                          ALU.mult, ALU.add)
                else:
                    m = dve.tensor_scalar(dst[:, c, :], src[:, c, 0:T], pcol(weight, c), None, ALU.mult)
                m.then_inc(sem(name), 1)
            w0 = stack_at(weight)
            with dve.Fori(0, taps - 1) as k:
                for c in range(chunks):
                    dve.wait_ge(sem(name), first + c + 1 + chunks * k)
                    dve.scalar_tensor_tensor(out=dst[:, c, :], in0=src[:, c, bass.ds(k + 1, T)],
                                             scalar=par[:, bass.ds(k * chunks + (w0 + chunks + c), 1)],
                                             in1=dst[:, c, :], op0=ALU.mult, op1=ALU.add)\
                       .then_inc(sem(name), 1)
            ev.count[name] += chunks * taps
            ev.seen[(name, key)] = ev.count[name]

        yab = view(0, 16, T)
        cin = view(4096, 8, T + TAPS - 1)
        sq_c = view(4096, 8, T)
        hc = view(6384, 8, T)
        state = view(6384, 1024)
        sg = view(8432, 8, T)
        var_c = view(8432, T)
        xdt = view(8432, NT, 1024)
        xp = view(10480, 12, T + SCONV - 1)
        L = view(10480, 16, P)
        xds = view(12528, 1024)
        xc = view(13588, 12, T)
        y = view(13588, NT, 1024)
        zs = view(16660, NT, 1024)
        xs = view(18708, NT, 1024)
        cbm = view(20756, 2, P)
        BT = view(21012, 256)
        o = 21268
        wdt = view(o, KC, 16)
        dtx, dtl, dt, adt, acs, eac = (view(o + 128 + 32 * i, 32) for i in range(6))
        ea = view(o + 320, 16)
        dse = view(o + 336, 16)
        KEYS_A = [("g", 0, 1024), ("v", 0, 0), ("g", 1, 1536), ("v", 1, 512)]

        def pe_mixer_a():
            for name, i, _ in KEYS_A:
                pe_cols_fm(u, ("A", name, i))
            claim(6)
            pe.wait_ge(sem("wdt_landed"), 16)
            for t in range(NT):
                for k in range(KC):
                    m = pe.matmul(bank(6)[:, t * 16:(t + 1) * 16], u[:, k, t * P:(t + 1) * P], wdt[:, k, :],
                                  start=(k == 0), stop=(k == KC - 1))
            m.then_inc(bank_full(6), fill(6, ("A", "dt")))
            for i in range(3):
                pe_cols_fm(u, ("A", "xbc", i))
            for i in range(2):
                pe_cols_tm(u, ("A", "z", i))
            pe.wait_ge(sem("conv_tap"), at("conv_tap", "A"))
            claim(6)
            for c in range(8):
                m = pe.matmul(bank(6)[:, 0:T], cst("ones"), hc[:, c, :], start=(c == 0), stop=(c == 7))
            m.then_inc(bank_full(6), fill(6, ("A", "sum")))
            pe.wait_ge(sem("squared"), at("squared", "A"))
            claim(7)
            for c in range(8):
                m = pe.matmul(bank(7)[:, 0:T], cst("ones"), sq_c[:, c, :], start=(c == 0), stop=(c == 7))
            m.then_inc(bank_full(7), fill(7, ("A", "sumsq")))
            for t in range(NT):
                for b in range(2):
                    claim(4 + b)
                    pe.wait_ge(sem("xbc_ready"), at("xbc_ready", 4 * b + 3))
                    for c in range(4):
                        m = pe.transpose(bank(4 + b)[:, c * P:(c + 1) * P], xc[:, 4 * b + c, t * P:(t + 1) * P],
                                         cst("ident"))
                    m.then_inc(bank_full(4 + b), fill(4 + b, ("A", "xs", t)))
            pe.wait_ge(sem("xbc_ready"), at("xbc_ready", 11))
            claim(6)
            for g in range(2):
                m = pe.transpose(bank(6)[:, g * P:(g + 1) * P], xc[:, 8 + g, 0:P], cst("ident"))
            m.then_inc(bank_full(6), fill(6, ("A", "BT")))
            for t in range(NT):
                pe.wait_ge(sem("adt"), at("adt", "A"))
                claim(7)
                pe.matmul(bank(7)[:, 0:16], cst("upper"), adt[:, 16 * t:16 * t + 16], start=True, stop=True)
                pe.matmul(bank(7)[:, 16:32], cst("ones"), adt[:, 16 * t:16 * t + 16], start=True, stop=True)
                for g in range(2):
                    m = pe.matmul(bank(7)[:, P + g * P:P + (g + 1) * P], xc[:, 8 + g, t * P:(t + 1) * P],
                                  xc[:, 10 + g, t * P:(t + 1) * P], start=True, stop=True)
                m.then_inc(bank_full(7), fill(7, ("A", "col", t)))
                for b in range(4):
                    claim(b)
                    for i in range(4):
                        hh = 4 * b + i
                        m = pe.matmul(bank(b)[:, i * P:(i + 1) * P],
                                      adt[:, 16 * t + hh:16 * t + hh + 1].broadcast_to([P, P]), cst("upper"),
                                      start=True, stop=True)
                    m.then_inc(bank_full(b), fill(b, ("A", "row", t)))
                if t == 0:
                    pe.wait_ge(sem("xds"), at("xds", "A"))
                    pe.wait_ge(sem("BT"), at("BT", "A"))
                    for g in range(2):
                        claim(6 + g)
                        m = pe.matmul(bank(6 + g), BT[:, g * P:(g + 1) * P], xds[:, g * 512:(g + 1) * 512],
                                      start=True, stop=True)
                        m.then_inc(bank_full(6 + g), fill(6 + g, ("A", "state")))
                else:
                    pe.wait_ge(sem("state"), at("state", 1))
                    for g in range(2):
                        claim(6 + g)
                        m = pe.matmul(bank(6 + g), xc[:, 10 + g, P:T], state[:, g * 512:(g + 1) * 512],
                                      start=True, stop=True)
                        m.then_inc(bank_full(6 + g), fill(6 + g, ("A", "yoff")))
                pe.wait_ge(sem("weighted"), at("weighted", ("A", t)))
                claim(4, 5)
                for hh in range(16):
                    m = pe.matmul(bank(4 + hh // 8)[:, (hh % 8) * 64:(hh % 8 + 1) * 64], L[:, hh, :],
                                  xdt[:, t, hh * 64:(hh + 1) * 64], start=True, stop=True)
                    if hh % 8 == 7:
                        m.then_inc(bank_full(4 + hh // 8), fill(4 + hh // 8, ("A", "ydiag", t)))
            pe.wait_ge(sem("normed"), at("normed", ("A", "y", 1)))
            pe_to_fm(y, KC, ("A", "y"))
            pe_fm_wait(("A", "y"), KC)
            pe.wait_ge(sem("ya"), at("ya", 7))
            pe_rows_acc(yab, 16, "mixA")

        def act_mixer_a():
            for i in range(2):
                for b in range(2):
                    act.wait_ge(bank_full(4 + b), filled_at(4 + b, ("A", "g", i)))
                    act.activation(sg[:, 4 * i + 2 * b:4 * i + 2 * b + 2, :], split(bank(4 + b), 2),
                                        ACT.Sigmoid).then_inc(sem("sigma"), mark_read("sigma", 4 + b, ("A", "g", i)))
            act.wait_ge(sem("dtx"), at("dtx", "A"))
            A(act.activation(dtl[:, :], dtx[:, :], ACT.Abs))
            A(act.activation(dtl[:, :], dtl[:, :], ACT.Exp, scale=-1.0))
            act.activation(dtl[:, :], dtl[:, :], ACT.Ln, bias=1.0).then_inc(sem("dtl"), mark("dtl", "A"))
            act.activation(ea[:, :], alog, ACT.Exp).then_inc(sem("ea"), mark("ea", "A"))
            for i in range(3):
                for b in range(2):
                    act.wait_ge(bank_full(4 + b), filled_at(4 + b, ("A", "xbc", i)))
                    act.activation(xp[:, 4 * i + 2 * b:4 * i + 2 * b + 2, SCONV - 1:], split(bank(4 + b), 2),
                                        ACT.Copy).then_inc(sem("xbc_in"), mark_read("xbc_in", 4 + b, ("A", "xbc", i)))
            for i in range(2):
                for t in range(NT):
                    act.wait_ge(bank_full(4 + t), filled_at(4 + t, ("A", "z", i)))
                    act.activation(zs[:, t, i * 512:(i + 1) * 512], bank(4 + t), ACT.Silu)\
                        .then_inc(sem("zs"), mark_read("zs", 4 + t, ("A", "z", i)))
            act.wait_ge(sem("centred"), at("centred", "A"))
            act.activation(sq_c[:, :, :], hc[:, :, :], ACT.Square).then_inc(sem("squared"), mark("squared", "A"))
            act.wait_ge(sem("var_c"), at("var_c", "A"))
            act.activation(var_c[:, :], var_c[:, :], ACT.Sqrt).then_inc(sem("root_c"), mark("root_c", "A"))
            act.wait_ge(sem("scaled_c"), at("scaled_c", "A"))
            for c in range(8):
                act.activation(yab[:, c, :], hc[:, c, :], ACT.Silu, bias=pcol("conv_ln_b", c),
                                         scale=pcol("conv_ln_g", c)).then_inc(sem("ya"), mark("ya", c))
            act.wait_ge(sem("ssm_tap"), at("ssm_tap", "A"))
            for c in range(12):
                act.activation(xc[:, c, :], xc[:, c, :], ACT.Silu, bias=pcol("ssm_conv_b", c))\
                    .then_inc(sem("xbc_ready"), mark("xbc_ready", c))
            for t in range(NT):
                for b in range(2):
                    act.wait_ge(bank_full(4 + b), filled_at(4 + b, ("A", "xs", t)))
                    act.activation(xs[:, t, b * 512:(b + 1) * 512], bank(4 + b), ACT.Copy)\
                        .then_inc(sem("xs"), mark_read("xs", 4 + b, ("A", "xs", t)))
            act.wait_ge(bank_full(6), filled_at(6, ("A", "BT")))
            act.activation(BT[:, :], bank(6)[:, 0:256], ACT.Copy).then_inc(sem("BT"), mark("BT", "A"))
            was_read(6, ("A", "BT"), "BT")
            for t in range(NT):
                if t == 0:
                    act.wait_ge(sem("to_end"), at("to_end", "A"))
                    act.activation(dse[:, :], dse[:, :], ACT.Exp).then_inc(sem("dse"), mark("dse", "A"))
                act.wait_ge(sem("acs"), at("acs", ("A", t)))
                act.activation(eac[:, 16 * t:16 * t + 16], acs[:, 16 * t:16 * t + 16], ACT.Exp)\
                    .then_inc(sem("eac"), mark("eac", ("A", t)))
                act.wait_ge(sem("diff"), at("diff", ("A", t)))
                act.activation(L[:, :, :], L[:, :, :], ACT.Exp).then_inc(sem("decayed"), mark("decayed", ("A", t)))
                if t == 0:
                    for g in range(2):
                        act.wait_ge(bank_full(6 + g), filled_at(6 + g, ("A", "state")))
                        act.activation(state[:, g * 512:(g + 1) * 512], bank(6 + g), ACT.Copy)\
                            .then_inc(sem("state"), mark("state", g))
                        was_read(6 + g, ("A", "state"), "state")
            act.wait_ge(sem("gated"), at("gated", ("A", 1)))
            for t in range(NT):
                m = act.activation(L.rearrange("p a b -> p (a b)")[:, t * 1024:(t + 1) * 1024], y[:, t, :],
                                   ACT.Square, accum_out=ssq[:, t:t + 1])
            m.then_inc(sem("sumsq"), mark("sumsq", ("A", "y")))
            act_root(("A", "y"), 2)
            act_to_fm(yab[:, 8:16, :], KC, ("A", "y"), gain=lambda c: pcol("ssm_norm_g", c))

        def dve_mixer_a():
            dve.wait_ge(sem("fm_ready"), at("fm_ready", (("mixA", "pre"), 3)))
            V(dve.memset(cin[:, :, 0:TAPS - 1], 0.0))
            V(dve.memset(xp[:, :, 0:SCONV - 1], 0.0))
            for i in range(2):
                for b in range(2):
                    dve.wait_ge(bank_full(4 + b), filled_at(4 + b, ("A", "v", i)))
                    dve.wait_ge(sem("sigma"), at("sigma", ("read", 4 + b, ("A", "g", i))))
                    c = 4 * i + 2 * b
                    dve.tensor_tensor(cin[:, c:c + 2, TAPS - 1:], sg[:, c:c + 2, :], split(bank(4 + b), 2),
                                           ALU.mult)\
                                               .then_inc(sem("gated_in"), mark_read("gated_in", 4 + b, ("A", "v", i)))
            dve.wait_ge(sem("gated_in"), latest("gated_in"))
            dve.wait_ge(bank_full(6), filled_at(6, ("A", "dt")))
            dve.tensor_tensor(split(dtx, 2), split(bank(6)[:, 0:32], 2), bc(dtb, 1, [P, 2, 16]), ALU.add)\
                .then_inc(sem("dtx"), mark("dtx", "A"))
            was_read(6, ("A", "dt"), "dtx")
            dve_conv("conv_tap", "A", hc, cin, 8, TAPS, "conv_dw_w", "conv_dw_b")
            dve.wait_ge(bank_full(6), filled_at(6, ("A", "sum")))
            dve.scalar_tensor_tensor(out=hc[:, :, :], in0=bc(bank(6)[:, 0:T], 1, [P, 8, T]),
                                               scalar=-1.0 / 1024, in1=hc[:, :, :], op0=ALU.mult, op1=ALU.add)\
                                                   .then_inc(sem("centred"), mark("centred", "A"))
            was_read(6, ("A", "sum"), "centred")
            dve.wait_ge(sem("xbc_in"), at("xbc_in", ("read", 5, ("A", "xbc", 2))))
            dve_conv("ssm_tap", "A", xc, xp, 12, SCONV, "ssm_conv_w", None)
            dve.wait_ge(bank_full(7), filled_at(7, ("A", "sumsq")))
            dve.tensor_scalar(var_c[:, :], bank(7)[:, 0:T], 1.0 / 1024, 1e-6, ALU.mult, ALU.add)\
                .then_inc(sem("var_c"), mark("var_c", "A"))
            was_read(7, ("A", "sumsq"), "var_c")
            dve.wait_ge(sem("root_c"), at("root_c", "A"))
            V(dve.reciprocal(var_c[:, :], var_c[:, :]))
            dve.tensor_tensor(hc[:, :, :], hc[:, :, :], bc(var_c, 1, [P, 8, T]), ALU.mult)\
                .then_inc(sem("scaled_c"), mark("scaled_c", "A"))
            dve.wait_ge(sem("scaled_c"), latest("scaled_c"))
            dve.wait_ge(sem("dtl"), at("dtl", "A"))
            dve.wait_ge(sem("ea"), at("ea", "A"))
            V(dve.scalar_tensor_tensor(out=dt[:, :], in0=dtx[:, :], scalar=0.0, in1=dtl[:, :],
                                       op0=ALU.max, op1=ALU.add))
            dve.scalar_tensor_tensor(out=split(adt, 2), in0=split(dt, 2), scalar=-1.0,
                                               in1=bc(ea, 1, [P, 2, 16]), op0=ALU.mult, op1=ALU.mult)\
                                                   .then_inc(sem("adt"), mark("adt", "A"))
            h64 = [P, 16, 64]
            for t in range(NT):
                ts = slice(16 * t, 16 * t + 16)
                dve.wait_ge(bank_full(7), filled_at(7, ("A", "col", t)))
                dve.tensor_copy(acs[:, ts], bank(7)[:, 0:16]).then_inc(sem("acs"), mark("acs", ("A", t)))
                dve.wait_ge(sem("acs"), latest("acs"))
                if t == 0:
                    dve.tensor_tensor(dse[:, :], bank(7)[:, 16:32], acs[:, ts], ALU.subtract)\
                        .then_inc(sem("to_end"), mark("to_end", "A"))
                dve.tensor_tensor(cbm[:, :, :], split(bank(7)[:, P:3 * P], 2), bc(cst("upper"), 1, [P, 2, P]),
                                       ALU.mult).then_inc(sem("masked"), mark_read("masked", 7, ("A", "col", t)))
                for b in range(4):
                    dve.wait_ge(bank_full(b), filled_at(b, ("A", "row", t)))
                dve.tensor_tensor(L[:, :, :], acc[:, :, :].rearrange("p a (b l) -> p (a b) l", l=P),
                                       bc(acs[:, ts], 2, [P, 16, P]), ALU.subtract)\
                                           .then_inc(sem("diff0"), mark_read("diff0", 0, ("A", "row", t)))
                for b in range(1, 4):
                    was_read(b, ("A", "row", t), "diff0")
                dve.wait_ge(sem("diff0"), latest("diff0"))
                dve.tensor_scalar(L[:, :, :], L[:, :, :], 0.0, None, ALU.min)\
                    .then_inc(sem("diff"), mark("diff", ("A", t)))
                dve.wait_ge(sem("xs"), at("xs", ("read", 5, ("A", "xs", t))))
                V(dve.tensor_tensor(split(xdt[:, t, :], 16), split(xs[:, t, :], 16), bc(dt[:, ts], 2, h64),
                                    ALU.mult))
                if t == 0:
                    dve.wait_ge(sem("dse"), at("dse", "A"))
                    dve.tensor_tensor(split(xds, 16), split(xdt[:, 0, :], 16), bc(dse, 2, h64),
                                                ALU.mult).then_inc(sem("xds"), mark("xds", "A"))
                dve.wait_ge(sem("decayed"), at("decayed", ("A", t)))
                L4 = L.rearrange("p (g r) l -> p g r l", g=2)
                dve.tensor_tensor(L4, L4, bc(cbm, 2, [P, 2, 8, P]), ALU.mult)\
                    .then_inc(sem("weighted"), mark("weighted", ("A", t)))
                if t == 0:
                    dve.wait_ge(bank_full(5), filled_at(5, ("A", "xs", 1)))
                V(dve.tensor_tensor(split(y[:, t, :], 16), split(xs[:, t, :], 16), bc(dskip, 2, h64), ALU.mult))
                for b in range(2):
                    dve.wait_ge(bank_full(4 + b), filled_at(4 + b, ("A", "ydiag", t)))
                dve.tensor_tensor(split(y[:, t, :], 2), split(y[:, t, :], 2), duo[:, :, :], ALU.add)\
                    .then_inc(sem("y_diag"), mark_read("y_diag", 4, ("A", "ydiag", t)))
                was_read(5, ("A", "ydiag", t), "y_diag")
                dve.wait_ge(sem("y_diag"), latest("y_diag"))
                if t == 1:
                    for g in range(2):
                        dve.wait_ge(bank_full(6 + g), filled_at(6 + g, ("A", "yoff")))
                    dve.wait_ge(sem("eac"), at("eac", ("A", 1)))
                    dve.tensor_tensor(split(xds, 16), aux[:, :, :].rearrange("p a (b l) -> p (a b) l", l=64),
                                           bc(eac[:, 16:32], 2, h64), ALU.mult)\
                                               .then_inc(sem("y_off"), mark_read("y_off", 6, ("A", "yoff")))
                    was_read(7, ("A", "yoff"), "y_off")
                    dve.wait_ge(sem("y_off"), latest("y_off"))
                    V(dve.tensor_tensor(y[:, t, :], y[:, t, :], xds[:, :], ALU.add))
                dve.wait_ge(sem("zs"), at("zs", ("read", 5, ("A", "z", 1))))
                dve.tensor_tensor(y[:, t, :], y[:, t, :], zs[:, t, :], ALU.mult)\
                    .then_inc(sem("gated"), mark("gated", ("A", t)))
            dve_mean(("A", "y"), 2, 1.0 / 1024, 1e-6)
            dve_recip(("A", "y"), 2)
            for t in range(NT):
                dve.tensor_scalar(y[:, t, :], y[:, t, :], rsd[:, t:t + 1], None, ALU.mult)\
                    .then_inc(sem("normed"), mark("normed", ("A", "y", t)))

        qB, kB = view(4096, 12, T), view(7168, 12, T)
        vB = view(10240, NT, 3, 512)
        sB = [view(13312 + 768 * i, 768) for i in range(2)]
        pB = [view(14848 + 768 * i, 768) for i in range(2)]
        oB = view(16384, NT, 512)
        oBf = view(17408, 4, T)
        UNITS_B = [(hh, qt) for hh in range(8) for qt in range(NT)]

        def pair(tensor, n):
            return tensor.rearrange("p a n -> p (a n)")[:, 0:n]

        def pe_mixer_b():
            for i in range(3):
                pe_cols_fm(u, ("B", "q", i))
            for i in range(3):
                pe_cols_fm(u, ("B", "k", i))
            for i in range(3):
                pe_cols_tm(u, ("B", "v", i))
            pe.wait_ge(sem("qk_ready"), at("qk_ready", ("read", 5, ("B", "k", 2))))

            def scores(n):
                hh, qt = UNITS_B[n]
                nk, b0, r = (qt + 1) * P, 2 * (n % 2), 64 * (hh % 2)
                claim(b0, b0 + 1)
                dst = pair(acc[:, b0:b0 + 2, :], 1024)
                for g in range(3):
                    m = pe.matmul(dst[:, g * nk:(g + 1) * nk], qB[r:r + 64, 4 * g + hh // 2, qt * P:(qt + 1) * P],
                                  kB[r:r + 64, 4 * g + hh // 2, 0:nk], start=True, stop=True)
                m.then_inc(bank_full(b0), fill(b0, ("B", "s", n)))

            def values(n):
                hh, qt = UNITS_B[n]
                nk, b0 = (qt + 1) * P, 2 * (n % 2)
                blocks = 3 * (qt + 1)
                tb = (duo, aux)[n % 2]
                pe.wait_ge(sem("probs"), at("probs", ("B", n)))
                claim(4 + 2 * (n % 2), 5 + 2 * (n % 2))
                for i in range(blocks):
                    m = pe.transpose(pair(tb[:, :, :], 1024)[:, i * P:(i + 1) * P], sB[n % 2][:, i * P:(i + 1) * P],
                                     cst("ident"))
                m.then_inc(bank_full(4 + 2 * (n % 2)), fill(4 + 2 * (n % 2), ("B", "t", n)))
                pe.wait_ge(sem("probsT"), at("probsT", ("B", n)))
                for i in range(blocks):
                    g, kt = i // (qt + 1), i % (qt + 1)
                    m = pe.matmul(acc[:, b0 + 1, 448:512], pB[n % 2][:, i * P:(i + 1) * P],
                                  vB[:, kt, g, hh * 64:(hh + 1) * 64], start=(i == 0), stop=(i == blocks - 1))
                m.then_inc(bank_full(b0 + 1), fill(b0 + 1, ("B", "o", n)))

            scores(0)
            for n in range(len(UNITS_B)):
                if n + 1 < len(UNITS_B):
                    scores(n + 1)
                if n == 0:
                    pe.wait_ge(sem("v_ready"), at("v_ready", ("read", 5, ("B", "v", 2))))
                values(n)
            pe.wait_ge(sem("o_ready"), at("o_ready", ("B", len(UNITS_B) - 1)))
            pe_to_fm(oB, 4, ("B", "o"))
            pe_fm_wait(("B", "o"), 4)
            pe_rows_acc(oBf, 4, "mixB")

        def act_mixer_b():
            for name, dst, scale in (("q", qB, 0.125), ("k", kB, 1.0)):
                for i in range(3):
                    for b in range(2):
                        act.wait_ge(bank_full(4 + b), filled_at(4 + b, ("B", name, i)))
                        act.activation(dst[:, 4 * i + 2 * b:4 * i + 2 * b + 2, :], split(bank(4 + b), 2),
                                            ACT.Copy, scale=scale)\
                                                .then_inc(sem("qk_ready"), mark_read("qk_ready", 4 + b, ("B", name, i)))
            for n, (hh, qt) in enumerate(UNITS_B):
                w = 3 * (qt + 1) * P
                act.wait_ge(sem("negmax"), at("negmax", ("B", n)))
                act.activation(sB[n % 2][:, 0:w], sB[n % 2][:, 0:w], ACT.Exp,
                                         bias=smax[:, n % 2:n % 2 + 1], accum_out=ssum[:, n % 2:n % 2 + 1])\
                                             .then_inc(sem("probs"), mark("probs", ("B", n)))
                b = 4 + 2 * (n % 2)
                act.wait_ge(bank_full(b), filled_at(b, ("B", "t", n)))
                act.activation(pB[n % 2][:, 0:w], pair((duo, aux)[n % 2][:, :, :], w), ACT.Copy)\
                    .then_inc(sem("probsT"), mark("probsT", ("B", n)))
                was_read(b, ("B", "t", n), "probsT")
            act_to_fm(oBf, 4, ("B", "o"))

        def dve_mixer_b():
            for i in range(3):
                for t in range(NT):
                    dve.wait_ge(bank_full(4 + t), filled_at(4 + t, ("B", "v", i)))
                    dve.tensor_copy(vB[:, t, i, :], bank(4 + t))\
                        .then_inc(sem("v_ready"), mark_read("v_ready", 4 + t, ("B", "v", i)))

            def softmax(n):
                hh, qt = UNITS_B[n]
                nk, b0, w = (qt + 1) * P, 2 * (n % 2), 3 * (qt + 1) * P
                slope = 2.0 ** -(hh + 1)
                off = cat[f"dist{qt}0"][0]
                dve.wait_ge(bank_full(b0), filled_at(b0, ("B", "s", n)))
                if n >= 2:
                    dve.wait_ge(bank_full(4 + 2 * (n % 2)), filled_at(4 + 2 * (n % 2), ("B", "t", n - 2)))
                m = dve.scalar_tensor_tensor(out=sB[n % 2][:, 0:w], in0=con[:, off:off + w], scalar=-slope,
                                             in1=pair(acc[:, b0:b0 + 2, :], w), op0=ALU.mult, op1=ALU.add)
                m.then_inc(sem("biased"), mark_read("biased", b0, ("B", "s", n)))
                dve.wait_ge(sem("biased"), latest("biased"))
                dve.tensor_reduce(smax[:, n % 2:n % 2 + 1], sB[n % 2][:, 0:w], AX.X, ALU.max,
                                            negate=True).then_inc(sem("negmax"), mark("negmax", ("B", n)))

            def divide(n):
                hh, qt = UNITS_B[n]
                dve.wait_ge(sem("probs"), at("probs", ("B", n)))
                V(dve.reciprocal(prob[:, n % 2:n % 2 + 1], ssum[:, n % 2:n % 2 + 1]))
                dve.wait_ge(bank_full(2 * (n % 2) + 1), filled_at(2 * (n % 2) + 1, ("B", "o", n)))
                m = dve.tensor_scalar(oB[:, qt, hh * 64:(hh + 1) * 64], acc[:, 2 * (n % 2) + 1, 448:512],
                                      prob[:, n % 2:n % 2 + 1], None, ALU.mult)
                m.then_inc(sem("o_ready"), mark("o_ready", ("B", n)))
                was_read(2 * (n % 2) + 1, ("B", "o", n), "o_ready")

            softmax(0)
            for n in range(len(UNITS_B)):
                if n + 1 < len(UNITS_B):
                    softmax(n + 1)
                divide(n)

        merged = view(0, NT, D)
        cF = view(2048, KC, T)
        rqk = view(4096, 8, T)
        rtmp = view(6144, 2, T)
        rv, rg = view(6656, NT, D), view(8704, NT, D)
        rS = [view(10752 + 384 * i, 384) for i in range(2)]
        ro = view(11520, NT, D)
        rj = view(13568, NT, D)
        gA = view(15616, NT, D)

        def pe_gate(l, name):
            for i in range(2):
                pe_cols_tm(u, (l, name, i))

        def act_gate(l, name, dst):
            for i in range(2):
                for t in range(NT):
                    act.wait_ge(bank_full(4 + t), filled_at(4 + t, (l, name, i)))
                    act.activation(dst[:, t, i * 512:(i + 1) * 512], bank(4 + t), ACT.Sigmoid)\
                        .then_inc(sem("gate_ready"), mark_read("gate_ready", 4 + t, (l, name, i)))

        def dve_merge(l, name, gate, key):
            dve.wait_ge(sem("gate_ready"), at("gate_ready", ("read", 5, (l, name, 1))))
            for t in range(NT):
                for half in range(2):
                    dve.wait_ge(bank_full(2 * t + half), filled_at(2 * t + half, key))
                    cut = slice(half * 512, (half + 1) * 512)
                    dst = merged if name == "ga" else gate
                    m = dve.tensor_tensor(dst[:, t, cut], gate[:, t, cut], acc[:, 2 * t + half, :], ALU.mult)
                    m.then_inc(sem("merging"), mark_read("merging", 2 * t + half, key))
            dve.wait_ge(sem("merging"), latest("merging"))
            if name != "ga":
                for t in range(NT):
                    dve.tensor_tensor(merged[:, t, :], merged[:, t, :], gate[:, t, :], ALU.add)\
                        .then_inc(sem("merged"), mark("merged", (l, name, t)))
                dve.wait_ge(sem("merged"), latest("merged"))

        def pe_retention(l):
            pe_cols_fm(u, (l, "rq"))
            pe_cols_fm(u, (l, "rk"))
            for name in ("rv", "rg"):
                for i in range(2):
                    pe_cols_tm(u, (l, name, i))
            pe_gate(l, "ga")
            pe.wait_ge(sem("rotated"), at("rotated", (l, 3)))
            pe.wait_ge(sem("rv_ready"), at("rv_ready", ("read", 5, (l, "rv", 1))))

            def scores(hh):
                b = 6 + hh % 2
                claim(b)
                pe.matmul(bank(b)[:, 0:T], rqk[:, 4 + hh, 0:P], rqk[:, hh, :], start=True, stop=True)
                m = pe.matmul(bank(b)[:, T:T + P], rqk[:, 4 + hh, P:T], rqk[:, hh, P:T], start=True, stop=True)
                m.then_inc(bank_full(b), fill(b, (l, "rs", hh)))

            def values(hh):
                pe.wait_ge(sem("decayed_scores"), at("decayed_scores", (l, hh)))
                if hh == 0:
                    claim(0, 1, 2, 3)
                half, o0 = hh // 2, (hh % 2) * 256
                s = rS[hh % 2]
                v = [rv[:, t, hh * 256:(hh + 1) * 256] for t in range(NT)]
                m0 = pe.matmul(acc[:, half, o0:o0 + 256], s[:, 0:P], v[0], start=True, stop=True)
                pe.matmul(acc[:, 2 + half, o0:o0 + 256], s[:, P:T], v[0], start=True, stop=False)
                m1 = pe.matmul(acc[:, 2 + half, o0:o0 + 256], s[:, T:T + P], v[1], start=False, stop=True)
                if hh % 2:
                    m0.then_inc(bank_full(half), fill(half, (l, "ro")))
                    m1.then_inc(bank_full(2 + half), fill(2 + half, (l, "ro")))
                else:
                    m1.then_inc(sem("head_out"), mark("head_out", (l, hh)))

            scores(0)
            for hh in range(4):
                if hh < 3:
                    scores(hh + 1)
                values(hh)
            pe.wait_ge(sem("ro_ready"), at("ro_ready", (l, 1)))
            pe_to_fm(ro, KC, (l, "ro"))
            pe_fm_wait((l, "ro"), KC)
            pe_rows_acc(cF, KC, (l, "ya"))

        def act_retention(l):
            for i in range(2):
                for t in range(NT):
                    act.wait_ge(bank_full(4 + t), filled_at(4 + t, (l, "rv", i)))
                    act.activation(rv[:, t, i * 512:(i + 1) * 512], bank(4 + t), ACT.Copy)\
                        .then_inc(sem("rv_ready"), mark_read("rv_ready", 4 + t, (l, "rv", i)))
            for i in range(2):
                for t in range(NT):
                    act.wait_ge(bank_full(4 + t), filled_at(4 + t, (l, "rg", i)))
                    act.activation(rg[:, t, i * 512:(i + 1) * 512], bank(4 + t), ACT.Silu)\
                        .then_inc(sem("rg_ready"), mark_read("rg_ready", 4 + t, (l, "rg", i)))
            act_gate(l, "ga", gA)
            for t in range(NT):
                for hh in range(4):
                    act.wait_ge(bank_full(2 * t + hh // 2), filled_at(2 * t + hh // 2, (l, "ro")))
                    m = act.activation(rj[:, t, hh * 256:(hh + 1) * 256],
                                       acc[:, 2 * t + hh // 2, (hh % 2) * 256:(hh % 2 + 1) * 256],
                                       ACT.Square, accum_out=ssq[:, 4 * t + hh:4 * t + hh + 1])
            m.then_inc(sem("sumsq"), mark("sumsq", (l, "ro")))
            act_root((l, "ro"), 8)
            act_to_fm(cF, KC, (l, "ro"))

        def dve_retention(l):
            for i, name in enumerate(("rq", "rk")):
                for b in range(2):
                    dve.wait_ge(bank_full(4 + b), filled_at(4 + b, (l, name)))
                    n = 2 * i + b
                    dst = rqk[:, 4 * i + 2 * b:4 * i + 2 * b + 2, :]
                    x = split(bank(4 + b), 2)
                    for lo, hi in ((0, 64), (64, 128)):
                        V(dve.tensor_tensor(rtmp[lo:lo + 64, :, :] if lo else rtmp[0:64, :, :],
                                            x[64 - lo:128 - lo, :, :],
                                            bc(cst("sin")[64 - lo:128 - lo, :], 1, [64, 2, T]), ALU.mult))
                    dve.tensor_tensor(dst, x, bc(cst("cos"), 1, [P, 2, T]), ALU.mult)\
                        .then_inc(sem("cos_part"), mark_read("cos_part", 4 + b, (l, name)))
                    dve.wait_ge(sem("cos_part"), latest("cos_part"))
                    dve.tensor_tensor(dst, dst, rtmp[:, :, :], ALU.add)\
                        .then_inc(sem("rotated"), mark("rotated", (l, n)))
                    dve.wait_ge(sem("rotated"), latest("rotated"))
            for hh in range(4):
                b = 6 + hh % 2
                dve.wait_ge(bank_full(b), filled_at(b, (l, "rs", hh)))
                if hh >= 2:
                    if hh == 2:
                        dve.wait_ge(sem("head_out"), at("head_out", (l, 0)))
                    else:
                        dve.wait_ge(bank_full(2), filled_at(2, (l, "ro")))
                dec = cst(f"decay{hh}")
                dve.tensor_tensor(rS[hh % 2][:, 0:T], bank(b)[:, 0:T], dec, ALU.mult)\
                   .then_inc(sem("scores_part"), 1)
                m = dve.tensor_tensor(rS[hh % 2][:, T:T + P], bank(b)[:, T:T + P], dec[:, 0:P], ALU.mult)
                m.then_inc(sem("decayed_scores"), mark("decayed_scores", (l, hh)))
                was_read(b, (l, "rs", hh), "decayed_scores")
            dve_mean((l, "ro"), 8, 1.0 / 256, 1e-6)
            dve_recip((l, "ro"), 8)
            dve.wait_ge(sem("rg_ready"), at("rg_ready", ("read", 5, (l, "rg", 1))))
            for t in range(NT):
                x = acc[:, 2 * t:2 * t + 2, :].rearrange("p a (b n) -> p (a b) n", n=256)
                for b in range(2):
                    dve.wait_ge(bank_full(2 * t + b), filled_at(2 * t + b, (l, "ro")))
                dve.tensor_tensor(split(ro[:, t, :], 4), x, bc(rsd[:, 4 * t:4 * t + 4], 2, [P, 4, 256]),
                                       ALU.mult).then_inc(sem("ro_scaled"), mark_read("ro_scaled", 2 * t, (l, "ro")))
                was_read(2 * t + 1, (l, "ro"), "ro_scaled")
                dve.wait_ge(sem("ro_scaled"), latest("ro_scaled"))
                dve.tensor_tensor(ro[:, t, :], ro[:, t, :], rg[:, t, :], ALU.mult)\
                    .then_inc(sem("ro_ready"), mark("ro_ready", (l, t)))
            dve_merge(l, "ga", gA, (l, "ya"))

        hQ, hZ, hK, hB = (view(4096 + 2048 * i, 8, T) for i in range(4))
        hKT, hKS, hG = (view(12288 + 2048 * i, 8, T) for i in range(3))
        hV = view(18432, NT, D)
        hstate = view(6144, 16, P)
        hvx = [view(8192 + 1024 * i, 8, P) for i in range(2)]
        hksT, hAT = view(20480, NT, P), view(20736, NT, P)
        hdec = view(20992, 8, 16)
        gB = view(14336, NT, D)

        def flat(x):
            return x.rearrange("p a b -> p (a b)")

        def pe_hgrn(l):
            for name in ("hq", "hf"):
                for i in range(2):
                    pe_cols_fm(u, (l, name, i))
            for i in range(2):
                pe_cols_tm(u, (l, "hi", i))
            for i in range(2):
                pe_cols_fm(u, (l, "hg", i))
            pe.wait_ge(sem("h_factors"), at("h_factors", l))
            for hh in range(8):
                claim(6)
                for t in range(NT):
                    m = pe.transpose(bank(6)[:, t * P:(t + 1) * P], hKS[:, hh, t * P:(t + 1) * P], cst("ident"))
                m.then_inc(bank_full(6), fill(6, (l, "ksT", hh)))
                claim(7)
                for t in range(NT):
                    m = pe.matmul(bank(7)[:, t * P:(t + 1) * P], hKT[:, hh, t * P:(t + 1) * P],
                                  hQ[:, hh, t * P:(t + 1) * P], start=True, stop=True)
                m.then_inc(bank_full(7), fill(7, (l, "AT", hh)))
                pe.wait_ge(sem("ksT"), at("ksT", (l, hh)))
                for t in range(NT):
                    pe.wait_ge(sem("vx"), at("vx", (l, hh, t)))
                    for half in range(2):
                        b = 2 * t + half
                        claim(b)
                        m = pe.matmul(bank(b), hksT[:, t, :], flat(hvx[t])[:, half * 512:(half + 1) * 512],
                                      start=True, stop=True)
                        m.then_inc(bank_full(b), fill(b, (l, "U", hh)))
                ob = 4 + hh % 2
                claim(ob)
                pe.wait_ge(sem("AT"), at("AT", (l, hh)))
                for t in range(NT):
                    pe.matmul(bank(ob)[:, t * P:(t + 1) * P], hV[:, t, hh * P:(hh + 1) * P], hAT[:, t, :],
                              start=True, stop=False, skip_group_check=True)
                    for j in range(max(8 * t, 1), 8 * t + 8):
                        if j in (1, 8):
                            pe.wait_ge(sem("hstate"), at("hstate", (l, hh, 7 if j == 1 else 15)))
                        m = pe.matmul(bank(ob)[:, 16 * j:16 * j + 16], hstate[:, j, :],
                                      hQ[:, hh, 16 * j:16 * j + 16], start=False, stop=(j == 8 * t + 7),
                                      skip_group_check=True)
                m.then_inc(bank_full(ob), fill(ob, (l, "ho", hh)))
            pe.wait_ge(sem("squared"), at("squared", (l, "ho")))
            for b in range(4):
                claim(b)
                m = pe.matmul(bank(b), cst("ones"), flat(hB)[:, b * 512:(b + 1) * 512], start=True, stop=True)
                m.then_inc(bank_full(b), fill(b, (l, "hsum")))
            pe_gate(l, "gb")
            pe.wait_ge(sem("hgrn_out"), at("hgrn_out", l))
            pe_rows_acc(cF, KC, (l, "yb"))

        def act_hgrn(l):
            for name, dst, fn in (("hq", hQ, ACT.Copy), ("hf", hZ, ACT.Copy)):
                for i in range(2):
                    for b in range(2):
                        act.wait_ge(bank_full(4 + b), filled_at(4 + b, (l, name, i)))
                        act.activation(dst[:, 4 * i + 2 * b:4 * i + 2 * b + 2, :], split(bank(4 + b), 2), fn)\
                            .then_inc(sem("hqf"), mark_read("hqf", 4 + b, (l, name, i)))
            act.wait_ge(sem("hqf"), latest("hqf"))
            A(act.activation(flat(hKT), flat(hZ), ACT.Abs))
            A(act.activation(flat(hKT), flat(hKT), ACT.Exp, scale=-1.0))
            act.activation(flat(hKT), flat(hKT), ACT.Ln, bias=1.0).then_inc(sem("soft"), mark("soft", (l, 0)))
            for i in range(2):
                for t in range(NT):
                    act.wait_ge(bank_full(4 + t), filled_at(4 + t, (l, "hi", i)))
                    act.activation(hV[:, t, i * 512:(i + 1) * 512], bank(4 + t), ACT.Copy)\
                        .then_inc(sem("hV"), mark_read("hV", 4 + t, (l, "hi", i)))
            act.wait_ge(sem("merging"), at("merging", ("read", 3, (l, "ya"))))
            for i in range(2):
                for b in range(2):
                    act.wait_ge(bank_full(4 + b), filled_at(4 + b, (l, "hg", i)))
                    act.activation(hG[:, 4 * i + 2 * b:4 * i + 2 * b + 2, :], split(bank(4 + b), 2), ACT.Silu)\
                        .then_inc(sem("hG"), mark_read("hG", 4 + b, (l, "hg", i)))
            act.wait_ge(sem("logk"), at("logk", l))
            act.activation(flat(hK), flat(hK), ACT.Exp).then_inc(sem("hK"), mark("hK", l))
            if l == 1:
                act.wait_ge(sem("logdiff"), at("logdiff", l))
                A(act.activation(flat(hKT), flat(hKT), ACT.Abs))
                A(act.activation(flat(hKT), flat(hKT), ACT.Exp, scale=-1.0))
                act.activation(flat(hKT), flat(hKT), ACT.Ln, bias=1.0).then_inc(sem("soft"), mark("soft", (l, 1)))
            act.wait_ge(sem("bcum"), at("bcum", l))
            act.activation(flat(hB), flat(hZ), ACT.Exp).then_inc(sem("expb"), mark("expb", (l, 0)))
            act.activation(flat(hKT), flat(hZ), ACT.Exp, scale=-1.0).then_inc(sem("expb"), mark("expb", (l, 1)))
            act.wait_ge(sem("to_block_end"), at("to_block_end", l))
            act.activation(flat(hKS), flat(hKS), ACT.Exp).then_inc(sem("expb"), mark("expb", (l, 2)))
            for hh in range(8):
                act.wait_ge(bank_full(6), filled_at(6, (l, "ksT", hh)))
                act.activation(flat(hksT), bank(6)[:, 0:T], ACT.Copy).then_inc(sem("ksT"), mark("ksT", (l, hh)))
                was_read(6, (l, "ksT", hh), "ksT")
                act.wait_ge(bank_full(4 + hh % 2), filled_at(4 + hh % 2, (l, "ho", hh)))
                act.activation(hQ[:, hh, :], bank(4 + hh % 2)[:, 0:T], ACT.Copy)\
                    .then_inc(sem("ho"), mark("ho", (l, hh)))
                was_read(4 + hh % 2, (l, "ho", hh), "ho")
            act.wait_ge(sem("ho"), latest("ho"))
            act.activation(flat(hB), flat(hQ), ACT.Square).then_inc(sem("squared"), mark("squared", (l, "ho")))
            act.wait_ge(sem("hvar"), at("hvar", (l, 3)))
            act.activation(flat(hKT), flat(hKT), ACT.Sqrt).then_inc(sem("hroot"), mark("hroot", l))
            act_gate(l, "gb", gB)

        def dve_hgrn(l):
            bcb = [P, 8, T]
            dve.wait_ge(sem("soft"), at("soft", (l, 0)))
            V(dve.scalar_tensor_tensor(out=flat(hB), in0=flat(hZ), scalar=0.0, in1=flat(hKT),
                                       op0=ALU.min, op1=ALU.subtract))
            if l == 0:
                dve.tensor_tensor(flat(hK), flat(hB), flat(hZ), ALU.subtract).then_inc(sem("logk"), mark("logk", l))
            else:
                V(dve.tensor_tensor(hB[:, :, :], hB[:, :, :], bc(lbC[:, 0:8], 2, bcb), ALU.add))
                dve.tensor_tensor(flat(hK), flat(hB), flat(hZ), ALU.subtract).then_inc(sem("logk"), mark("logk", l))
                dve.tensor_tensor(hKT[:, :, :], hB[:, :, :], bc(lbA[:, 0:8], 2, bcb), ALU.subtract)\
                    .then_inc(sem("logdiff"), mark("logdiff", l))
                V(dve.tensor_tensor(hB[:, :, :], hB[:, :, :], bc(lbA[:, 0:8], 2, bcb), ALU.max))
                dve.wait_ge(sem("soft"), at("soft", (l, 1)))
                V(dve.tensor_tensor(flat(hB), flat(hB), flat(hKT), ALU.add))
            V(dve.memset(flat(hKS), 1.0))
            V(dve.memset(flat(hKS).rearrange("p (a b) -> p a b", b=16)[:, :, 0:1], 0.0))
            dve.wait_ge(sem("logk"), latest("logk"))
            dve.tensor_tensor_scan(flat(hZ), flat(hKS), flat(hB), 0.0, ALU.mult, ALU.add)\
                .then_inc(sem("bcum"), mark("bcum", l))
            dve.wait_ge(sem("bcum"), latest("bcum"))
            blocks = flat(hZ).rearrange("p (a b) -> p a b", b=16)
            dve.tensor_tensor(flat(hKS).rearrange("p (a b) -> p a b", b=16),
                                        blocks[:, :, 15:16].broadcast_to([P, P, 16]), blocks, ALU.subtract)\
                                            .then_inc(sem("to_block_end"), mark("to_block_end", l))
            dve.wait_ge(sem("expb"), at("expb", (l, 0)))
            V(dve.tensor_copy(flat(hdec), flat(hB).rearrange("p (a b) -> p a b", b=16)[:, :, 15]))
            V(dve.tensor_tensor(flat(hQ), flat(hQ), flat(hB), ALU.mult))
            dve.wait_ge(sem("hK"), at("hK", l))
            dve.wait_ge(sem("expb"), at("expb", (l, 1)))
            V(dve.tensor_tensor(flat(hKT), flat(hKT), flat(hK), ALU.mult))
            dve.wait_ge(sem("expb"), at("expb", (l, 2)))
            dve.tensor_tensor(flat(hKS), flat(hKS), flat(hK), ALU.mult)\
                .then_inc(sem("h_factors"), mark("h_factors", l))
            dve.wait_ge(sem("h_factors"), latest("h_factors"))
            dve.wait_ge(sem("hV"), at("hV", ("read", 5, (l, "hi", 1))))
            for hh in range(8):
                for t in range(NT):
                    if hh:
                        dve.wait_ge(bank_full(2 * t + 1), filled_at(2 * t + 1, (l, "U", hh - 1)))
                    v = bc(hV[:, t, hh * P:(hh + 1) * P], 1, [P, 8, P])
                    dve.tensor_tensor(hvx[t][:, :, :], v, bc(cst("block"), 2, [P, 8, P]), ALU.mult)\
                        .then_inc(sem("vx"), mark("vx", (l, hh, t)))
                dve.wait_ge(bank_full(7), filled_at(7, (l, "AT", hh)))
                if hh:
                    dve.wait_ge(bank_full(4 + (hh - 1) % 2), filled_at(4 + (hh - 1) % 2, (l, "ho", hh - 1)))
                dve.tensor_tensor(hAT[:, :, :], split(bank(7)[:, 0:T], 2),
                                            bc(cst("blockcausal"), 1, [P, 2, P]), ALU.mult)\
                                                .then_inc(sem("AT"), mark("AT", (l, hh)))
                was_read(7, (l, "AT", hh), "AT")
                for j in range(1, 16):
                    dve.wait_ge(bank_full((j - 1) // 4), filled_at((j - 1) // 4, (l, "U", hh)))
                    U = bank((j - 1) // 4)[:, ((j - 1) % 4) * P:((j - 1) % 4 + 1) * P]
                    if j == 1:
                        m = dve.tensor_copy(hstate[:, j, :], U)
                    else:
                        m = dve.scalar_tensor_tensor(out=hstate[:, j, :], in0=hstate[:, j - 1, :],
                                                     scalar=hdec[:, hh, j - 1:j], in1=U, op0=ALU.mult, op1=ALU.add)
                    m.then_inc(sem("hstate"), mark("hstate", (l, hh, j)))
                    if j % 4 == 0 or j == 15:
                        was_read((j - 1) // 4, (l, "U", hh), "hstate")
                    dve.wait_ge(sem("hstate"), latest("hstate"))
            for b in range(4):
                dve.wait_ge(bank_full(b), filled_at(b, (l, "hsum")))
                dve.tensor_scalar(flat(hKT)[:, b * 512:(b + 1) * 512], bank(b), 1.0 / 128, 1e-6,
                                            ALU.mult, ALU.add).then_inc(sem("hvar"), mark("hvar", (l, b)))
                was_read(b, (l, "hsum"), "hvar")
            dve.wait_ge(sem("hroot"), at("hroot", l))
            V(dve.reciprocal(flat(hKT), flat(hKT)))
            V(dve.tensor_tensor(flat(hQ), flat(hQ), flat(hKT), ALU.mult))
            dve.wait_ge(sem("hG"), at("hG", ("read", 5, (l, "hg", 1))))
            dve.scalar_tensor_tensor(out=flat(cF), in0=flat(hQ), scalar=pcol("hgrn_norm_g_2", l),
                                               in1=flat(hG), op0=ALU.mult, op1=ALU.mult)\
                                                   .then_inc(sem("hgrn_out"), mark("hgrn_out", l))
            dve_merge(l, "gb", gB, (l, "yb"))

        wq, wk = view(4096, 8, T), view(6144, 4, T)
        wv = view(7168, NT, 256)
        wS = [view(7680 + 1024 * i, 1024) for i in range(2)]
        wP = [view(9728 + 1024 * i, 1024) for i in range(2)]
        wo = view(11776, NT, D)
        gC = view(13824, NT, D)
        HEAD_AT = (0, 2, 1, 3)
        UNITS_W = [(j, qt) for j in range(4) for qt in range(NT)]

        def pe_swa(l):
            for i in range(2):
                pe_cols_fm(u, (l, "sq", i))
            slot = arrived().rearrange("p (t n) -> p t n", n=COLS)
            for b in range(2):
                claim(4 + b)
                for c in range(2):
                    j = 2 * b + c
                    for rep in range(2):
                        for k in range(KC):
                            m = pe.matmul(bank(4 + b)[64 * rep:64 * rep + 64, c * T:(c + 1) * T],
                                          slot[:, k, j * 64:(j + 1) * 64], u[:, k, :],
                                          start=(k == 0), stop=(k == KC - 1))
                m.then_inc(bank_full(4 + b), fill(4 + b, (l, "sk")))
            claim(6)
            for t in range(NT):
                for k in range(KC):
                    m = pe.matmul(bank(6)[:, t * 256:(t + 1) * 256], u[:, k, t * P:(t + 1) * P],
                                  slot[:, k, 256:512], start=(k == 0), stop=(k == KC - 1))
            m.then_inc(bank_full(6), fill(6, (l, "sv")))
            released_last("bank_full6")
            pe_gate(l, "gc")
            pe.wait_ge(sem("w_ready"), at("w_ready", ("read", 6, (l, "sv"))))

            def scores(n):
                j, qt = UNITS_W[n]
                nk, b0 = (qt + 1) * P, 2 * (n % 2)
                claim(b0, b0 + 1)
                for r in range(4):
                    lo = 64 * (r % 2)
                    c0 = 256 * (r // 2)
                    m = pe.matmul(acc[:, b0 + r % 2, c0:c0 + nk],
                                  wq[lo:lo + 64, 2 * j + r // 2, qt * P:(qt + 1) * P],
                                  wk[lo:lo + 64, j, 0:nk], start=True, stop=True)
                m.then_inc(bank_full(b0), fill(b0, (l, "ws", n)))

            def values(n):
                j, qt = UNITS_W[n]
                b0, blocks = 2 * (n % 2), 4 * (qt + 1)
                tb = (duo, aux)[n % 2]
                pe.wait_ge(sem("w_probs"), at("w_probs", (l, n, 3)))
                claim(4 + 2 * (n % 2), 5 + 2 * (n % 2))
                for i in range(blocks):
                    m = pe.transpose(pair(tb[:, :, :], 1024)[:, i * P:(i + 1) * P], wS[n % 2][:, i * P:(i + 1) * P],
                                     cst("ident"))
                m.then_inc(bank_full(4 + 2 * (n % 2)), fill(4 + 2 * (n % 2), (l, "wt", n)))
                pe.wait_ge(sem("w_probsT"), at("w_probsT", (l, n)))
                for i in range(blocks):
                    r, kt = HEAD_AT[i // (qt + 1)], i % (qt + 1)
                    m = pe.matmul(acc[:, b0 + 1, r * 64:(r + 1) * 64], wP[n % 2][:, i * P:(i + 1) * P],
                                  wv[:, kt, j * 64:(j + 1) * 64], start=(kt == 0), stop=(kt == qt))
                m.then_inc(bank_full(b0 + 1), fill(b0 + 1, (l, "wo", n)))

            scores(0)
            for n in range(len(UNITS_W)):
                if n + 1 < len(UNITS_W):
                    scores(n + 1)
                values(n)
            pe.wait_ge(sem("wo_ready"), at("wo_ready", (l, len(UNITS_W) - 1)))
            pe_to_fm(wo, KC, (l, "wo"))
            pe_fm_wait((l, "wo"), KC)
            pe_rows_acc(cF, KC, (l, "yc"))
            pe.wait_ge(sem("merged"), at("merged", (l, "gc", 1)))
            pe_to_fm(merged, KC, (l, "merged"))
            pe_fm_wait((l, "merged"), KC)
            pe_rows_acc(cF, KC, ("mix", l))

        def act_swa(l):
            act.wait_ge(sem("merged"), at("merged", (l, "gb", 1)))
            for i in range(2):
                for b in range(2):
                    act.wait_ge(bank_full(4 + b), filled_at(4 + b, (l, "sq", i)))
                    act.activation(wq[:, 4 * i + 2 * b:4 * i + 2 * b + 2, :], split(bank(4 + b), 2), ACT.Copy)\
                        .then_inc(sem("w_ready"), mark_read("w_ready", 4 + b, (l, "sq", i)))
            for b in range(2):
                act.wait_ge(bank_full(4 + b), filled_at(4 + b, (l, "sk")))
                act.activation(wk[:, 2 * b:2 * b + 2, :], split(bank(4 + b), 2), ACT.Copy)\
                    .then_inc(sem("w_ready"), mark_read("w_ready", 4 + b, (l, "sk")))
            act.wait_ge(bank_full(6), filled_at(6, (l, "sv")))
            act.activation(wv[:, :, :], split(bank(6), 2), ACT.Copy)\
                .then_inc(sem("w_ready"), mark_read("w_ready", 6, (l, "sv")))
            act_gate(l, "gc", gC)
            for n, (j, qt) in enumerate(UNITS_W):
                nk, x = (qt + 1) * P, 4 * (n % 2)
                act.wait_ge(sem("w_negmax"), at("w_negmax", (l, n)))
                for r in range(4):
                    m = act.activation(wS[n % 2][:, r * nk:(r + 1) * nk], wS[n % 2][:, r * nk:(r + 1) * nk], ACT.Exp,
                                       bias=smax[:, 8 + x + r:9 + x + r], accum_out=ssum[:, x + r:x + r + 1])
                    m.then_inc(sem("w_probs"), mark("w_probs", (l, n, r)))
                act.wait_ge(sem("w_sink"), at("w_sink", (l, n)))
                act.activation(sinke[:, x:x + 4], sinke[:, x:x + 4], ACT.Exp)\
                    .then_inc(sem("w_sinke"), mark("w_sinke", (l, n)))
                b = 4 + 2 * (n % 2)
                act.wait_ge(bank_full(b), filled_at(b, (l, "wt", n)))
                act.activation(wP[n % 2][:, 0:4 * nk], pair((duo, aux)[n % 2][:, :, :], 4 * nk), ACT.Copy)\
                    .then_inc(sem("w_probsT"), mark("w_probsT", (l, n)))
                was_read(b, (l, "wt", n), "w_probsT")
            act_to_fm(cF, KC, (l, "wo"))
            act_to_fm(cF, KC, (l, "merged"))

        def dve_swa(l):
            def softmax(n):
                j, qt = UNITS_W[n]
                nk, b0, x = (qt + 1) * P, 2 * (n % 2), 4 * (n % 2)
                dve.wait_ge(bank_full(b0), filled_at(b0, (l, "ws", n)))
                if n >= 2:
                    dve.wait_ge(bank_full(4 + 2 * (n % 2)), filled_at(4 + 2 * (n % 2), (l, "wt", n - 2)))
                s4 = split(wS[n % 2][:, 0:4 * nk], 4)
                m = dve.scalar_tensor_tensor(out=s4, in0=split(pair(acc[:, b0:b0 + 2, :], 1024), 4)[:, :, 0:nk],
                                             scalar=0.125,
                                             in1=bc(cst(f"window{qt}"), 1, [P, 4, nk]), op0=ALU.mult, op1=ALU.add)
                m.then_inc(sem("w_biased"), mark_read("w_biased", b0, (l, "ws", n)))
                dve.wait_ge(sem("w_biased"), latest("w_biased"))
                V(dve.tensor_reduce(smax[:, x:x + 4], s4, AX.X, ALU.max))
                sk = sinks[:, 16 * l + 4 * j:16 * l + 4 * j + 4].rearrange("p (a b) -> p b a", a=2)
                V(dve.tensor_tensor(split(smax[:, x:x + 4], 2), split(smax[:, x:x + 4], 2), sk, ALU.max))
                dve.tensor_scalar(smax[:, 8 + x:12 + x], smax[:, x:x + 4], -1.0, None, ALU.mult)\
                    .then_inc(sem("w_negmax"), mark("w_negmax", (l, n)))
                dve.tensor_tensor(split(sinke[:, x:x + 4], 2), sk, split(smax[:, x:x + 4], 2), ALU.subtract)\
                    .then_inc(sem("w_sink"), mark("w_sink", (l, n)))

            def divide(n):
                j, qt = UNITS_W[n]
                x = 4 * (n % 2)
                dve.wait_ge(sem("w_sinke"), at("w_sinke", (l, n)))
                V(dve.tensor_tensor(ssum[:, x:x + 4], ssum[:, x:x + 4], sinke[:, x:x + 4], ALU.add))
                V(dve.reciprocal(ssum[:, x:x + 4], ssum[:, x:x + 4]))
                dve.wait_ge(bank_full(2 * (n % 2) + 1), filled_at(2 * (n % 2) + 1, (l, "wo", n)))
                def heads(v):
                    return v.rearrange("p (a b d) -> p a b d", a=2, b=2)
                m = dve.tensor_tensor(heads(wo[:, qt, j * 256:(j + 1) * 256]),
                                      heads(acc[:, 2 * (n % 2) + 1, 0:256]),
                                      bc(ssum[:, x:x + 4].rearrange("p (b a) -> p a b", a=2), 3, [P, 2, 2, 64]),
                                      ALU.mult)
                m.then_inc(sem("wo_ready"), mark("wo_ready", (l, n)))
                was_read(2 * (n % 2) + 1, (l, "wo", n), "wo_ready")

            softmax(0)
            for n in range(len(UNITS_W)):
                if n + 1 < len(UNITS_W):
                    softmax(n + 1)
                divide(n)
            dve_merge(l, "gc", gC, (l, "yc"))

        tmp1 = cols(1)
        chosen = cols(16)
        most = cols(1).bitcast(mybir.dt.int32)
        rtr = sb("rtr", [P, KC, NE])

        def pe_router():
            claim(4)
            for t in range(NT):
                for k in range(KC):
                    m = pe.matmul(bank(4)[:, t * NE:(t + 1) * NE], u[:, k, t * P:(t + 1) * P], rtr[:, k, :],
                                  start=(k == 0), stop=(k == KC - 1))
            m.then_inc(bank_full(4), fill(4, "router"))
            pe.wait_ge(sem("chosen"), at("chosen", 0))
            claim(5)
            c0, c1 = chosen[:, 0:NE], chosen[:, NE:2 * NE]
            pe.matmul(bank(5)[:, 0:NE], cst("upper"), c0, start=True, stop=True)
            pe.matmul(bank(5)[:, NE:2 * NE], cst("ones"), c0, start=True, stop=False)
            pe.matmul(bank(5)[:, NE:2 * NE], cst("upper"), c1, start=False, stop=True)
            pe.matmul(bank(5)[:, 2 * NE:3 * NE], cst("ones"), c0, start=True, stop=False)
            pe.matmul(bank(5)[:, 2 * NE:3 * NE], cst("ones"), c1, start=False, stop=True)\
              .then_inc(bank_full(5), fill(5, "places"))

        def act_router():
            act.wait_ge(sem("top_diff"), at("top_diff", 0))
            act.activation(prob[:, 0:2], prob[:, 0:2], ACT.Exp).then_inc(sem("top_exp"), mark("top_exp", 0))

        def dve_router():
            dve.wait_ge(bank_full(4), filled_at(4, "router"))
            dve.tensor_copy(logits, bank(4)[:, 0:16]).then_inc(sem("logits"), mark_read("logits", 4, "router"))
            dve.wait_ge(sem("logits"), latest("logits"))
            for t in range(NT):
                e = slice(8 * t, 8 * t + 8)
                V(dve.max(top[:, e], logits[:, e]))
                V(dve.max_index(topi[:, e], top[:, e], logits[:, e]))
            V(dve.tensor_copy(topf, topi))
            t2 = split(top, 2)
            dve.tensor_tensor(prob[:, 0:2], t2[:, :, 1], t2[:, :, 0], ALU.subtract)\
                .then_inc(sem("top_diff"), mark("top_diff", 0))
            dve.wait_ge(sem("top_exp"), at("top_exp", 0))
            V(dve.tensor_scalar(prob[:, 2:4], prob[:, 0:2], 1.0, None, ALU.add))
            V(dve.reciprocal(prob[:, 2:4], prob[:, 2:4]))
            V(dve.tensor_tensor(prob[:, 4:6], prob[:, 0:2], prob[:, 2:4], ALU.mult))
            for t in range(NT):
                e = slice(8 * t, 8 * t + 8)
                V(dve.tensor_scalar(top[:, e], cst("iota8"), topf[:, 8 * t:8 * t + 1], None, ALU.is_equal))
                V(dve.tensor_scalar(logits[:, e], cst("iota8"), topf[:, 8 * t + 1:8 * t + 2], None, ALU.is_equal))
            dve.tensor_tensor(chosen, top, logits, ALU.add).then_inc(sem("chosen"), mark("chosen", 0))
            for t in range(NT):
                e = slice(8 * t, 8 * t + 8)
                V(dve.tensor_scalar(gates[:, e], top[:, e], prob[:, 2 + t:3 + t], None, ALU.mult))
                V(dve.scalar_tensor_tensor(out=gates[:, e], in0=logits[:, e], scalar=prob[:, 4 + t:5 + t],
                                           in1=gates[:, e], op0=ALU.mult, op1=ALU.add))
            dve.wait_ge(bank_full(5), filled_at(5, "places"))
            V(dve.memset(slot_of[:, :, :], -1.0))
            V(dve.memset(gate_of[:, :, :], 0.0))
            V(dve.tensor_tensor(topf, bank(5)[:, 0:2 * NE], chosen, ALU.mult))
            V(dve.tensor_scalar(slot_of[:, :, 0:NE], split(topf, 2), -1.0, None, ALU.add))
            V(dve.tensor_copy(gate_of[:, :, 0:NE], split(gates, 2)))
            dve.tensor_reduce(tmp1, bank(5)[:, 2 * NE:3 * NE], AX.X, ALU.max)\
               .then_inc(sem("most"), mark_read("most", 5, "places"))
            dve.wait_ge(sem("most"), latest("most"))
            dve.tensor_copy(most, tmp1).then_inc(sem("most_tokens"), mark("most_tokens", 0))
            V(dve.scalar_tensor_tensor(out=split(gates, 2), in0=slot_of[:, :, 0:NE], scalar=float(SLOTS),
                                       in1=gate_of[:, :, 0:NE], op0=ALU.is_ge, op1=ALU.mult))
            if SLOTS < P:
                V(dve.tensor_tensor(gate_of[:, :, 0:8], gate_of[:, :, 0:8], split(gates, 2), ALU.subtract))

        stack = view(6144, STACKS, P)
        last_rows = STACK_ROWS - (STACKS - 1) * P

        def act_start():
            loads = [(con[:, :], consts), (h[:, :, :], a["x"][0].rearrange("(t p) d -> p t d", p=P)),
                     (dtb, a["ssm_dt_bias"][0].partition_broadcast(P)),
                     (alog, a["ssm_a_log"][0].partition_broadcast(P)),
                     (dskip, a["ssm_d"][0].partition_broadcast(P)),
                     (sinks, a["swa_sinks_2"].rearrange("l h -> (l h)").partition_broadcast(P)),
                     (rtr[:, :, :], a["moe_router_2"][0].rearrange("(t p) e -> p t e", p=P))]
            for name, n in STACK:
                v = a[name]
                v = v.rearrange({2: "a (c p) -> (a c) p", 3: "a b (c p) -> (a b c) p"}[len(v.shape)], p=P)
                row = 0
                while row < n:
                    pos = stack_at(name) + row
                    k = min(n - row, P - pos % P)
                    loads.append((stack[pos % P:pos % P + k, pos // P, :], v[row:row + k, :]))
                    row += k
            for dst, src in loads:
                act.dma_start(dst, src).then_inc(sem("start_loads"), 16)
            ev.seen[("start_loads", 0)] = 16 * len(loads)
            act.wait_ge(sem("start_loads"), 16 * len(loads))
            act.wait_ge(bank_full(6), filled_at(6, "stack"))
            act.activation(par[:, 0:STACK_ROWS], bank(6)[:, 0:STACK_ROWS], ACT.Copy)\
                .then_inc(sem("par"), mark("par", 0))
            was_read(6, "stack", "par")
            act.wait_ge(sem("par"), latest("par"))
            act.wait_ge(sem("lb_diff"), at("lb_diff", 0))
            A(act.activation(lb1[:, 0:8], lbd, ACT.Abs))
            A(act.activation(lb1[:, 0:8], lb1[:, 0:8], ACT.Exp, scale=-1.0))
            act.activation(lb1[:, 0:8], lb1[:, 0:8], ACT.Ln, bias=1.0).then_inc(sem("lb_soft"), mark("lb_soft", 0))

        def pe_start():
            pe.wait_ge(sem("start_loads"), at("start_loads", 0))
            for s in range(STACKS):
                k = P if s < STACKS - 1 else last_rows
                m = pe.transpose(bank(6)[:, s * P:s * P + k], stack[0:k, s, :], cst("ident")[0:k, 0:k])
            m.then_inc(bank_full(6), fill(6, "stack"))

        def dve_start():
            dve.wait_ge(sem("par"), at("par", 0))
            lb = stack_at("hgrn_lower_bounds_2")
            dve.tensor_tensor(lbd, par[:, lb + 8:lb + 16], par[:, lb:lb + 8], ALU.subtract)\
                .then_inc(sem("lb_diff"), mark("lb_diff", 0))
            dve.wait_ge(sem("lb_diff"), latest("lb_diff"))
            V(dve.tensor_scalar(lb2[:, 0:8], lbd, 0.0, None, ALU.min))
            V(dve.tensor_scalar(lb3[:, 0:8], lbd, -1.0, 0.0, ALU.mult, ALU.min))
            dve.wait_ge(sem("lb_soft"), at("lb_soft", 0))
            V(dve.tensor_tensor(lbA[:, 0:8], lb2[:, 0:8], lb1[:, 0:8], ALU.subtract))
            V(dve.tensor_tensor(lbC[:, 0:8], lb3[:, 0:8], lb1[:, 0:8], ALU.subtract))
            dve.wait_ge(sem("start_loads"), at("start_loads", 0))
            dve.tensor_copy(tmp1, lbA[:, 0:1]).then_inc(sem("h_ready"), mark("h_ready", ("ffn00", "pre")))

        FIRST = [("ffn00", 0, 0, 0.5), ("mixA", 0, 2, 1.0), ("ffn01", 0, 4, 0.5),
                 ("ffn10", 1, 0, 0.5), ("mixB", 1, 2, 1.0), ("ffn11", 1, 4, 0.5)]

        block = ctx.enter_context(nc.Block())

        def pe_h_to_fm(key):
            pe.wait_ge(sem("h_ready"), at("h_ready", key))
            pe_to_fm(h, KC, key)
            pe_fm_wait(key, KC)

        @block.tensor
        def _(_e):
            pe_start()
            for key, layer, g, _ in FIRST:
                pe_prenorm((key, "pre"))
                if key == "mixA":
                    pe_mixer_a()
                elif key == "mixB":
                    pe_mixer_b()
                else:
                    pe_ffn(key, FFB, 4)
            for l in range(2):
                pe_h_to_fm(("h", l))
                pe_retention(l)
                pe_hgrn(l)
                pe_swa(l)
                pe_h_to_fm(("f", l))
                if l == 0:
                    pe_ffn(("ff", 0), FFB, 4)
                else:
                    pe_router()
                    pe_moe()
                    with pe.If(overflows(pe)):
                        pe_ffn("over", NE * MOEB, NE)

        @block.scalar
        def _(_e):
            act_start()
            for key, layer, g, _ in FIRST:
                act_prenorm((key, "pre"), 6 * layer + g)
                if key == "mixA":
                    act_mixer_a()
                elif key == "mixB":
                    act_mixer_b()
                else:
                    act_ffn(key, FFB, 4)
                act_postnorm(key)
            act_root("ln_in", 2)
            for l in range(2):
                act_to_fm(u, KC, ("h", l))
                act_retention(l)
                act_hgrn(l)
                act_swa(l)
                act_root(("mix", l), 2)
                act_to_fm(u, KC, ("f", l))
                if l == 0:
                    act_ffn(("ff", 0), FFB, 4)
                else:
                    act_router()
                    act_moe()
                    with act.If(overflows(act)):
                        act_ffn("over", NE * MOEB, NE)
                act_root(("ff", l), 2)

        @block.vector
        def _(_e):
            dve_start()
            for n, (key, layer, g, factor) in enumerate(FIRST):
                dve_prenorm((key, "pre"))
                if key == "mixA":
                    dve_mixer_a()
                elif key == "mixB":
                    dve_mixer_b()
                else:
                    dve_ffn(key, FFB, 4, False)
                dve_postnorm(key, factor, (FIRST[n + 1][0], "pre") if n + 1 < len(FIRST) else "ln_in")
            dve_layernorm("ln_in", False, ("h", 0))
            for l in range(2):
                dve_retention(l)
                dve_hgrn(l)
                dve_swa(l)
                dve_layernorm(("mix", l), True, ("f", l))
                if l == 0:
                    dve_ffn(("ff", 0), FFB, 4, False)
                    dve_layernorm(("ff", 0), True, ("h", 1))
                else:
                    dve_router()
                    dve_moe()
                    dve_layernorm(("ff", 1), "experts", ("h", 2))

        @block.gpsimd
        def _(_e):
            prev = None
            for n, (key, layer, g, _) in enumerate(FIRST):
                pool_rows(key, prev, a["norm_g"][layer, g + 1])
                prev = (FIRST[n + 1][0], "pre") if n + 1 < len(FIRST) else "ln_in"
            pool_rows("ln_in", prev, a["ln_in_g_2"], a["ln_in_b_2"])
            prev = ("h", 0)
            for l in range(2):
                pool_rows(("mix", l), prev, a["ln_mix_g_2"][l], a["ln_mix_b_2"][l])
                pool_rows(("ff", l), ("f", l), a["ln_ffn_g_2"][l], a["ln_ffn_b_2"][l])
                prev = ("h", l + 1)

        @block.sync
        def _(_e):
            for key, layer, g, _ in FIRST:
                if key == "mixA":
                    w = a["hyb_w_in"][0]
                    sp.wait_ge(sem("h_ready"), at("h_ready", ("mixA", "pre")))
                    sp.dma_start(wdt[:, :, :], w[:, 4608:4624].rearrange("(t p) n -> p t n", p=P))\
                      .then_inc(sem("wdt_landed"), 16)
                    load(*[col_block(w, c) for _, _, c in KEYS_A])
                    load(*[col_block(w, 3072 + 512 * i) for i in range(3)])
                    load(*[col_block(w, 2048 + 512 * i) for i in range(2)])
                    load(*[row_block(a["hyb_w_out"][0], 512 * i) for i in range(4)])
                elif key == "mixB":
                    load(*[col_block(a["attn_w_qkv"][0], 512 * i) for i in range(9)])
                    load(row_block(a["attn_w_o"][0], 0))
                else:
                    w = a["ffn_w1"][layer, g // 4]
                    sp_ffn(key, FFB, 4, *dense_sources(w[:, 0:FF], w[:, FF:2 * FF], a["ffn_w2"][layer, g // 4], 4))
            for l in range(2):
                w = a["w_in_2"][l]

                def wcols(*starts):
                    load(*[col_block(w, c) for c in starts])
                wcols(0, 512, 1024, 1536, 2048, 2560, 8704, 9216)
                load(*[row_block(a["ret_w_out_2"][l], 512 * i) for i in range(2)])
                wcols(3072, 3584, 4096, 4608, 5120, 5632, 6144, 6656, 9728, 10240)
                load(*[row_block(a["hgrn_w_out_2"][l], 512 * i) for i in range(2)])
                wcols(7168, 7680, 8192, 10752, 11264)
                load(*[row_block(a["swa_w_out_2"][l], 512 * i) for i in range(2)])
                load(*[row_block(a["w_o_2"][l], 512 * i) for i in range(2)])
                if l == 0:
                    sp_ffn(("ff", l), FFB, 4, *dense_sources(a["ffn_w_gate_2"][0], a["ffn_w_up_2"][0],
                                                             a["ffn_w_down_2"][0], 4))
                else:
                    experts = a["moe_w_gate_2"][0], a["moe_w_up_2"][0], a["moe_w_down_2"][0]
                    sp_moe(*experts)
                    with sp.If(overflows(sp)):
                        sp_ffn("over", NE * MOEB, NE, *moe_sources(*experts))
            sp.wait_ge(sem("h_ready"), at("h_ready", ("h", 2)))
            sp.dma_start(out[0].rearrange("(t p) d -> p t d", p=P), h[:, :, :]).then_inc(sem("stored"), 16)
            sp.wait_ge(sem("stored"), 16)
    return ev.seen


INS = ["x", "norm_g", "ffn_w1", "ffn_w2", "hyb_w_in", "conv_dw_w", "conv_dw_b", "conv_ln_g", "conv_ln_b",
       "ssm_conv_w", "ssm_conv_b", "ssm_dt_bias", "ssm_a_log", "ssm_d", "ssm_norm_g", "hyb_w_out", "attn_w_qkv",
       "attn_w_o", "ln_in_g_2", "ln_in_b_2", "w_in_2", "ret_w_out_2", "hgrn_lower_bounds_2", "hgrn_norm_g_2",
       "hgrn_w_out_2", "swa_sinks_2", "swa_w_out_2", "w_o_2", "ln_mix_g_2", "ln_mix_b_2", "ffn_w_gate_2",
       "ffn_w_up_2", "ffn_w_down_2", "moe_router_2", "moe_w_gate_2", "moe_w_up_2", "moe_w_down_2", "ln_ffn_g_2",
       "ln_ffn_b_2"]


def program(nc, shapes, known):
    a = {n: nc.dram_tensor(f"in_{n}_dram", s, F32, kind="ExternalInput").ap() for n, s in shapes.items()}
    _, ccols = const_layout()
    consts = nc.dram_tensor("in_consts_dram", (P, ccols), F32, kind="ExternalInput").ap()
    out = nc.dram_tensor("out_0_dram", (1, T, D), F32, kind="ExternalOutput").ap()
    return build(nc, a, out, consts, known)


def kernel(**inputs):
    import concourse.bacc as bacc
    from concourse.bass_utils import run_bass_kernel_spmd

    arrays = {f"in_{n}_dram": np.ascontiguousarray(inputs[n]) for n in INS}
    shapes = {n: inputs[n].shape for n in INS}
    arrays["in_consts_dram"] = np.concatenate(list(shape_constants().values()), 1)
    counts = program(bacc.Bacc("TRN2", target_bir_lowering=False, num_devices=1), shapes, {})
    nc = bacc.Bacc("TRN2", target_bir_lowering=False, num_devices=1)
    program(nc, shapes, counts)
    r = run_bass_kernel_spmd(nc, [arrays], core_ids=[0])
    return r.results[0]["out_0_dram"]
```

```python
from contextlib import ExitStack

import numpy as np

import concourse.bass as bass
from concourse import mybir

F32 = mybir.dt.float32
F32R = mybir.dt.float32r
U32 = mybir.dt.uint32
ACT = mybir.ActivationFunctionType
ALU = mybir.AluOpType
AX = mybir.AxisListType

P = 128
T = 256
NT = T // P
D = 1024
KC = D // P
COLS = 512
FF = 2816
FFB = FF // 256
NE = 8
DE = 3584
MOEB = DE // 256
SLOTS = P
RING = 4
RING2 = 2
TAPS = 31
SCONV = 4
HEADS_SSM = 16
ALPHA = 4.0 ** 0.25
NEG = -1.0e30



def shape_constants():
    f = np.float32
    p = np.arange(P)
    c = {}
    c["ident"] = np.eye(P, dtype=f)
    c["ones"] = np.ones((P, P), f)
    c["upper"] = (p[:, None] <= p[None, :]).astype(f)
    inv = (1.0 / (np.float32(10000.0) ** np.linspace(0.0, 1.0, 64, dtype=f))).astype(f)
    ang = (np.arange(T, dtype=f)[None, :] * inv[:, None]).astype(f)
    c["cos"] = np.tile(np.cos(ang), (2, 1)).astype(f)
    c["sin"] = np.concatenate([np.sin(ang), -np.sin(ang)], 0).astype(f)
    diff = np.arange(T)[None, :] - p[:, None]
    for h in range(4):
        lg = np.log(f(1.0) - f(2.0) ** f(-5.0 - h)).astype(f)
        dec = np.where(diff >= 0, np.exp(np.maximum(diff, 0).astype(f) * lg), 0.0)
        c[f"decay{h}"] = (dec * 128.0 ** -0.5).astype(f)
    for qt in range(2):
        q = qt * P + p[:, None]
        k = np.arange((qt + 1) * P)[None, :]
        rel = q - k
        for g, dil in enumerate((1, 4, 16)):
            ok = (rel >= 0) & (rel % dil == 0) & (rel // dil <= P)
            c[f"dist{qt}{g}"] = np.where(ok, rel, 1e30).astype(f)
        cd = q // 64 - k // 64
        c[f"window{qt}"] = np.where((cd >= 0) & (cd <= 2), 0.0, NEG).astype(f)
    c["block"] = (p[:, None] // 16 == np.arange(8)[None, :]).astype(f)
    c["blockcausal"] = ((p[:, None] // 16 == p[None, :] // 16) & (p[:, None] <= p[None, :])).astype(f)
    c["iota128"] = np.tile(np.arange(P, dtype=f), (P, 1))
    c["iota8"] = np.tile(np.arange(8, dtype=f), (P, 1))
    return c


def const_layout():
    at, off = {}, 0
    for name, v in shape_constants().items():
        at[name] = (off, v.shape[1])
        off += v.shape[1]
    return at, off


STACK = [("norm_g", 96), ("conv_dw_w", TAPS * 8), ("conv_dw_b", 8), ("conv_ln_g", 8), ("conv_ln_b", 8),
         ("ssm_conv_w", SCONV * 12), ("ssm_conv_b", 12), ("ssm_norm_g", 8), ("hgrn_lower_bounds_2", 16),
         ("hgrn_norm_g_2", 2)]
STACK_ROWS = sum(n for _, n in STACK)
STACKS = -(-STACK_ROWS // P)


def stack_at(name):
    off = 0
    for n, r in STACK:
        if n == name:
            return off
        off += r
    raise KeyError(name)


class Events:

    def __init__(self, nc, ctx, known):
        self.nc, self.ctx, self.known = nc, ctx, known
        self.seen, self.count, self.sems = {}, {}, {}

    def sem(self, name):
        if name not in self.sems:
            self.sems[name] = self.ctx.enter_context(self.nc.semaphore(name))
            self.count.setdefault(name, 0)
        return self.sems[name]

    def value(self, name, key):
        assert not self.known or (name, key) in self.known, (name, key)
        return self.known.get((name, key), 1)

    def mark(self, name, key, inc=1):
        self.sem(name)
        self.count[name] += inc
        assert (name, key) not in self.seen, (name, key)
        self.seen[(name, key)] = self.count[name]
        return inc

    def start(self, name, stage):
        self.sem(name)
        self.seen[(name, ("start", stage))] = self.count[name]

    def base(self, name, stage):
        assert not self.known or (name, ("start", stage)) in self.known, (name, stage)
        return self.known.get((name, ("start", stage)), 1)


def build(nc, a, out, consts, known):
    ctx = ExitStack()
    with ctx:
        ev = Events(nc, ctx, known)
        cat, ccols = const_layout()

        def sb(name, shape, dt=F32):
            return ctx.enter_context(nc.sbuf_tensor(name, shape, dt))

        w1 = sb("w1", [P, RING, 4096])
        w2 = sb("w2", [P, RING2, 2, D])
        con = sb("con", [P, ccols])
        h = sb("h", [P, NT, D])
        u = sb("u", [P, KC, T])
        rows = sb("rows", [P, 2, D])
        par = sb("par", [P, STACKS * P])
        small = sb("small", [P, 512])
        ARENA = 21760
        with nc.sbuf_tensor("arena", [P, ARENA], F32) as arena:
            pass
        sb("under_normed", [P, 2048])
        ul = sb("u_low", [P, KC, T], F32R)
        sb("under_hidden", [P, 1024])
        hT = sb("hidden_T_split", [P, 2, 2, T], F32R)
        uh = sb("u_high", [P, KC, T], F32R)
        units = sb("weights_split", [P, 3, 2, 2048], F32R)
        sb("arena_rest", [P, ARENA - 20480])
        acc = ctx.enter_context(nc.psum_tensor("acc", [P, 4, 512], F32))
        duo = ctx.enter_context(nc.psum_tensor("duo", [P, 2, 512], F32))
        aux = ctx.enter_context(nc.psum_tensor("aux", [P, 2, 512], F32))

        def cst(name):
            o, n = cat[name]
            return con[:, o:o + n]

        def view(off, *shape):
            n = int(np.prod(shape))
            assert off + n <= ARENA, (off, shape)
            v = arena[:, off:off + n]
            if len(shape) == 2:
                v = v.rearrange("p (a b) -> p a b", b=shape[1])
            if len(shape) == 3:
                v = v.rearrange("p (a b c) -> p a b c", b=shape[1], c=shape[2])
            return v

        def bc(x, axis, shape):
            return x.unsqueeze(axis).broadcast_to(shape)

        def split(x, n):
            return x.rearrange("p (a b) -> p a b", a=n)

        def pcol(name, row):
            o = stack_at(name) + row
            return par[:, o:o + 1]

        used = [0]

        def cols(n):
            used[0] += n
            assert used[0] <= 512
            return small[:, used[0] - n:used[0]]

        ssq, msq, rot, rsd = cols(8), cols(8), cols(8), cols(8)
        stats, mv = cols(24), cols(4)
        dtb, alog, dskip = cols(16), cols(16), cols(16)
        sinks = cols(32)
        gates, logits, top = cols(16), cols(16), cols(16)
        topi = cols(16).bitcast(U32)
        topf, prob = cols(16), cols(8)
        lbd, lb1, lb2, lb3, lbA, lbC = cols(8), cols(16), cols(16), cols(16), cols(16), cols(16)
        smax, ssum, sinke = cols(16), cols(16), cols(16)
        decay_tot = cols(16)

        pe, act, dve, pool, sp = nc.tensor, nc.scalar, nc.vector, nc.gpsimd, nc.sync

        sem = ev.sem
        at = ev.value
        mark = ev.mark

        def latest(name):
            return ev.count[name]

        orders = {"act_order": 0, "dve_order": 0}

        def A(ins):
            ins.then_inc(sem("act_order"), 1)
            orders["act_order"] += 1
            act.wait_ge(sem("act_order"), orders["act_order"])

        def V(ins):
            ins.then_inc(sem("dve_order"), 1)
            orders["dve_order"] += 1
            dve.wait_ge(sem("dve_order"), orders["dve_order"])

        last_fill = {}

        def bank(b):
            return acc[:, b, :] if b < 4 else (duo, aux)[(b - 4) // 2][:, b % 2, :]

        def bank_full(b):
            return sem(f"bank_full{b}")

        def filled_at(b, key):
            return at(f"bank_full{b}", key)

        def fill(b, key):
            last_fill[b] = key
            return mark(f"bank_full{b}", key)

        def claim(*banks):
            for b in banks:
                if b in last_fill and known:
                    name, count = known[("read", b, last_fill[b])]
                    pe.wait_ge(sem(name), count)

        def was_read(b, key, name):
            ev.seen[("read", b, key)] = (name, ev.count[name])

        def mark_read(name, b, key):
            inc = mark(name, ("read", b, key))
            was_read(b, key, name)
            return inc

        ring_pe, ring_sp = {"w1": 0, "w2": 0}, {"w1": 0, "w2": 0}

        def arrived():
            n = ring_pe["w1"]
            ring_pe["w1"] += 1
            pe.wait_ge(sem(f"w1_landed{n % RING}"), 32 * (n // RING + 1))
            return w1[:, n % RING, :]

        def released(ring, n, name, count=None):
            ev.seen[("release", ring, n)] = (name, ev.count[name] if count is None else count)

        def released_last(name):
            released("w1", ring_pe["w1"] - 1, name)

        def slot_free(ring):
            n = ring_sp[ring] - (RING if ring == "w1" else RING2)
            if n >= 0 and known:
                name, count = known[("release", ring, n)]
                sp.wait_ge(sem(name), count)

        def load(*blocks):
            for parts in blocks:
                slot_free("w1")
                n = ring_sp["w1"]
                ring_sp["w1"] += 1
                for dst, src in parts(w1[:, n % RING, :]):
                    sp.dma_start(dst, src).then_inc(sem(f"w1_landed{n % RING}"), 16)

        def col_block(w, c0):
            def parts(slot):
                s = slot.rearrange("p (t n) -> p t n", n=COLS)
                src = w.rearrange("(t p) n -> p t n", p=P)
                return [(s[:, 4 * i:4 * i + 4, :], src[:, 4 * i:4 * i + 4, c0:c0 + COLS]) for i in range(2)]
            return parts

        def row_block(w, r0):
            def parts(slot):
                s = slot.rearrange("p (t n) -> p t n", n=D)
                src = w[r0:r0 + 4 * P, :].rearrange("(t p) n -> p t n", p=P)
                return [(s[:, 2 * i:2 * i + 2, :], src[:, 2 * i:2 * i + 2, :]) for i in range(2)]
            return parts

        def pe_cols_tm(src, key):
            slot = arrived().rearrange("p (t n) -> p t n", n=COLS)
            for t in range(NT):
                claim(4 + t)
                for k in range(KC):
                    m = pe.matmul(bank(4 + t), src[:, k, t * P:(t + 1) * P], slot[:, k, :],
                                  start=(k == 0), stop=(k == KC - 1))
                m.then_inc(bank_full(4 + t), fill(4 + t, key))
            released_last("bank_full5")

        def pe_cols_fm(src, key):
            slot = arrived().rearrange("p (t n) -> p t n", n=COLS)
            for b in range(2):
                claim(4 + b)
                for c in range(2):
                    for k in range(KC):
                        m = pe.matmul(bank(4 + b)[:, c * T:(c + 1) * T],
                                      slot[:, k, (2 * b + c) * P:(2 * b + c + 1) * P], src[:, k, :],
                                      start=(k == 0), stop=(k == KC - 1))
                m.then_inc(bank_full(4 + b), fill(4 + b, key))
            released_last("bank_full5")

        def pe_rows_acc(src, chunks, key):
            claim(0, 1, 2, 3)
            for blk in range(chunks // 4):
                slot = arrived().rearrange("p (t n) -> p t n", n=D)
                for t in range(NT):
                    for half in range(2):
                        for k in range(4):
                            kk = 4 * blk + k
                            m = pe.matmul(acc[:, 2 * t + half, :], src[:, kk, t * P:(t + 1) * P],
                                          slot[:, k, half * 512:(half + 1) * 512],
                                          start=(kk == 0), stop=(kk == chunks - 1))
                        if kk == chunks - 1:
                            m.then_inc(bank_full(2 * t + half), fill(2 * t + half, key))
                if blk == chunks // 4 - 1:
                    released_last("bank_full3")
                else:
                    m.then_inc(sem("rows_multiplied"), mark("rows_multiplied", (key, blk)))
                    released_last("rows_multiplied")

        def pe_to_fm(src, chunks, key):
            for c in range(chunks):
                b = 6 + (c // 2) % 2
                if c % 2 == 0:
                    claim(b)
                for t in range(NT):
                    m = pe.transpose(bank(b)[:, (c % 2) * T + t * P:(c % 2) * T + (t + 1) * P],
                                     src[:, t, c * P:(c + 1) * P], cst("ident"))
                if c % 2:
                    m.then_inc(bank_full(b), fill(b, (key, c // 2)))

        def act_to_fm(dst, chunks, key, gain=None):
            for c in range(0, chunks, 2):
                b = 6 + (c // 2) % 2
                act.wait_ge(bank_full(b), filled_at(b, (key, c // 2)))
                if gain is None:
                    m = act.activation(dst[:, c:c + 2, :], split(bank(b), 2), ACT.Copy)
                else:
                    act.activation(dst[:, c, :], bank(b)[:, 0:T], ACT.Copy, scale=gain(c))
                    m = act.activation(dst[:, c + 1, :], bank(b)[:, T:2 * T], ACT.Copy, scale=gain(c + 1))
                m.then_inc(sem("fm_ready"), mark("fm_ready", (key, c // 2)))
                was_read(b, (key, c // 2), "fm_ready")

        def pe_fm_wait(key, chunks):
            pe.wait_ge(sem("fm_ready"), at("fm_ready", (key, chunks // 2 - 1)))

        def dve_mean(key, n, scale, eps):
            dve.wait_ge(sem("sumsq"), at("sumsq", key))
            dve.tensor_scalar(msq[:, 0:n], ssq[:, 0:n], scale, eps, ALU.mult, ALU.add)\
                .then_inc(sem("meansq"), mark("meansq", key))

        def act_roots(key, n):
            act.wait_ge(sem("meansq"), at("meansq", key))
            act.activation(rot[:, 0:n], msq[:, 0:n], ACT.Sqrt).then_inc(sem("root"), mark("root", key))

        def dve_recips(key, n):
            dve.wait_ge(sem("root"), at("root", key))
            V(dve.reciprocal(rsd[:, 0:n], rot[:, 0:n]))

        hn = view(0, NT, D)
        junk = view(2048, NT, D)

        def pe_prenorm(key):
            pe.wait_ge(sem("normed"), at("normed", (key, 1)))
            pe_to_fm(hn, KC, key)
            pe_fm_wait(key, KC)

        def h_part(key, t):
            return key if t or key[0] == "ffn00" else (key, "first")

        def act_prenorm_sums(key):
            for t in range(NT):
                act.wait_ge(sem("h_ready"), at("h_ready", h_part(key, t)))
                act.activation(junk[:, t, :], h[:, t, :], ACT.Square, accum_out=ssq[:, t:t + 1])\
                   .then_inc(sem("sumsq"), mark("sumsq", (key, t)))
                act_root(key, t)

        def act_prenorm(key, row):
            act_prenorm_sums(key)
            act_to_fm(u, KC, key, gain=lambda c: pcol("norm_g", row * 8 + c))

        def act_root(key, t):
            act.wait_ge(sem("meansq"), at("meansq", (key, t)))
            act.activation(rot[:, t:t + 1], msq[:, t:t + 1], ACT.Sqrt).then_inc(sem("root"), mark("root", (key, t)))

        def dve_recip(key, t):
            dve.wait_ge(sem("root"), at("root", (key, t)))
            V(dve.reciprocal(rsd[:, t:t + 1], rot[:, t:t + 1]))

        def dve_prenorm(key):
            for t in range(NT):
                dve.wait_ge(sem("sumsq"), at("sumsq", (key, t)))
                dve.tensor_scalar(msq[:, t:t + 1], ssq[:, t:t + 1], 1.0 / D, 1e-6, ALU.mult, ALU.add)\
                    .then_inc(sem("meansq"), mark("meansq", (key, t)))
                dve_recip(key, t)
                dve.tensor_scalar(hn[:, t, :], h[:, t, :], rsd[:, t:t + 1], None, ALU.mult)\
                    .then_inc(sem("normed"), mark("normed", (key, t)))

        def act_postnorm(key):
            for t in range(NT):
                for half in range(2):
                    b = 3 if key.startswith("mix") else 2 * t + half
                    act.wait_ge(bank_full(b), filled_at(b, key))
                    m = act.activation(hn[:, t, half * 512:(half + 1) * 512], acc[:, 2 * t + half, :],
                                       ACT.Square, accum_out=ssq[:, 2 * t + half:2 * t + half + 1])
                m.then_inc(sem("sumsq"), mark("sumsq", (key, t)))
                act_root(key, t)

        def dve_postnorm(key, factor, next_key):
            dve.wait_ge(sem("rows_landed"), at("rows_landed", key))

            def mean(t):
                dve.wait_ge(sem("sumsq"), at("sumsq", (key, t)))
                V(dve.tensor_tensor(msq[:, t:t + 1], ssq[:, 2 * t:2 * t + 1], ssq[:, 2 * t + 1:2 * t + 2], ALU.add))
                dve.tensor_scalar(msq[:, t:t + 1], msq[:, t:t + 1], 1.0 / D, 1e-6, ALU.mult, ALU.add)\
                    .then_inc(sem("meansq"), mark("meansq", (key, t)))

            mean(0)
            for t in range(NT):
                dve_recip(key, t)
                for half in range(2):
                    cut = slice(half * 512, (half + 1) * 512)
                    m = dve.scalar_tensor_tensor(out=hn[:, t, cut], in0=acc[:, 2 * t + half, :],
                                                 scalar=rsd[:, t:t + 1], in1=rows[:, 0, cut],
                                                 op0=ALU.mult, op1=ALU.mult)
                    m.then_inc(sem("acc_scaled"), mark("acc_scaled", (key, t, half)))
                    was_read(2 * t + half, key, "acc_scaled")
                scaled = latest("acc_scaled")
                if t == 0:
                    mean(1)
                dve.wait_ge(sem("acc_scaled"), scaled)
                part = h_part(next_key, t) if next_key != "ln_in" or t else ("ln_in", "first")
                dve.scalar_tensor_tensor(out=h[:, t, :], in0=hn[:, t, :], scalar=factor, in1=h[:, t, :],
                                         op0=ALU.mult, op1=ALU.add).then_inc(sem("h_ready"), mark("h_ready", part))

        def dve_layernorm(key, with_acc, next_key):
            if with_acc == "experts":
                V(dve.scalar_tensor_tensor(out=h[:, :, :], in0=h[:, :, :], scalar=ALPHA, in1=ysum[:, :, :],
                                           op0=ALU.mult, op1=ALU.add))
                with dve.If(overflows(dve)):
                    dve_ffn("over", NE * MOEB, NE, True)
                    for t in range(NT):
                        for half in range(2):
                            dve.wait_ge(bank_full(2 * t + half), filled_at(2 * t + half, "over"))
                            cut = slice(half * 512, (half + 1) * 512)
                            dve.tensor_tensor(h[:, t, cut], h[:, t, cut], acc[:, 2 * t + half, :], ALU.add)\
                               .then_inc(sem("over_added"), 1)
                    dve.wait_ge(sem("over_added"), 4)
            elif with_acc:
                for t in range(NT):
                    for half in range(2):
                        dve.wait_ge(bank_full(2 * t + half), filled_at(2 * t + half, key))
                        cut = slice(half * 512, (half + 1) * 512)
                        m = dve.scalar_tensor_tensor(out=h[:, t, cut], in0=h[:, t, cut], scalar=ALPHA,
                                                     in1=acc[:, 2 * t + half, :], op0=ALU.mult, op1=ALU.add)
                        m.then_inc(sem("acc_scaled"), mark("acc_scaled", (key, t, half)))
                        was_read(2 * t + half, key, "acc_scaled")
                dve.wait_ge(sem("acc_scaled"), latest("acc_scaled"))
            else:
                dve.wait_ge(sem("h_ready"), at("h_ready", key))
            for t in range(NT):
                for half in range(2):
                    i = 2 * t + half
                    V(dve.bn_stats(stats[:, 6 * i:6 * i + 6], h[:, t, half * 512:(half + 1) * 512]))
                V(dve.bn_aggr(mv[:, 2 * t:2 * t + 2], stats[:, 12 * t:12 * t + 12]))
            dve.tensor_scalar(msq[:, 0:2], mv.rearrange("p (t x) -> p t x", x=2)[:, :, 1],
                                        1.0, 1e-5, ALU.mult, ALU.add).then_inc(sem("meansq"), mark("meansq", key))
            dve_recips(key, 2)
            dve.wait_ge(sem("rows_landed"), at("rows_landed", key))
            for t in range(NT):
                V(dve.tensor_scalar(h[:, t, :], h[:, t, :], mv[:, 2 * t:2 * t + 1], rsd[:, t:t + 1],
                                    ALU.subtract, ALU.mult))
                V(dve.tensor_tensor(h[:, t, :], h[:, t, :], rows[:, 0, :], ALU.mult))
                m = dve.tensor_tensor(h[:, t, :], h[:, t, :], rows[:, 1, :], ALU.add)
            m.then_inc(sem("h_ready"), mark("h_ready", next_key))

        def pool_rows(key, previous, gain, bias=None):
            if previous is not None:
                pool.wait_ge(sem("h_ready"), at("h_ready", previous))
            pool.dma_start(rows[:, 0, :], gain.partition_broadcast(P))\
                .then_inc(sem("rows_landed"), mark("rows_landed", key if bias is None else (key, 0), 16))
            if bias is not None:
                pool.dma_start(rows[:, 1, :], bias.partition_broadcast(P))\
                    .then_inc(sem("rows_landed"), mark("rows_landed", key, 16))

        silu = view(4096, NT, 256)
        hid = view(4608, NT, 256)
        hidT = view(5120, 2, T)

        def loop_blocks(engine, total, body, step):
            trips = (total - 2) // body
            step(0, -1)
            step(0, 0)
            with engine.Fori(0, trips) as i:
                for j in range(1, body + 1):
                    step(i, j)
            for n in range(2 + trips * body, total):
                step(trips, n - 1 - trips * body)

        def pe_ffn(key, total, body):
            r1, r2 = ring_pe["w1"], ring_pe["w2"]
            hid0, hidT0 = ev.base("hidden_ready", key), ev.base("hidT_ready", key)
            for b in (4, 5, 6):
                ev.start(f"bank_full{b}", key)
            ev.start("w2_used", key)
            full5, used2 = ev.count["bank_full5"], ev.count["w2_used"]

            def up(i, j):
                n1 = r1 + 1 + j
                pe.wait_ge(sem(f"w1_landed{n1 % RING}"), 32 * (n1 // RING + 1) + 32 * (body // RING) * i)
                slot = w1[:, n1 % RING, :].rearrange("p (t n) -> p t n", n=COLS)
                for t in range(NT):
                    if j < 0:
                        claim(4 + t)
                    else:
                        pe.wait_ge(sem("hidden_ready"), hid0 + 2 * j + t + 1 + 2 * body * i)
                    for k in range(KC):
                        m = pe.matmul(bank(4 + t), u[:, k, t * P:(t + 1) * P], slot[:, k, :],
                                      start=(k == 0), stop=(k == KC - 1))
                    m.then_inc(bank_full(4 + t), 1)

            def turn(i, j):
                if j < 0:
                    claim(6)
                pe.wait_ge(sem("hidden_ready"), hid0 + 2 * (j + 2) + 2 * body * i)
                for c in range(2):
                    for t in range(NT):
                        m = pe.transpose(bank(6)[:, c * T + t * P:c * T + (t + 1) * P],
                                         hid[:, t, c * P:(c + 1) * P], cst("ident"))
                m.then_inc(bank_full(6), 1)

            def down(i, j, first=False, last=False):
                if first:
                    claim(0, 1, 2, 3)
                n2 = r2 + 1 + j
                pe.wait_ge(sem(f"w2_landed{n2 % RING2}"), 16 * (n2 // RING2 + 1) + 16 * (body // RING2) * i)
                pe.wait_ge(sem("hidT_ready"), hidT0 + j + 2 + body * i)
                for t in range(NT):
                    for half in range(2):
                        for c in range(2):
                            m = pe.matmul(acc[:, 2 * t + half, :], hidT[:, c, t * P:(t + 1) * P],
                                          w2[:, n2 % RING2, c, half * 512:(half + 1) * 512],
                                          start=(first and c == 0), stop=(last and c == 1),
                                          skip_group_check=True)
                        if last:
                            m.then_inc(bank_full(2 * t + half), fill(2 * t + half, key))
                if not last:
                    m.then_inc(sem("w2_used"), 1)

            def step(i, j):
                up(i, j)
                if j >= 0:
                    down(i, j - 1, first=(j == 0))
                turn(i, j)

            loop_blocks(pe, total, body, step)
            trips = (total - 2) // body
            down(trips, total - 2 - trips * body, last=True)
            ring_pe["w1"] += total
            ring_pe["w2"] += total
            for b in (4, 5, 6):
                ev.count[f"bank_full{b}"] += total
                last_fill[b] = ("ffn", key)
            ev.count["w2_used"] += total - 1
            for n in range(total):
                released("w1", r1 + n, "bank_full5", full5 + n + 1)
                released("w2", r2 + n, "w2_used", used2 + n + 1)
            released("w2", r2 + total - 1, "bank_full3")

        def act_ffn(key, total, body):
            full0 = [ev.base(f"bank_full{b}", key) for b in (4, 5, 6)]
            ev.start("silu_ready", key)
            ev.start("hidT_ready", key)

            def step(i, j):
                for t in range(NT):
                    act.wait_ge(bank_full(4 + t), full0[t] + 2 + j + body * i)
                    act.activation(silu[:, t, :], bank(4 + t)[:, 0:256], ACT.Silu)\
                       .then_inc(sem("silu_ready"), 1)
                act.wait_ge(bank_full(6), full0[2] + 2 + j + body * i)
                act.activation(hidT[:, :, :], split(bank(6), 2), ACT.Copy).then_inc(sem("hidT_ready"), 1)

            loop_blocks(act, total, body, step)
            ev.count["silu_ready"] += 2 * total
            ev.count["hidT_ready"] += total
            was_read(6, ("ffn", key), "hidT_ready")

        def dve_ffn(key, total, body, moe):
            silu0 = ev.base("silu_ready", key)
            ev.start("hidden_ready", key)

            def step(i, j):
                for t in range(NT):
                    dve.wait_ge(sem("silu_ready"), silu0 + 2 * (1 + j) + t + 1 + 2 * body * i)
                    if moe:
                        e = (1 + j) % NE
                        m = dve.scalar_tensor_tensor(out=hid[:, t, :], in0=silu[:, t, :],
                                                     scalar=gates[:, t * NE + e:t * NE + e + 1],
                                                     in1=bank(4 + t)[:, 256:512], op0=ALU.mult, op1=ALU.mult)
                    else:
                        m = dve.tensor_tensor(hid[:, t, :], silu[:, t, :], bank(4 + t)[:, 256:512], ALU.mult)
                    m.then_inc(sem("hidden_ready"), 1)

            loop_blocks(dve, total, body, step)
            ev.count["hidden_ready"] += 2 * total
            for t in range(NT):
                was_read(4 + t, ("ffn", key), "hidden_ready")

        def sp_ffn(key, total, body, gate, up, down):
            r1, r2 = ring_sp["w1"], ring_sp["w2"]
            full5, used2 = ev.base("bank_full5", key), ev.base("w2_used", key)

            def step(i, n):
                n1, n2 = r1 + n, r2 + n
                if n < RING:
                    slot_free("w1")
                else:
                    sp.wait_ge(bank_full(5), full5 + n - RING + 1 + body * i)
                slot = w1[:, n1 % RING, :].rearrange("p (t n) -> p t n", n=COLS)
                for half, src in enumerate((gate(n, i), up(n, i))):
                    sp.dma_start(slot[:, :, half * 256:(half + 1) * 256], src)\
                      .then_inc(sem(f"w1_landed{n1 % RING}"), 16)
                if n < RING2:
                    slot_free("w2")
                else:
                    sp.wait_ge(sem("w2_used"), used2 + n - RING2 + 1 + body * i)
                sp.dma_start(w2[:, n2 % RING2, :, :], down(n, i)).then_inc(sem(f"w2_landed{n2 % RING2}"), 16)

            for n in range(RING):
                step(0, n)
                ring_sp["w1"] += 1
                ring_sp["w2"] += 1
            trips = (total - RING) // body
            with sp.Fori(0, trips) as i:
                for n in range(RING, RING + body):
                    step(i, n)
            for n in range(RING + trips * body, total):
                step(trips, n - trips * body)
            ring_sp["w1"] = r1 + total
            ring_sp["w2"] = r2 + total

        ffn_rings = {}

        def act_to_fm_split(key, gain=None):
            for c in range(0, KC, 2):
                b = 6 + (c // 2) % 2
                act.wait_ge(bank_full(b), filled_at(b, (key, c // 2)))
                if gain is None:
                    m = act.activation(uh[:, c:c + 2, :], split(bank(b), 2), ACT.Copy)
                else:
                    act.activation(uh[:, c, :], bank(b)[:, 0:T], ACT.Copy, scale=gain(c))
                    m = act.activation(uh[:, c + 1, :], bank(b)[:, T:2 * T], ACT.Copy, scale=gain(c + 1))
                m.then_inc(sem("fm_high"), mark("fm_high", (key, c // 2)))

        def dve_to_fm_split(key, gain=None):
            for c in range(0, KC, 2):
                b = 6 + (c // 2) % 2
                dve.wait_ge(sem("fm_high"), at("fm_high", (key, c // 2)))
                if gain is None:
                    m = dve.tensor_tensor(ul[:, c:c + 2, :], split(bank(b), 2), uh[:, c:c + 2, :], ALU.subtract)
                else:
                    for x in range(2):
                        m = dve.scalar_tensor_tensor(out=ul[:, c + x, :], in0=bank(b)[:, x * T:(x + 1) * T],
                                                     scalar=gain(c + x), in1=uh[:, c + x, :],
                                                     op0=ALU.mult, op1=ALU.subtract)
                m.then_inc(sem("fm_split"), mark("fm_split", (key, c // 2)))
                was_read(b, (key, c // 2), "fm_split")

        def products(bank_out, x_hi, x_lo, w_hi, w_lo, first, last):
            pe.matmul(bank_out, x_hi, w_hi, start=first, stop=False, skip_group_check=True)
            pe.matmul(bank_out, x_hi, w_lo, start=False, stop=False, skip_group_check=True)
            return pe.matmul(bank_out, x_lo, w_hi, start=False, stop=last, skip_group_check=True)

        def pe_dense(key, fm_key, total, body):
            ffn_rings[key] = ring_pe["w1"], ring_pe["w2"]
            split0 = [ev.base(f"unit_split{x}", key) for x in range(3)]
            hid0, hidT0 = ev.base("hidden_ready", key), ev.base("hidT_split", key)
            for name in ("bank_full4", "bank_full5", "bank_full6", "unit_used0", "unit_used2"):
                ev.start(name, key)

            def up(i, j):
                for x in range(2):
                    pe.wait_ge(sem(f"unit_split{x}"), split0[x] + j + 2 + body * i)
                    if j < 0:
                        pe.wait_ge(sem("fm_split"), at("fm_split", (fm_key, 2 * x + 1)))
                    whi, wlo = (units[:, x, y, :].rearrange("p (t n) -> p t n", n=COLS) for y in range(2))
                    for t in range(NT):
                        if x == 0 and j < 0:
                            claim(4 + t)
                        elif x == 0:
                            pe.wait_ge(sem("hidden_ready"), hid0 + 2 * j + t + 1 + 2 * body * i)
                        cut = slice(t * P, (t + 1) * P)
                        for k in range(4):
                            m = products(bank(4 + t), uh[:, 4 * x + k, cut], ul[:, 4 * x + k, cut],
                                         whi[:, k, :], wlo[:, k, :], first=(x == 0 and k == 0),
                                         last=(x == 1 and k == 3))
                        if x == 1:
                            m.then_inc(bank_full(4 + t), 1)
                    if x == 0:
                        m.then_inc(sem("unit_used0"), 1)

            def turn(i, j):
                if j < 0:
                    claim(6)
                pe.wait_ge(sem("hidden_ready"), hid0 + 2 * (j + 2) + 2 * body * i)
                for c in range(2):
                    for t in range(NT):
                        m = pe.transpose(bank(6)[:, c * T + t * P:c * T + (t + 1) * P],
                                         hid[:, t, c * P:(c + 1) * P], cst("ident"))
                m.then_inc(bank_full(6), 1)

            def down(i, j, first=False, last=False):
                if first:
                    claim(0, 1, 2, 3)
                pe.wait_ge(sem("unit_split2"), split0[2] + j + 2 + body * i)
                pe.wait_ge(sem("hidT_split"), hidT0 + j + 2 + body * i)
                whi, wlo = (units[:, 2, y, :].rearrange("p (t n) -> p t n", n=D) for y in range(2))
                for t in range(NT):
                    for half in range(2):
                        cut, cols_of = slice(t * P, (t + 1) * P), slice(half * 512, (half + 1) * 512)
                        for c in range(2):
                            m = products(acc[:, 2 * t + half, :], hT[:, 0, c, cut], hT[:, 1, c, cut],
                                         whi[:, c, cols_of], wlo[:, c, cols_of],
                                         first=(first and c == 0), last=(last and c == 1))
                        if last:
                            m.then_inc(bank_full(2 * t + half), fill(2 * t + half, key))
                if not last:
                    m.then_inc(sem("unit_used2"), 1)

            def step(i, j):
                up(i, j)
                if j >= 0:
                    down(i, j - 1, first=(j == 0))
                turn(i, j)

            loop_blocks(pe, total, body, step)
            trips = (total - 2) // body
            down(trips, total - 2 - trips * body, last=True)
            ring_pe["w1"] += total
            ring_pe["w2"] += total
            for b in (4, 5, 6):
                ev.count[f"bank_full{b}"] += total
                last_fill[b] = ("ffn", key)
            ev.count["unit_used0"] += total
            ev.count["unit_used2"] += total - 1

        def act_unit(key, x, i, n, body):
            r1, r2 = ffn_rings[key]
            used = ("unit_used0", "moe_up" if key == "moe" else "bank_full5", "unit_used2")[x]
            if x == 2:
                n2 = r2 + n
                act.wait_ge(sem(f"w2_landed{n2 % RING2}"), 16 * (n2 // RING2 + 1) + 16 * (body // RING2) * i)
                src = w2[:, n2 % RING2, :, :].rearrange("p c n -> p (c n)")
            else:
                n1 = r1 + n
                act.wait_ge(sem(f"w1_landed{n1 % RING}"), 32 * (n1 // RING + 1) + 32 * (body // RING) * i)
                src = w1[:, n1 % RING, 2048 * x:2048 * (x + 1)]
            if n > 0 or not isinstance(i, int) or i > 0:
                act.wait_ge(sem(used), ev.base(used, key) + n + body * i)
            for piece in range(2):
                cut = slice(1024 * piece, 1024 * (piece + 1))
                act.activation(units[:, x, 0, cut], src[:, cut], ACT.Copy).then_inc(sem(f"unit_hi{x}"), 1)

        def dve_unit(key, x, i, n, body, pieces=(0, 1)):
            r1, r2 = ffn_rings[key]
            if x == 2:
                src = w2[:, (r2 + n) % RING2, :, :].rearrange("p c n -> p (c n)")
            else:
                src = w1[:, (r1 + n) % RING, 2048 * x:2048 * (x + 1)]
            for piece in pieces:
                cut = slice(1024 * piece, 1024 * (piece + 1))
                dve.wait_ge(sem(f"unit_hi{x}"), ev.base(f"unit_hi{x}", key) + 2 * n + piece + 1 + 2 * body * i)
                m = dve.tensor_tensor(units[:, x, 1, cut], src[:, cut], units[:, x, 0, cut], ALU.subtract)
            if 1 in pieces:
                m.then_inc(sem(f"unit_split{x}"), 1)

        def is_last(i, j, total, body):
            return isinstance(i, int) and 1 + j + body * i == total - 1

        def act_dense(key, total, body):
            full0 = [ev.base(f"bank_full{b}", key) for b in (4, 5, 6)]
            ev.start("silu_ready", key)
            ev.start("hidT_high", key)

            def step(i, j):
                more = not is_last(i, j, total, body)
                if more:
                    act_unit(key, 0, i, j + 2, body)
                for t in range(NT):
                    act.wait_ge(bank_full(4 + t), full0[t] + 2 + j + body * i)
                    act.activation(silu[:, t, :], bank(4 + t)[:, 0:256], ACT.Silu)\
                       .then_inc(sem("silu_ready"), 1)
                if more:
                    act_unit(key, 1, i, j + 2, body)
                act.wait_ge(bank_full(6), full0[2] + 2 + j + body * i)
                act.activation(hT[:, 0, :, :], split(bank(6), 2), ACT.Copy).then_inc(sem("hidT_high"), 1)
                act_unit(key, 2, i, j + 1, body)

            loop_blocks(act, total, body, step)
            ev.count["silu_ready"] += 2 * total
            ev.count["hidT_high"] += total
            for x in range(3):
                ev.count[f"unit_hi{x}"] += 2 * total

        def dve_dense(key, total, body):
            silu0, high0 = ev.base("silu_ready", key), ev.base("hidT_high", key)
            ev.start("hidden_ready", key)
            ev.start("hidT_split", key)

            def step(i, j):
                more = not is_last(i, j, total, body)
                if more:
                    dve_unit(key, 0, i, j + 2, body)
                for t in range(NT):
                    dve.wait_ge(sem("silu_ready"), silu0 + 2 * (1 + j) + t + 1 + 2 * body * i)
                    dve.tensor_tensor(hid[:, t, :], silu[:, t, :], bank(4 + t)[:, 256:512], ALU.mult)\
                       .then_inc(sem("hidden_ready"), 1)
                if more:
                    dve_unit(key, 1, i, j + 2, body)
                dve.wait_ge(sem("hidT_high"), high0 + 2 + j + body * i)
                dve.tensor_tensor(hT[:, 1, :, :], split(bank(6), 2), hT[:, 0, :, :], ALU.subtract)\
                   .then_inc(sem("hidT_split"), 1)
                dve_unit(key, 2, i, j + 1, body)

            loop_blocks(dve, total, body, step)
            ev.count["hidden_ready"] += 2 * total
            ev.count["hidT_split"] += total
            r1, r2 = ffn_rings[key]
            for n in range(total):
                released("w1", r1 + n, "unit_split1", ev.count["unit_split1"] + n + 1)
                released("w2", r2 + n, "unit_split2", ev.count["unit_split2"] + n + 1)
            for x in range(3):
                ev.count[f"unit_split{x}"] += total
            for t in range(NT):
                was_read(4 + t, ("ffn", key), "hidden_ready")
            was_read(6, ("ffn", key), "hidT_split")

        def act_first_unit(key):
            for x in range(3):
                ev.start(f"unit_hi{x}", key)
            act_unit(key, 0, 0, 0, 4)

        def act_dense_prenorm(key, row):
            act_prenorm_sums((key, "pre"))
            act_first_unit(key)
            act_to_fm_split((key, "pre"), gain=lambda c: pcol("norm_g", row * 8 + c))
            act_unit(key, 1, 0, 0, 4)

        def dve_dense_prenorm(key, row):
            for x in range(3):
                ev.start(f"unit_split{x}", key)
            dve_prenorm((key, "pre"))
            dve_unit(key, 0, 0, 0, 4)
            dve_to_fm_split((key, "pre"), gain=lambda c: pcol("norm_g", row * 8 + c))
            dve_unit(key, 1, 0, 0, 4)

        def run_ahead(total, trips, body, up, down):
            for n in range(RING):
                up(0, n)
                ring_sp["w1"] += 1
                if n >= RING - RING2:
                    down(0, n - (RING - RING2))
                    ring_sp["w2"] += 1
            with sp.Fori(0, trips) as i:
                for n in range(RING, RING + body):
                    up(i, n)
                    down(i, n - RING + RING2)
            for n in range(RING + trips * body, total + RING - RING2):
                if n < total:
                    up(trips, n - trips * body)
                down(trips, n - trips * body - RING + RING2)
            ring_sp["w1"] += total - RING
            ring_sp["w2"] += total - RING2

        def sp_dense(key, total, body, gate, up, down):
            r1, r2 = ring_sp["w1"], ring_sp["w2"]
            split1, split2 = ev.base("unit_split1", key), ev.base("unit_split2", key)

            def load_up(i, n):
                n1 = r1 + n
                if n < RING:
                    slot_free("w1")
                else:
                    sp.wait_ge(sem("unit_split1"), split1 + n - RING + 1 + body * i)
                slot = w1[:, n1 % RING, :].rearrange("p (t n) -> p t n", n=COLS)
                for half, src in enumerate((gate(n, i), up(n, i))):
                    sp.dma_start(slot[:, :, half * 256:(half + 1) * 256], src)\
                      .then_inc(sem(f"w1_landed{n1 % RING}"), 16)

            def load_down(i, n):
                n2 = r2 + n
                if n < RING2:
                    slot_free("w2")
                else:
                    sp.wait_ge(sem("unit_split2"), split2 + n - RING2 + 1 + body * i)
                sp.dma_start(w2[:, n2 % RING2, :, :], down(n, i)).then_inc(sem(f"w2_landed{n2 % RING2}"), 16)

            run_ahead(total, (total - RING) // body, body, load_up, load_down)

        def dense_sources(wg, wu, wd, body):
            g, uu = (x.rearrange("(t p) n -> p t n", p=P) for x in (wg, wu))
            d = wd.rearrange("(b c p) n -> b p c n", c=2, p=P)
            return (lambda n, i: g[:, :, bass.ds(256 * n + 256 * body * i, 256)],
                    lambda n, i: uu[:, :, bass.ds(256 * n + 256 * body * i, 256)],
                    lambda n, i: d[bass.ds(n + body * i, 1)].rearrange("b p c n -> p (b c) n"))

        def moe_sources(wg, wu, wd):
            def cols_of(w):
                v = w.rearrange("e (t p) n -> e p t n", p=P)
                return lambda n, i: v[n % NE][:, :, bass.ds(256 * (n // NE) + 256 * i, 256)]
            d = wd.rearrange("e (b c p) n -> e b p c n", c=2, p=P)
            return (cols_of(wg), cols_of(wu),
                    lambda n, i: d[n % NE][bass.ds(n // NE + i, 1)].rearrange("b p c n -> p (b c) n"))

        BODY = 2 * MOEB
        ysum = view(0, NT, D)
        mye = view(4096, D)
        msilu = view(20480, 256)
        mhid = msilu
        mG, mW = view(20736, NT, P), view(20992, NT, P)
        mWT = [view(21248 + 256 * i, T) for i in range(2)]
        mx = [[x[:, KC // 2 * i:KC // 2 * (i + 1), :].rearrange("p c (x n) -> p (c x) n", n=P)
               for i in range(2)] for x in (uh, ul)]
        mhT = [hT[:, y, :, 0:P] for y in range(2)]
        slot_of, gate_of = split(smax, NT), split(ssum, NT)
        TRIPS = NE // 2

        def moe_trips(engine, trip):
            with engine.Fori(0, TRIPS - 1) as i:
                trip(i, False)
            trip(TRIPS - 1, True)

        def pe_moe():
            r1, r2 = ring_pe["w1"], ring_pe["w2"]
            ffn_rings["moe"] = r1, r2
            for name in ("unit_used0", "unit_used2", "moe_up"):
                ev.start(name, "moe")
            split0 = [ev.base(f"unit_split{x}", "moe") for x in range(3)]

            def gather(i, e, half):
                if half == 0:
                    pe.wait_ge(sem("moe_picked"), 2 * i + e + 1)
                    if not (isinstance(i, int) and 2 * i + e == 0):
                        pe.wait_ge(sem("moe_moved"), 6 * i + 3 * e)
                else:
                    pe.wait_ge(sem("moe_low"), 4 * i + 2 * e + 1)
                for c in range(4):
                    for t in range(NT):
                        k = 4 * half + c
                        m = pe.matmul(bank(7)[:, c * P:(c + 1) * P], h[:, t, k * P:(k + 1) * P], mG[:, t, :],
                                      start=(t == 0), stop=(t == NT - 1))
                m.then_inc(sem("moe_prepared"), 1)

            def turn_weighted(i, e):
                pe.wait_ge(sem("moe_low"), 4 * i + 2 * e + 2)
                for t in range(NT):
                    m = pe.transpose(bank(7)[:, t * P:(t + 1) * P], mW[:, t, :], cst("ident"))
                m.then_inc(sem("moe_prepared"), 1)

            def up(i, b):
                e, c = b // MOEB, b % MOEB
                if c == 0:
                    pe.wait_ge(sem("moe_moved"), 6 * i + 3 * e + 3)
                    pe.wait_ge(sem("moe_low"), 4 * i + 2 * e + 2)
                pe.wait_ge(sem("moe_hidden"), BODY * i + b + 1)
                for x in range(2):
                    pe.wait_ge(sem(f"unit_split{x}"), split0[x] + BODY * i + b + 1)
                    whi, wlo = (units[:, x, y, :].rearrange("p (t n) -> p t n", n=COLS) for y in range(2))
                    for k in range(4):
                        m = products(bank(4), mx[0][e][:, 4 * x + k, :], mx[1][e][:, 4 * x + k, :],
                                     whi[:, k, :], wlo[:, k, :], first=(x == 0 and k == 0),
                                     last=(x == 1 and k == 3))
                    if x == 0:
                        m.then_inc(sem("unit_used0"), 1)
                m.then_inc(sem("moe_up"), 1)

            def down(i, b):
                pe.wait_ge(sem("unit_split2"), split0[2] + BODY * i + b + 1)
                pe.wait_ge(sem("moe_hidT"), BODY * i + b + 1)
                if b == MOEB:
                    pe.wait_ge(sem("moe_ye"), 4 * i + 2)
                whi, wlo = (units[:, 2, y, :].rearrange("p (t n) -> p t n", n=D) for y in range(2))
                for half in range(2):
                    cut = slice(half * 512, (half + 1) * 512)
                    for c in range(2):
                        m = products(bank(half), mhT[0][:, c, :], mhT[1][:, c, :], whi[:, c, cut], wlo[:, c, cut],
                                     first=(b % MOEB == 0 and c == 0), last=(b % MOEB == MOEB - 1 and c == 1))
                m.then_inc(sem("unit_used2"), 1)

            def scatter(i, e):
                pe.wait_ge(sem("moe_ye"), 4 * i + 2 * e + 2)
                for t in range(NT):
                    pe.wait_ge(sem("moe_added"), 8 * i + 4 * e + 2 * t + 1)
                    for half in range(2):
                        pe.matmul(bank(2 + half), mWT[e][:, t * P:(t + 1) * P], mye[:, half * 512:(half + 1) * 512],
                                  start=True, stop=True).then_inc(sem("moe_scattered"), 1)

            def trip(i, final):
                for b in range(BODY):
                    e, c = b // MOEB, b % MOEB
                    up(i, b)
                    if b:
                        down(i, b - 1)
                    pe.wait_ge(sem("moe_hidden"), BODY * i + b + 2)
                    for k in range(2):
                        m = pe.transpose(bank(6)[:, k * P:(k + 1) * P], mhid[:, k * P:(k + 1) * P], cst("ident"))
                    m.then_inc(sem("moe_turned"), 1)
                    if b == MOEB + 2:
                        scatter(i, 0)
                    if not (final and e == 1):
                        if c in (6, 7):
                            gather(i, e + 1, c - 6)
                        if c == 8:
                            turn_weighted(i, e + 1)
                down(i, BODY - 1)
                scatter(i, 1)

            claim(0, 1, 2, 3, 4, 6, 7)
            gather(0, 0, 0)
            gather(0, 0, 1)
            turn_weighted(0, 0)
            moe_trips(pe, trip)
            ring_pe["w1"] += NE * MOEB
            ring_pe["w2"] += NE * MOEB
            ev.count["unit_used0"] += NE * MOEB
            ev.count["unit_used2"] += NE * MOEB
            for b in (0, 1, 2, 3, 4, 6, 7):
                last_fill[b] = "moe"

        def act_moe():
            down0 = ev.base("unit_used2", "moe")

            def moved(i, e, part):
                act.wait_ge(sem("moe_prepared"), 6 * i + 3 * e + part + 1)
                if part < 2:
                    act.activation(mx[0][e % 2][:, 4 * part:4 * part + 4, :], split(bank(7), 4), ACT.Copy)\
                       .then_inc(sem("moe_moved"), 1)
                else:
                    act.activation(mWT[e % 2][:, :], bank(7)[:, 0:T], ACT.Copy).then_inc(sem("moe_moved"), 1)

            def output(i, e):
                act.wait_ge(sem("unit_used2"), down0 + BODY * i + MOEB * (e + 1))
                for half in range(2):
                    act.activation(mye[:, half * 512:(half + 1) * 512], bank(half), ACT.Copy)\
                       .then_inc(sem("moe_ye"), 1)

            def trip(i, final):
                for b in range(BODY):
                    more = not (final and b == BODY - 1)
                    if more:
                        act_unit("moe", 0, i, b + 1, BODY)
                    act.wait_ge(sem("moe_up"), BODY * i + b + 1)
                    act.activation(msilu[:, :], bank(4)[:, 0:256], ACT.Silu).then_inc(sem("moe_silu"), 1)
                    if b == MOEB:
                        output(i, 0)
                    if more:
                        act_unit("moe", 1, i, b + 1, BODY)
                    act.wait_ge(sem("moe_turned"), BODY * i + b + 1)
                    act.activation(mhT[0], split(bank(6)[:, 0:256], 2), ACT.Copy).then_inc(sem("moe_hidT_high"), 1)
                    act_unit("moe", 2, i, b, BODY)
                    if b % MOEB in (6, 7, 8) and not (final and b >= MOEB):
                        moved(i, b // MOEB + 1, b % MOEB - 6)
                output(i, 1)

            for part in range(3):
                moved(0, 0, part)
            moe_trips(act, trip)
            for x in range(3):
                ev.count[f"unit_hi{x}"] += 2 * NE * MOEB
            for b, name, count in ((0, "moe_ye", 2 * NE), (1, "moe_ye", 2 * NE), (7, "moe_moved", 3 * NE)):
                ev.seen[("read", b, "moe")] = (name, count)

        def dve_moe():
            def pick(i, e):
                if not (isinstance(i, int) and 2 * i + e == 0):
                    dve.wait_ge(sem("moe_prepared"), 6 * i + 3 * e)
                for t in range(NT):
                    col = slot_of[:, t, bass.ds(2 * i + e, 1)]
                    dve.tensor_scalar(mG[:, t, :], cst("iota128"), col, None, ALU.is_equal)\
                       .then_inc(sem("moe_matrix"), 1)
                    m = dve.tensor_scalar(mW[:, t, :], cst("iota128"), col, gate_of[:, t, bass.ds(2 * i + e, 1)],
                                          ALU.is_equal, ALU.mult)
                    m.then_inc(sem("moe_picked" if t else "moe_matrix"), 1)

            def low(i, e, half):
                dve.wait_ge(sem("moe_moved"), 6 * i + 3 * e + half + 1)
                cut = slice(4 * half, 4 * half + 4)
                dve.tensor_tensor(mx[1][e % 2][:, cut, :], split(bank(7), 4), mx[0][e % 2][:, cut, :], ALU.subtract)\
                   .then_inc(sem("moe_low"), 1)

            def add(i, e):
                for t in range(NT):
                    for half in range(2):
                        dve.wait_ge(sem("moe_scattered"), 8 * i + 4 * e + 2 * t + half + 1)
                        cut = slice(half * 512, (half + 1) * 512)
                        dve.tensor_tensor(ysum[:, t, cut], ysum[:, t, cut], bank(2 + half), ALU.add)\
                           .then_inc(sem("moe_added"), 1)

            def trip(i, final):
                for b in range(BODY):
                    more = not (final and b == BODY - 1)
                    if more:
                        dve_unit("moe", 0, i, b + 1, BODY)
                    dve.wait_ge(sem("moe_silu"), BODY * i + b + 1)
                    dve.tensor_tensor(mhid[:, :], msilu[:, :], bank(4)[:, 256:512], ALU.mult)\
                       .then_inc(sem("moe_hidden"), 1)
                    if more:
                        dve_unit("moe", 1, i, b + 1, BODY)
                    dve.wait_ge(sem("moe_hidT_high"), BODY * i + b + 1)
                    dve.tensor_tensor(mhT[1], split(bank(6)[:, 0:256], 2), mhT[0], ALU.subtract)\
                       .then_inc(sem("moe_hidT"), 1)
                    dve_unit("moe", 2, i, b, BODY)
                    if b == MOEB + 2:
                        add(i, 0)
                    if not (final and b >= MOEB):
                        if b % MOEB == 5:
                            pick(i, b // MOEB + 1)
                        if b % MOEB in (6, 7):
                            low(i, b // MOEB + 1, b % MOEB - 6)
                add(i, 1)
                dve.wait_ge(sem("moe_added"), 8 * i + 9)

            dve.memset(ysum[:, :, :], 0.0).then_inc(sem("moe_added"), 1)
            dve.memset(mhid[:, :], 0.0).then_inc(sem("moe_hidden"), 1)
            dve.wait_ge(sem("moe_added"), 1)
            dve.wait_ge(sem("moe_hidden"), 1)
            pick(0, 0)
            low(0, 0, 0)
            low(0, 0, 1)
            moe_trips(dve, trip)
            r1, r2 = ffn_rings["moe"]
            for n in range(NE * MOEB):
                released("w1", r1 + n, "unit_split1", ev.count["unit_split1"] + n + 1)
                released("w2", r2 + n, "unit_split2", ev.count["unit_split2"] + n + 1)
            for x in range(3):
                ev.count[f"unit_split{x}"] += NE * MOEB
            for b, name, count in ((2, "moe_added", 4 * NE + 1), (3, "moe_added", 4 * NE + 1),
                                   (4, "moe_hidden", NE * MOEB + 1), (6, "moe_hidT", NE * MOEB)):
                ev.seen[("read", b, "moe")] = (name, count)

        def sp_moe(wg, wu, wd):
            r1, r2 = ring_sp["w1"], ring_sp["w2"]
            g, uu = (x.rearrange("e (t p) n -> e p t n", p=P) for x in (wg, wu))
            d = wd.rearrange("e (b c p) n -> e b p c n", c=2, p=P)
            split1, split2 = ev.base("unit_split1", "moe"), ev.base("unit_split2", "moe")

            def load_up(i, n):
                e, c, n1 = n // MOEB, n % MOEB, r1 + n
                if n < RING:
                    slot_free("w1")
                else:
                    sp.wait_ge(sem("unit_split1"), split1 + BODY * i + n - RING + 1)
                slot = w1[:, n1 % RING, :].rearrange("p (t n) -> p t n", n=COLS)
                for half, w in enumerate((g, uu)):
                    src = w[bass.ds(2 * i + e, 1)].rearrange("e p t n -> p (e t) n")[:, :, c * 256:(c + 1) * 256]
                    sp.dma_start(slot[:, :, half * 256:(half + 1) * 256], src)\
                      .then_inc(sem(f"w1_landed{n1 % RING}"), 16)

            def load_down(i, n):
                e, c, n2 = n // MOEB, n % MOEB, r2 + n
                if n < RING2:
                    slot_free("w2")
                else:
                    sp.wait_ge(sem("unit_split2"), split2 + BODY * i + n - RING2 + 1)
                src = d[bass.ds(2 * i + e, 1)].rearrange("e b p c n -> p (e b c) n")[:, 2 * c:2 * c + 2, :]
                sp.dma_start(w2[:, n2 % RING2, :, :], src).then_inc(sem(f"w2_landed{n2 % RING2}"), 16)

            run_ahead(NE * MOEB, TRIPS - 1, BODY, load_up, load_down)

        def overflows(engine):
            engine.wait_ge(sem("most_tokens"), at("most_tokens", 0))
            return engine.value_load(most[0:1, 0:1], min_val=0, max_val=T) > SLOTS

        def dve_conv(name, key, dst, src, chunks, taps, weight, bias, part):
            ev.start(name, key)
            first = ev.count[name]
            for c in part:
                if bias:
                    m = dve.tensor_scalar(dst[:, c, :], src[:, c, 0:T], pcol(weight, c), pcol(bias, c),
                                          ALU.mult, ALU.add)
                else:
                    m = dve.tensor_scalar(dst[:, c, :], src[:, c, 0:T], pcol(weight, c), None, ALU.mult)
                m.then_inc(sem(name), 1)
            w0 = stack_at(weight)
            with dve.Fori(0, taps - 1) as k:
                for n, c in enumerate(part):
                    dve.wait_ge(sem(name), first + n + 1 + len(part) * k)
                    dve.scalar_tensor_tensor(out=dst[:, c, :], in0=src[:, c, bass.ds(k + 1, T)],
                                             scalar=par[:, bass.ds(k * chunks + (w0 + chunks + c), 1)],
                                             in1=dst[:, c, :], op0=ALU.mult, op1=ALU.add)\
                       .then_inc(sem(name), 1)
            ev.count[name] += len(part) * taps
            ev.seen[(name, key)] = ev.count[name]

        yab = view(0, 16, T)
        cin = view(4096, 8, T + TAPS - 1)
        sq_c = view(4096, 8, T)
        hc = view(6384, 8, T)
        state = view(6384, 1024)
        sg = view(8432, 8, T)
        var_c = view(8432, T)
        xdt = view(8432, NT, 1024)
        xp = view(10480, 12, T + SCONV - 1)
        L = view(10480, 16, P)
        xds = view(12528, 1024)
        xc = view(13588, 12, T)
        y = view(13588, NT, 1024)
        zs = view(16660, NT, 1024)
        xs = view(18708, NT, 1024)
        cbm = view(20756, 2, P)
        BT = view(21012, 256)
        o = 21268
        wdt = view(o, KC, 16)
        dtx, dtl, dt, adt, acs, eac = (view(o + 128 + 32 * i, 32) for i in range(6))
        ea = view(o + 320, 16)
        dse = view(o + 336, 16)
        KEYS_A = [("g", 0, 1024), ("v", 0, 0), ("g", 1, 1536), ("v", 1, 512)]

        def pe_mixer_a():
            for name, i, _ in KEYS_A:
                pe_cols_fm(u, ("A", name, i))
            claim(6)
            pe.wait_ge(sem("wdt_landed"), 16)
            for t in range(NT):
                for k in range(KC):
                    m = pe.matmul(bank(6)[:, t * 16:(t + 1) * 16], u[:, k, t * P:(t + 1) * P], wdt[:, k, :],
                                  start=(k == 0), stop=(k == KC - 1))
            m.then_inc(bank_full(6), fill(6, ("A", "dt")))
            for i in range(3):
                pe_cols_fm(u, ("A", "xbc", i))
            pe.wait_ge(sem("conv_tap"), at("conv_tap", "A"))
            claim(6)
            for c in range(8):
                m = pe.matmul(bank(6)[:, 0:T], cst("ones"), hc[:, c, :], start=(c == 0), stop=(c == 7))
            m.then_inc(bank_full(6), fill(6, ("A", "sum")))
            pe_cols_tm(u, ("A", "z", 0))
            pe.wait_ge(sem("squared"), at("squared", "A"))
            claim(7)
            for c in range(8):
                m = pe.matmul(bank(7)[:, 0:T], cst("ones"), sq_c[:, c, :], start=(c == 0), stop=(c == 7))
            m.then_inc(bank_full(7), fill(7, ("A", "sumsq")))
            pe_cols_tm(u, ("A", "z", 1))
            for t in range(NT):
                for b in range(2):
                    claim(4 + b)
                    pe.wait_ge(sem("xbc_ready"), at("xbc_ready", 4 * b + 3))
                    for c in range(4):
                        m = pe.transpose(bank(4 + b)[:, c * P:(c + 1) * P], xc[:, 4 * b + c, t * P:(t + 1) * P],
                                         cst("ident"))
                    m.then_inc(bank_full(4 + b), fill(4 + b, ("A", "xs", t)))
            pe.wait_ge(sem("xbc_ready"), at("xbc_ready", 11))
            claim(6)
            for g in range(2):
                m = pe.transpose(bank(6)[:, g * P:(g + 1) * P], xc[:, 8 + g, 0:P], cst("ident"))
            m.then_inc(bank_full(6), fill(6, ("A", "BT")))
            for t in range(NT):
                pe.wait_ge(sem("adt"), at("adt", "A"))
                claim(7)
                pe.matmul(bank(7)[:, 0:16], cst("upper"), adt[:, 16 * t:16 * t + 16], start=True, stop=True)
                pe.matmul(bank(7)[:, 16:32], cst("ones"), adt[:, 16 * t:16 * t + 16], start=True, stop=True)
                for g in range(2):
                    m = pe.matmul(bank(7)[:, P + g * P:P + (g + 1) * P], xc[:, 8 + g, t * P:(t + 1) * P],
                                  xc[:, 10 + g, t * P:(t + 1) * P], start=True, stop=True)
                m.then_inc(bank_full(7), fill(7, ("A", "col", t)))
                for b in range(4):
                    claim(b)
                    for i in range(4):
                        hh = 4 * b + i
                        m = pe.matmul(bank(b)[:, i * P:(i + 1) * P],
                                      adt[:, 16 * t + hh:16 * t + hh + 1].broadcast_to([P, P]), cst("upper"),
                                      start=True, stop=True)
                    m.then_inc(bank_full(b), fill(b, ("A", "row", t)))
                if t == 0:
                    pe.wait_ge(sem("xds"), at("xds", "A"))
                    pe.wait_ge(sem("BT"), at("BT", "A"))
                    for g in range(2):
                        claim(6 + g)
                        m = pe.matmul(bank(6 + g), BT[:, g * P:(g + 1) * P], xds[:, g * 512:(g + 1) * 512],
                                      start=True, stop=True)
                        m.then_inc(bank_full(6 + g), fill(6 + g, ("A", "state")))
                else:
                    pe.wait_ge(sem("state"), at("state", 1))
                    for g in range(2):
                        claim(6 + g)
                        m = pe.matmul(bank(6 + g), xc[:, 10 + g, P:T], state[:, g * 512:(g + 1) * 512],
                                      start=True, stop=True)
                        m.then_inc(bank_full(6 + g), fill(6 + g, ("A", "yoff")))
                pe.wait_ge(sem("weighted"), at("weighted", ("A", t)))
                claim(4, 5)
                for hh in range(16):
                    m = pe.matmul(bank(4 + hh // 8)[:, (hh % 8) * 64:(hh % 8 + 1) * 64], L[:, hh, :],
                                  xdt[:, t, hh * 64:(hh + 1) * 64], start=True, stop=True)
                    if hh % 8 == 7:
                        m.then_inc(bank_full(4 + hh // 8), fill(4 + hh // 8, ("A", "ydiag", t)))
            pe.wait_ge(sem("normed"), at("normed", ("A", "y", 1)))
            pe_to_fm(y, KC, ("A", "y"))
            pe_fm_wait(("A", "y"), KC)
            pe.wait_ge(sem("ya"), at("ya", 7))
            pe_rows_acc(yab, 16, "mixA")

        def act_mixer_a():
            for i in range(2):
                for b in range(2):
                    act.wait_ge(bank_full(4 + b), filled_at(4 + b, ("A", "g", i)))
                    act.activation(sg[:, 4 * i + 2 * b:4 * i + 2 * b + 2, :], split(bank(4 + b), 2),
                                        ACT.Sigmoid).then_inc(sem("sigma"), mark_read("sigma", 4 + b, ("A", "g", i)))
            act.wait_ge(sem("dtx"), at("dtx", "A"))
            A(act.activation(dtl[:, :], dtx[:, :], ACT.Abs))
            A(act.activation(dtl[:, :], dtl[:, :], ACT.Exp, scale=-1.0))
            act.activation(dtl[:, :], dtl[:, :], ACT.Ln, bias=1.0).then_inc(sem("dtl"), mark("dtl", "A"))
            act.activation(ea[:, :], alog, ACT.Exp).then_inc(sem("ea"), mark("ea", "A"))
            for i in range(3):
                for b in range(2):
                    act.wait_ge(bank_full(4 + b), filled_at(4 + b, ("A", "xbc", i)))
                    act.activation(xp[:, 4 * i + 2 * b:4 * i + 2 * b + 2, SCONV - 1:], split(bank(4 + b), 2),
                                        ACT.Copy).then_inc(sem("xbc_in"), mark_read("xbc_in", 4 + b, ("A", "xbc", i)))
            act.wait_ge(sem("centred"), at("centred", "A"))
            act.activation(sq_c[:, :, :], hc[:, :, :], ACT.Square).then_inc(sem("squared"), mark("squared", "A"))
            for i in range(2):
                for t in range(NT):
                    act.wait_ge(bank_full(4 + t), filled_at(4 + t, ("A", "z", i)))
                    act.activation(zs[:, t, i * 512:(i + 1) * 512], bank(4 + t), ACT.Silu)\
                        .then_inc(sem("zs"), mark_read("zs", 4 + t, ("A", "z", i)))
            act.wait_ge(sem("var_c"), at("var_c", "A"))
            act.activation(var_c[:, :], var_c[:, :], ACT.Sqrt).then_inc(sem("root_c"), mark("root_c", "A"))
            act.wait_ge(sem("ssm_tap"), at("ssm_tap", "A"))
            for c in range(12):
                act.activation(xc[:, c, :], xc[:, c, :], ACT.Silu, bias=pcol("ssm_conv_b", c))\
                    .then_inc(sem("xbc_ready"), mark("xbc_ready", c))
            for t in range(NT):
                for b in range(2):
                    act.wait_ge(bank_full(4 + b), filled_at(4 + b, ("A", "xs", t)))
                    act.activation(xs[:, t, b * 512:(b + 1) * 512], bank(4 + b), ACT.Copy)\
                        .then_inc(sem("xs"), mark_read("xs", 4 + b, ("A", "xs", t)))
            act.wait_ge(bank_full(6), filled_at(6, ("A", "BT")))
            act.activation(BT[:, :], bank(6)[:, 0:256], ACT.Copy).then_inc(sem("BT"), mark("BT", "A"))
            was_read(6, ("A", "BT"), "BT")
            act.wait_ge(sem("scaled_c"), at("scaled_c", "A"))
            for c in range(8):
                act.activation(yab[:, c, :], hc[:, c, :], ACT.Silu, bias=pcol("conv_ln_b", c),
                                         scale=pcol("conv_ln_g", c)).then_inc(sem("ya"), mark("ya", c))
            for t in range(NT):
                if t == 0:
                    act.wait_ge(sem("to_end"), at("to_end", "A"))
                    act.activation(dse[:, :], dse[:, :], ACT.Exp).then_inc(sem("dse"), mark("dse", "A"))
                act.wait_ge(sem("acs"), at("acs", ("A", t)))
                act.activation(eac[:, 16 * t:16 * t + 16], acs[:, 16 * t:16 * t + 16], ACT.Exp)\
                    .then_inc(sem("eac"), mark("eac", ("A", t)))
                act.wait_ge(sem("diff"), at("diff", ("A", t)))
                act.activation(L[:, :, :], L[:, :, :], ACT.Exp).then_inc(sem("decayed"), mark("decayed", ("A", t)))
                if t == 0:
                    for g in range(2):
                        act.wait_ge(bank_full(6 + g), filled_at(6 + g, ("A", "state")))
                        act.activation(state[:, g * 512:(g + 1) * 512], bank(6 + g), ACT.Copy)\
                            .then_inc(sem("state"), mark("state", g))
                        was_read(6 + g, ("A", "state"), "state")
            act.wait_ge(sem("gated"), at("gated", ("A", 1)))
            for t in range(NT):
                m = act.activation(L.rearrange("p a b -> p (a b)")[:, t * 1024:(t + 1) * 1024], y[:, t, :],
                                   ACT.Square, accum_out=ssq[:, t:t + 1])
            m.then_inc(sem("sumsq"), mark("sumsq", ("A", "y")))
            act_roots(("A", "y"), 2)
            act_to_fm(yab[:, 8:16, :], KC, ("A", "y"), gain=lambda c: pcol("ssm_norm_g", c))

        def dve_mixer_a():
            dve.wait_ge(sem("fm_ready"), at("fm_ready", (("mixA", "pre"), 3)))
            V(dve.memset(cin[:, :, 0:TAPS - 1], 0.0))
            V(dve.memset(xp[:, :, 0:SCONV - 1], 0.0))
            for i in range(2):
                if i == 1:
                    dve_conv("conv_tap", "A half", hc, cin, 8, TAPS, "conv_dw_w", "conv_dw_b", range(4))
                for b in range(2):
                    dve.wait_ge(bank_full(4 + b), filled_at(4 + b, ("A", "v", i)))
                    dve.wait_ge(sem("sigma"), at("sigma", ("read", 4 + b, ("A", "g", i))))
                    c = 4 * i + 2 * b
                    dve.tensor_tensor(cin[:, c:c + 2, TAPS - 1:], sg[:, c:c + 2, :], split(bank(4 + b), 2),
                                           ALU.mult)\
                                               .then_inc(sem("gated_in"), mark_read("gated_in", 4 + b, ("A", "v", i)))
                dve.wait_ge(sem("gated_in"), latest("gated_in"))
            dve.wait_ge(bank_full(6), filled_at(6, ("A", "dt")))
            dve.tensor_tensor(split(dtx, 2), split(bank(6)[:, 0:32], 2), bc(dtb, 1, [P, 2, 16]), ALU.add)\
                .then_inc(sem("dtx"), mark("dtx", "A"))
            was_read(6, ("A", "dt"), "dtx")
            dve_conv("conv_tap", "A", hc, cin, 8, TAPS, "conv_dw_w", "conv_dw_b", range(4, 8))
            dve.wait_ge(bank_full(6), filled_at(6, ("A", "sum")))
            dve.scalar_tensor_tensor(out=hc[:, :, :], in0=bc(bank(6)[:, 0:T], 1, [P, 8, T]),
                                               scalar=-1.0 / 1024, in1=hc[:, :, :], op0=ALU.mult, op1=ALU.add)\
                                                   .then_inc(sem("centred"), mark("centred", "A"))
            was_read(6, ("A", "sum"), "centred")
            dve.wait_ge(sem("xbc_in"), at("xbc_in", ("read", 5, ("A", "xbc", 2))))
            dve_conv("ssm_tap", "A", xc, xp, 12, SCONV, "ssm_conv_w", None, range(12))
            dve.wait_ge(bank_full(7), filled_at(7, ("A", "sumsq")))
            dve.tensor_scalar(var_c[:, :], bank(7)[:, 0:T], 1.0 / 1024, 1e-6, ALU.mult, ALU.add)\
                .then_inc(sem("var_c"), mark("var_c", "A"))
            was_read(7, ("A", "sumsq"), "var_c")
            dve.wait_ge(sem("root_c"), at("root_c", "A"))
            V(dve.reciprocal(var_c[:, :], var_c[:, :]))
            dve.tensor_tensor(hc[:, :, :], hc[:, :, :], bc(var_c, 1, [P, 8, T]), ALU.mult)\
                .then_inc(sem("scaled_c"), mark("scaled_c", "A"))
            dve.wait_ge(sem("scaled_c"), latest("scaled_c"))
            dve.wait_ge(sem("dtl"), at("dtl", "A"))
            dve.wait_ge(sem("ea"), at("ea", "A"))
            V(dve.scalar_tensor_tensor(out=dt[:, :], in0=dtx[:, :], scalar=0.0, in1=dtl[:, :],
                                       op0=ALU.max, op1=ALU.add))
            dve.scalar_tensor_tensor(out=split(adt, 2), in0=split(dt, 2), scalar=-1.0,
                                               in1=bc(ea, 1, [P, 2, 16]), op0=ALU.mult, op1=ALU.mult)\
                                                   .then_inc(sem("adt"), mark("adt", "A"))
            h64 = [P, 16, 64]
            for t in range(NT):
                ts = slice(16 * t, 16 * t + 16)
                dve.wait_ge(bank_full(7), filled_at(7, ("A", "col", t)))
                dve.tensor_copy(acs[:, ts], bank(7)[:, 0:16]).then_inc(sem("acs"), mark("acs", ("A", t)))
                dve.wait_ge(sem("acs"), latest("acs"))
                if t == 0:
                    dve.tensor_tensor(dse[:, :], bank(7)[:, 16:32], acs[:, ts], ALU.subtract)\
                        .then_inc(sem("to_end"), mark("to_end", "A"))
                dve.tensor_tensor(cbm[:, :, :], split(bank(7)[:, P:3 * P], 2), bc(cst("upper"), 1, [P, 2, P]),
                                       ALU.mult).then_inc(sem("masked"), mark_read("masked", 7, ("A", "col", t)))
                for b in range(4):
                    dve.wait_ge(bank_full(b), filled_at(b, ("A", "row", t)))
                dve.tensor_tensor(L[:, :, :], acc[:, :, :].rearrange("p a (b l) -> p (a b) l", l=P),
                                       bc(acs[:, ts], 2, [P, 16, P]), ALU.subtract)\
                                           .then_inc(sem("diff0"), mark_read("diff0", 0, ("A", "row", t)))
                for b in range(1, 4):
                    was_read(b, ("A", "row", t), "diff0")
                dve.wait_ge(sem("diff0"), latest("diff0"))
                dve.tensor_scalar(L[:, :, :], L[:, :, :], 0.0, None, ALU.min)\
                    .then_inc(sem("diff"), mark("diff", ("A", t)))
                dve.wait_ge(sem("xs"), at("xs", ("read", 5, ("A", "xs", t))))
                V(dve.tensor_tensor(split(xdt[:, t, :], 16), split(xs[:, t, :], 16), bc(dt[:, ts], 2, h64),
                                    ALU.mult))
                if t == 0:
                    dve.wait_ge(sem("dse"), at("dse", "A"))
                    dve.tensor_tensor(split(xds, 16), split(xdt[:, 0, :], 16), bc(dse, 2, h64),
                                                ALU.mult).then_inc(sem("xds"), mark("xds", "A"))
                dve.wait_ge(sem("decayed"), at("decayed", ("A", t)))
                L4 = L.rearrange("p (g r) l -> p g r l", g=2)
                dve.tensor_tensor(L4, L4, bc(cbm, 2, [P, 2, 8, P]), ALU.mult)\
                    .then_inc(sem("weighted"), mark("weighted", ("A", t)))
                if t == 0:
                    dve.wait_ge(bank_full(5), filled_at(5, ("A", "xs", 1)))
                V(dve.tensor_tensor(split(y[:, t, :], 16), split(xs[:, t, :], 16), bc(dskip, 2, h64), ALU.mult))
                for b in range(2):
                    dve.wait_ge(bank_full(4 + b), filled_at(4 + b, ("A", "ydiag", t)))
                dve.tensor_tensor(split(y[:, t, :], 2), split(y[:, t, :], 2), duo[:, :, :], ALU.add)\
                    .then_inc(sem("y_diag"), mark_read("y_diag", 4, ("A", "ydiag", t)))
                was_read(5, ("A", "ydiag", t), "y_diag")
                dve.wait_ge(sem("y_diag"), latest("y_diag"))
                if t == 1:
                    for g in range(2):
                        dve.wait_ge(bank_full(6 + g), filled_at(6 + g, ("A", "yoff")))
                    dve.wait_ge(sem("eac"), at("eac", ("A", 1)))
                    dve.tensor_tensor(split(xds, 16), aux[:, :, :].rearrange("p a (b l) -> p (a b) l", l=64),
                                           bc(eac[:, 16:32], 2, h64), ALU.mult)\
                                               .then_inc(sem("y_off"), mark_read("y_off", 6, ("A", "yoff")))
                    was_read(7, ("A", "yoff"), "y_off")
                    dve.wait_ge(sem("y_off"), latest("y_off"))
                    V(dve.tensor_tensor(y[:, t, :], y[:, t, :], xds[:, :], ALU.add))
                dve.wait_ge(sem("zs"), at("zs", ("read", 5, ("A", "z", 1))))
                dve.tensor_tensor(y[:, t, :], y[:, t, :], zs[:, t, :], ALU.mult)\
                    .then_inc(sem("gated"), mark("gated", ("A", t)))
            dve_mean(("A", "y"), 2, 1.0 / 1024, 1e-6)
            dve_recips(("A", "y"), 2)
            for t in range(NT):
                dve.tensor_scalar(y[:, t, :], y[:, t, :], rsd[:, t:t + 1], None, ALU.mult)\
                    .then_inc(sem("normed"), mark("normed", ("A", "y", t)))

        qB, kB = view(4096, 12, T), view(7168, 12, T)
        vB = view(10240, NT, 3, 512)
        sB = [view(13312 + 768 * i, 768) for i in range(2)]
        pB = [view(14848 + 768 * i, 768) for i in range(2)]
        oB = view(16384, NT, 512)
        oBf = view(17408, 4, T)
        UNITS_B = [(hh, qt) for hh in range(8) for qt in range(NT)]

        def pair(tensor, n):
            return tensor.rearrange("p a n -> p (a n)")[:, 0:n]

        def pe_mixer_b():
            for i in range(3):
                pe_cols_fm(u, ("B", "q", i))
            for i in range(3):
                pe_cols_fm(u, ("B", "k", i))
            for i in range(3):
                pe_cols_tm(u, ("B", "v", i))
            pe.wait_ge(sem("qk_ready"), at("qk_ready", ("read", 5, ("B", "k", 2))))

            def scores(n):
                hh, qt = UNITS_B[n]
                nk, b0, r = (qt + 1) * P, 2 * (n % 2), 64 * (hh % 2)
                claim(b0, b0 + 1)
                dst = pair(acc[:, b0:b0 + 2, :], 1024)
                for g in range(3):
                    m = pe.matmul(dst[:, g * nk:(g + 1) * nk], qB[r:r + 64, 4 * g + hh // 2, qt * P:(qt + 1) * P],
                                  kB[r:r + 64, 4 * g + hh // 2, 0:nk], start=True, stop=True)
                m.then_inc(bank_full(b0), fill(b0, ("B", "s", n)))

            def values(n):
                hh, qt = UNITS_B[n]
                nk, b0 = (qt + 1) * P, 2 * (n % 2)
                blocks = 3 * (qt + 1)
                tb = (duo, aux)[n % 2]
                pe.wait_ge(sem("probs"), at("probs", ("B", n)))
                claim(4 + 2 * (n % 2), 5 + 2 * (n % 2))
                for i in range(blocks):
                    m = pe.transpose(pair(tb[:, :, :], 1024)[:, i * P:(i + 1) * P], sB[n % 2][:, i * P:(i + 1) * P],
                                     cst("ident"))
                m.then_inc(bank_full(4 + 2 * (n % 2)), fill(4 + 2 * (n % 2), ("B", "t", n)))
                pe.wait_ge(sem("probsT"), at("probsT", ("B", n)))
                for i in range(blocks):
                    g, kt = i // (qt + 1), i % (qt + 1)
                    m = pe.matmul(acc[:, b0 + 1, 448:512], pB[n % 2][:, i * P:(i + 1) * P],
                                  vB[:, kt, g, hh * 64:(hh + 1) * 64], start=(i == 0), stop=(i == blocks - 1))
                m.then_inc(bank_full(b0 + 1), fill(b0 + 1, ("B", "o", n)))

            scores(0)
            for n in range(len(UNITS_B)):
                if n + 1 < len(UNITS_B):
                    scores(n + 1)
                if n == 0:
                    pe.wait_ge(sem("v_ready"), at("v_ready", ("read", 5, ("B", "v", 2))))
                values(n)
            pe.wait_ge(sem("o_ready"), at("o_ready", ("B", len(UNITS_B) - 1)))
            pe_to_fm(oB, 4, ("B", "o"))
            pe_fm_wait(("B", "o"), 4)
            pe_rows_acc(oBf, 4, "mixB")

        def act_mixer_b():
            for name, dst, scale in (("q", qB, 0.125), ("k", kB, 1.0)):
                for i in range(3):
                    for b in range(2):
                        act.wait_ge(bank_full(4 + b), filled_at(4 + b, ("B", name, i)))
                        act.activation(dst[:, 4 * i + 2 * b:4 * i + 2 * b + 2, :], split(bank(4 + b), 2),
                                            ACT.Copy, scale=scale)\
                                                .then_inc(sem("qk_ready"), mark_read("qk_ready", 4 + b, ("B", name, i)))
            for n, (hh, qt) in enumerate(UNITS_B):
                w = 3 * (qt + 1) * P
                act.wait_ge(sem("negmax"), at("negmax", ("B", n)))
                act.activation(sB[n % 2][:, 0:w], sB[n % 2][:, 0:w], ACT.Exp,
                                         bias=smax[:, n % 2:n % 2 + 1], accum_out=ssum[:, n % 2:n % 2 + 1])\
                                             .then_inc(sem("probs"), mark("probs", ("B", n)))
                b = 4 + 2 * (n % 2)
                act.wait_ge(bank_full(b), filled_at(b, ("B", "t", n)))
                act.activation(pB[n % 2][:, 0:w], pair((duo, aux)[n % 2][:, :, :], w), ACT.Copy)\
                    .then_inc(sem("probsT"), mark("probsT", ("B", n)))
                was_read(b, ("B", "t", n), "probsT")
            act_to_fm(oBf, 4, ("B", "o"))

        def dve_mixer_b():
            for i in range(3):
                for t in range(NT):
                    dve.wait_ge(bank_full(4 + t), filled_at(4 + t, ("B", "v", i)))
                    dve.tensor_copy(vB[:, t, i, :], bank(4 + t))\
                        .then_inc(sem("v_ready"), mark_read("v_ready", 4 + t, ("B", "v", i)))

            def softmax(n):
                hh, qt = UNITS_B[n]
                nk, b0, w = (qt + 1) * P, 2 * (n % 2), 3 * (qt + 1) * P
                slope = 2.0 ** -(hh + 1)
                off = cat[f"dist{qt}0"][0]
                dve.wait_ge(bank_full(b0), filled_at(b0, ("B", "s", n)))
                if n >= 2:
                    dve.wait_ge(bank_full(4 + 2 * (n % 2)), filled_at(4 + 2 * (n % 2), ("B", "t", n - 2)))
                m = dve.scalar_tensor_tensor(out=sB[n % 2][:, 0:w], in0=con[:, off:off + w], scalar=-slope,
                                             in1=pair(acc[:, b0:b0 + 2, :], w), op0=ALU.mult, op1=ALU.add)
                m.then_inc(sem("biased"), mark_read("biased", b0, ("B", "s", n)))
                dve.wait_ge(sem("biased"), latest("biased"))
                dve.tensor_reduce(smax[:, n % 2:n % 2 + 1], sB[n % 2][:, 0:w], AX.X, ALU.max,
                                            negate=True).then_inc(sem("negmax"), mark("negmax", ("B", n)))

            def divide(n):
                hh, qt = UNITS_B[n]
                dve.wait_ge(sem("probs"), at("probs", ("B", n)))
                V(dve.reciprocal(prob[:, n % 2:n % 2 + 1], ssum[:, n % 2:n % 2 + 1]))
                dve.wait_ge(bank_full(2 * (n % 2) + 1), filled_at(2 * (n % 2) + 1, ("B", "o", n)))
                m = dve.tensor_scalar(oB[:, qt, hh * 64:(hh + 1) * 64], acc[:, 2 * (n % 2) + 1, 448:512],
                                      prob[:, n % 2:n % 2 + 1], None, ALU.mult)
                m.then_inc(sem("o_ready"), mark("o_ready", ("B", n)))
                was_read(2 * (n % 2) + 1, ("B", "o", n), "o_ready")

            softmax(0)
            for n in range(len(UNITS_B)):
                if n + 1 < len(UNITS_B):
                    softmax(n + 1)
                divide(n)

        merged = view(0, NT, D)
        cF = view(2048, KC, T)
        rqk = view(4096, 8, T)
        rtmp = view(6144, 2, T)
        rv, rg = view(6656, NT, D), view(8704, NT, D)
        rS = [view(10752 + 384 * i, 384) for i in range(2)]
        ro = view(11520, NT, D)
        rj = view(13568, NT, D)
        gA = view(15616, NT, D)

        def pe_gate(l, name):
            for i in range(2):
                pe_cols_tm(u, (l, name, i))

        def act_gate(l, name, dst):
            for i in range(2):
                for t in range(NT):
                    act.wait_ge(bank_full(4 + t), filled_at(4 + t, (l, name, i)))
                    act.activation(dst[:, t, i * 512:(i + 1) * 512], bank(4 + t), ACT.Sigmoid)\
                        .then_inc(sem("gate_ready"), mark_read("gate_ready", 4 + t, (l, name, i)))

        def dve_merge(l, name, gate, key):
            dve.wait_ge(sem("gate_ready"), at("gate_ready", ("read", 5, (l, name, 1))))
            for t in range(NT):
                for half in range(2):
                    dve.wait_ge(bank_full(2 * t + half), filled_at(2 * t + half, key))
                    cut = slice(half * 512, (half + 1) * 512)
                    dst = merged if name == "ga" else gate
                    m = dve.tensor_tensor(dst[:, t, cut], gate[:, t, cut], acc[:, 2 * t + half, :], ALU.mult)
                    m.then_inc(sem("merging"), mark_read("merging", 2 * t + half, key))
            dve.wait_ge(sem("merging"), latest("merging"))
            if name != "ga":
                for t in range(NT):
                    dve.tensor_tensor(merged[:, t, :], merged[:, t, :], gate[:, t, :], ALU.add)\
                        .then_inc(sem("merged"), mark("merged", (l, name, t)))
                dve.wait_ge(sem("merged"), latest("merged"))

        def pe_retention(l):
            pe_cols_fm(u, (l, "rq"))
            pe_cols_fm(u, (l, "rk"))
            for name in ("rv", "rg"):
                for i in range(2):
                    pe_cols_tm(u, (l, name, i))
            pe_gate(l, "ga")
            pe.wait_ge(sem("rotated"), at("rotated", (l, 3)))
            pe.wait_ge(sem("rv_ready"), at("rv_ready", ("read", 5, (l, "rv", 1))))

            def scores(hh):
                b = 6 + hh % 2
                claim(b)
                pe.matmul(bank(b)[:, 0:T], rqk[:, 4 + hh, 0:P], rqk[:, hh, :], start=True, stop=True)
                m = pe.matmul(bank(b)[:, T:T + P], rqk[:, 4 + hh, P:T], rqk[:, hh, P:T], start=True, stop=True)
                m.then_inc(bank_full(b), fill(b, (l, "rs", hh)))

            def values(hh):
                pe.wait_ge(sem("decayed_scores"), at("decayed_scores", (l, hh)))
                if hh == 0:
                    claim(0, 1, 2, 3)
                half, o0 = hh // 2, (hh % 2) * 256
                s = rS[hh % 2]
                v = [rv[:, t, hh * 256:(hh + 1) * 256] for t in range(NT)]
                m0 = pe.matmul(acc[:, half, o0:o0 + 256], s[:, 0:P], v[0], start=True, stop=True)
                pe.matmul(acc[:, 2 + half, o0:o0 + 256], s[:, P:T], v[0], start=True, stop=False)
                m1 = pe.matmul(acc[:, 2 + half, o0:o0 + 256], s[:, T:T + P], v[1], start=False, stop=True)
                if hh % 2:
                    m0.then_inc(bank_full(half), fill(half, (l, "ro")))
                    m1.then_inc(bank_full(2 + half), fill(2 + half, (l, "ro")))
                else:
                    m1.then_inc(sem("head_out"), mark("head_out", (l, hh)))

            scores(0)
            for hh in range(4):
                if hh < 3:
                    scores(hh + 1)
                values(hh)
            pe.wait_ge(sem("ro_ready"), at("ro_ready", (l, 1)))
            pe_to_fm(ro, KC, (l, "ro"))
            pe_fm_wait((l, "ro"), KC)
            pe_rows_acc(cF, KC, (l, "ya"))

        def act_retention(l):
            for i in range(2):
                for t in range(NT):
                    act.wait_ge(bank_full(4 + t), filled_at(4 + t, (l, "rv", i)))
                    act.activation(rv[:, t, i * 512:(i + 1) * 512], bank(4 + t), ACT.Copy)\
                        .then_inc(sem("rv_ready"), mark_read("rv_ready", 4 + t, (l, "rv", i)))
            for i in range(2):
                for t in range(NT):
                    act.wait_ge(bank_full(4 + t), filled_at(4 + t, (l, "rg", i)))
                    act.activation(rg[:, t, i * 512:(i + 1) * 512], bank(4 + t), ACT.Silu)\
                        .then_inc(sem("rg_ready"), mark_read("rg_ready", 4 + t, (l, "rg", i)))
            act_gate(l, "ga", gA)
            for t in range(NT):
                for hh in range(4):
                    act.wait_ge(bank_full(2 * t + hh // 2), filled_at(2 * t + hh // 2, (l, "ro")))
                    m = act.activation(rj[:, t, hh * 256:(hh + 1) * 256],
                                       acc[:, 2 * t + hh // 2, (hh % 2) * 256:(hh % 2 + 1) * 256],
                                       ACT.Square, accum_out=ssq[:, 4 * t + hh:4 * t + hh + 1])
            m.then_inc(sem("sumsq"), mark("sumsq", (l, "ro")))
            act_roots((l, "ro"), 8)
            act_to_fm(cF, KC, (l, "ro"))

        def dve_retention(l):
            for i, name in enumerate(("rq", "rk")):
                for b in range(2):
                    dve.wait_ge(bank_full(4 + b), filled_at(4 + b, (l, name)))
                    n = 2 * i + b
                    dst = rqk[:, 4 * i + 2 * b:4 * i + 2 * b + 2, :]
                    x = split(bank(4 + b), 2)
                    for lo, hi in ((0, 64), (64, 128)):
                        V(dve.tensor_tensor(rtmp[lo:lo + 64, :, :] if lo else rtmp[0:64, :, :],
                                            x[64 - lo:128 - lo, :, :],
                                            bc(cst("sin")[64 - lo:128 - lo, :], 1, [64, 2, T]), ALU.mult))
                    dve.tensor_tensor(dst, x, bc(cst("cos"), 1, [P, 2, T]), ALU.mult)\
                        .then_inc(sem("cos_part"), mark_read("cos_part", 4 + b, (l, name)))
                    dve.wait_ge(sem("cos_part"), latest("cos_part"))
                    dve.tensor_tensor(dst, dst, rtmp[:, :, :], ALU.add)\
                        .then_inc(sem("rotated"), mark("rotated", (l, n)))
                    dve.wait_ge(sem("rotated"), latest("rotated"))
            for hh in range(4):
                b = 6 + hh % 2
                dve.wait_ge(bank_full(b), filled_at(b, (l, "rs", hh)))
                if hh >= 2:
                    if hh == 2:
                        dve.wait_ge(sem("head_out"), at("head_out", (l, 0)))
                    else:
                        dve.wait_ge(bank_full(2), filled_at(2, (l, "ro")))
                dec = cst(f"decay{hh}")
                dve.tensor_tensor(rS[hh % 2][:, 0:T], bank(b)[:, 0:T], dec, ALU.mult)\
                   .then_inc(sem("scores_part"), 1)
                m = dve.tensor_tensor(rS[hh % 2][:, T:T + P], bank(b)[:, T:T + P], dec[:, 0:P], ALU.mult)
                m.then_inc(sem("decayed_scores"), mark("decayed_scores", (l, hh)))
                was_read(b, (l, "rs", hh), "decayed_scores")
            dve_mean((l, "ro"), 8, 1.0 / 256, 1e-6)
            dve_recips((l, "ro"), 8)
            dve.wait_ge(sem("rg_ready"), at("rg_ready", ("read", 5, (l, "rg", 1))))
            for t in range(NT):
                x = acc[:, 2 * t:2 * t + 2, :].rearrange("p a (b n) -> p (a b) n", n=256)
                for b in range(2):
                    dve.wait_ge(bank_full(2 * t + b), filled_at(2 * t + b, (l, "ro")))
                dve.tensor_tensor(split(ro[:, t, :], 4), x, bc(rsd[:, 4 * t:4 * t + 4], 2, [P, 4, 256]),
                                       ALU.mult).then_inc(sem("ro_scaled"), mark_read("ro_scaled", 2 * t, (l, "ro")))
                was_read(2 * t + 1, (l, "ro"), "ro_scaled")
                dve.wait_ge(sem("ro_scaled"), latest("ro_scaled"))
                dve.tensor_tensor(ro[:, t, :], ro[:, t, :], rg[:, t, :], ALU.mult)\
                    .then_inc(sem("ro_ready"), mark("ro_ready", (l, t)))
            dve_merge(l, "ga", gA, (l, "ya"))

        hQ, hZ, hK, hB = (view(4096 + 2048 * i, 8, T) for i in range(4))
        hKT, hKS, hG = (view(12288 + 2048 * i, 8, T) for i in range(3))
        hV = view(18432, NT, D)
        hstate = view(6144, 16, P)
        hvx = [view(8192 + 1024 * i, 8, P) for i in range(2)]
        hksT, hAT = view(20480, NT, P), view(20736, NT, P)
        hdec = view(20992, 8, 16)
        gB = w2[:, 0, :, :]

        def flat(x):
            return x.rearrange("p a b -> p (a b)")

        def pe_hgrn(l):
            for name in ("hq", "hf"):
                for i in range(2):
                    pe_cols_fm(u, (l, name, i))
            for i in range(2):
                pe_cols_tm(u, (l, "hi", i))
            for i in range(2):
                pe_cols_fm(u, (l, "hg", i))
            pe_cols_tm(u, (l, "gb", 0))
            pe.wait_ge(sem("h_factors"), at("h_factors", l))
            for hh in range(8):
                claim(6)
                for t in range(NT):
                    m = pe.transpose(bank(6)[:, t * P:(t + 1) * P], hKS[:, hh, t * P:(t + 1) * P], cst("ident"))
                m.then_inc(bank_full(6), fill(6, (l, "ksT", hh)))
                claim(7)
                for t in range(NT):
                    m = pe.matmul(bank(7)[:, t * P:(t + 1) * P], hKT[:, hh, t * P:(t + 1) * P],
                                  hQ[:, hh, t * P:(t + 1) * P], start=True, stop=True)
                m.then_inc(bank_full(7), fill(7, (l, "AT", hh)))
                pe.wait_ge(sem("ksT"), at("ksT", (l, hh)))
                for t in range(NT):
                    pe.wait_ge(sem("vx"), at("vx", (l, hh, t)))
                    for half in range(2):
                        b = 2 * t + half
                        claim(b)
                        m = pe.matmul(bank(b), hksT[:, t, :], flat(hvx[t])[:, half * 512:(half + 1) * 512],
                                      start=True, stop=True)
                        m.then_inc(bank_full(b), fill(b, (l, "U", hh)))
                ob = 4 + hh % 2
                claim(ob)
                pe.wait_ge(sem("AT"), at("AT", (l, hh)))
                for t in range(NT):
                    pe.matmul(bank(ob)[:, t * P:(t + 1) * P], hV[:, t, hh * P:(hh + 1) * P], hAT[:, t, :],
                              start=True, stop=False, skip_group_check=True)
                    for j in range(max(8 * t, 1), 8 * t + 8):
                        if j in (1, 8):
                            pe.wait_ge(sem("hstate"), at("hstate", (l, hh, 7 if j == 1 else 15)))
                        m = pe.matmul(bank(ob)[:, 16 * j:16 * j + 16], hstate[:, j, :],
                                      hQ[:, hh, 16 * j:16 * j + 16], start=False, stop=(j == 8 * t + 7),
                                      skip_group_check=True)
                m.then_inc(bank_full(ob), fill(ob, (l, "ho", hh)))
            pe.wait_ge(sem("squared"), at("squared", (l, "ho")))
            for b in range(4):
                claim(b)
                m = pe.matmul(bank(b), cst("ones"), flat(hB)[:, b * 512:(b + 1) * 512], start=True, stop=True)
                m.then_inc(bank_full(b), fill(b, (l, "hsum")))
            pe_cols_tm(u, (l, "gb", 1))
            pe.wait_ge(sem("hgrn_out"), at("hgrn_out", l))
            pe_rows_acc(cF, KC, (l, "yb"))

        def act_hgrn(l):
            def gate_raw():
                for t in range(NT):
                    act.wait_ge(bank_full(4 + t), filled_at(4 + t, (l, "gb", 0)))
                    act.activation(gB[:, t, 0:512], bank(4 + t), ACT.Copy)\
                        .then_inc(sem("gate_raw"), mark_read("gate_raw", 4 + t, (l, "gb", 0)))

            for name, dst, fn in (("hq", hQ, ACT.Copy), ("hf", hZ, ACT.Copy)):
                for i in range(2):
                    for b in range(2):
                        act.wait_ge(bank_full(4 + b), filled_at(4 + b, (l, name, i)))
                        act.activation(dst[:, 4 * i + 2 * b:4 * i + 2 * b + 2, :], split(bank(4 + b), 2), fn)\
                            .then_inc(sem("hqf"), mark_read("hqf", 4 + b, (l, name, i)))
            act.wait_ge(sem("hqf"), latest("hqf"))
            A(act.activation(flat(hKT), flat(hZ), ACT.Abs))
            A(act.activation(flat(hKT), flat(hKT), ACT.Exp, scale=-1.0))
            act.activation(flat(hKT), flat(hKT), ACT.Ln, bias=1.0).then_inc(sem("soft"), mark("soft", (l, 0)))
            for i in range(2):
                for t in range(NT):
                    act.wait_ge(bank_full(4 + t), filled_at(4 + t, (l, "hi", i)))
                    act.activation(hV[:, t, i * 512:(i + 1) * 512], bank(4 + t), ACT.Copy)\
                        .then_inc(sem("hV"), mark_read("hV", 4 + t, (l, "hi", i)))
            act.wait_ge(sem("merging"), at("merging", ("read", 3, (l, "ya"))))
            for i in range(2):
                for b in range(2):
                    act.wait_ge(bank_full(4 + b), filled_at(4 + b, (l, "hg", i)))
                    act.activation(hG[:, 4 * i + 2 * b:4 * i + 2 * b + 2, :], split(bank(4 + b), 2), ACT.Silu)\
                        .then_inc(sem("hG"), mark_read("hG", 4 + b, (l, "hg", i)))
            act.wait_ge(sem("logk"), at("logk", l))
            act.activation(flat(hK), flat(hK), ACT.Exp).then_inc(sem("hK"), mark("hK", l))
            if l == 1:
                act.wait_ge(sem("logdiff"), at("logdiff", l))
                A(act.activation(flat(hKT), flat(hKT), ACT.Abs))
                A(act.activation(flat(hKT), flat(hKT), ACT.Exp, scale=-1.0))
                act.activation(flat(hKT), flat(hKT), ACT.Ln, bias=1.0).then_inc(sem("soft"), mark("soft", (l, 1)))
            act.wait_ge(sem("bcum"), at("bcum", l))
            act.activation(flat(hB), flat(hZ), ACT.Exp).then_inc(sem("expb"), mark("expb", (l, 0)))
            act.activation(flat(hKT), flat(hZ), ACT.Exp, scale=-1.0).then_inc(sem("expb"), mark("expb", (l, 1)))
            gate_raw()
            act.wait_ge(sem("to_block_end"), at("to_block_end", l))
            act.activation(flat(hKS), flat(hKS), ACT.Exp).then_inc(sem("expb"), mark("expb", (l, 2)))
            for hh in range(8):
                act.wait_ge(bank_full(6), filled_at(6, (l, "ksT", hh)))
                act.activation(flat(hksT), bank(6)[:, 0:T], ACT.Copy).then_inc(sem("ksT"), mark("ksT", (l, hh)))
                was_read(6, (l, "ksT", hh), "ksT")
                act.wait_ge(bank_full(4 + hh % 2), filled_at(4 + hh % 2, (l, "ho", hh)))
                act.activation(hQ[:, hh, :], bank(4 + hh % 2)[:, 0:T], ACT.Copy)\
                    .then_inc(sem("ho"), mark("ho", (l, hh)))
                was_read(4 + hh % 2, (l, "ho", hh), "ho")
            act.wait_ge(sem("ho"), latest("ho"))
            act.activation(flat(hB), flat(hQ), ACT.Square).then_inc(sem("squared"), mark("squared", (l, "ho")))
            act.wait_ge(sem("hvar"), at("hvar", (l, 3)))
            act.activation(flat(hKT), flat(hKT), ACT.Sqrt).then_inc(sem("hroot"), mark("hroot", l))
            act.wait_ge(sem("gate_raw"), latest("gate_raw"))
            for t in range(NT):
                act.activation(gB[:, t, 0:512], gB[:, t, 0:512], ACT.Sigmoid)\
                    .then_inc(sem("gate_ready"), mark("gate_ready", (l, "gb", 0, t)))
            for t in range(NT):
                act.wait_ge(bank_full(4 + t), filled_at(4 + t, (l, "gb", 1)))
                act.activation(gB[:, t, 512:1024], bank(4 + t), ACT.Sigmoid)\
                    .then_inc(sem("gate_ready"), mark_read("gate_ready", 4 + t, (l, "gb", 1)))

        def dve_hgrn(l):
            bcb = [P, 8, T]
            dve.wait_ge(sem("soft"), at("soft", (l, 0)))
            V(dve.scalar_tensor_tensor(out=flat(hB), in0=flat(hZ), scalar=0.0, in1=flat(hKT),
                                       op0=ALU.min, op1=ALU.subtract))
            if l == 0:
                dve.tensor_tensor(flat(hK), flat(hB), flat(hZ), ALU.subtract).then_inc(sem("logk"), mark("logk", l))
            else:
                V(dve.tensor_tensor(hB[:, :, :], hB[:, :, :], bc(lbC[:, 0:8], 2, bcb), ALU.add))
                dve.tensor_tensor(flat(hK), flat(hB), flat(hZ), ALU.subtract).then_inc(sem("logk"), mark("logk", l))
                dve.tensor_tensor(hKT[:, :, :], hB[:, :, :], bc(lbA[:, 0:8], 2, bcb), ALU.subtract)\
                    .then_inc(sem("logdiff"), mark("logdiff", l))
                V(dve.tensor_tensor(hB[:, :, :], hB[:, :, :], bc(lbA[:, 0:8], 2, bcb), ALU.max))
                dve.wait_ge(sem("soft"), at("soft", (l, 1)))
                V(dve.tensor_tensor(flat(hB), flat(hB), flat(hKT), ALU.add))
            V(dve.memset(flat(hKS), 1.0))
            V(dve.memset(flat(hKS).rearrange("p (a b) -> p a b", b=16)[:, :, 0:1], 0.0))
            dve.wait_ge(sem("logk"), latest("logk"))
            dve.tensor_tensor_scan(flat(hZ), flat(hKS), flat(hB), 0.0, ALU.mult, ALU.add)\
                .then_inc(sem("bcum"), mark("bcum", l))
            dve.wait_ge(sem("bcum"), latest("bcum"))
            blocks = flat(hZ).rearrange("p (a b) -> p a b", b=16)
            dve.tensor_tensor(flat(hKS).rearrange("p (a b) -> p a b", b=16),
                                        blocks[:, :, 15:16].broadcast_to([P, P, 16]), blocks, ALU.subtract)\
                                            .then_inc(sem("to_block_end"), mark("to_block_end", l))
            dve.wait_ge(sem("expb"), at("expb", (l, 0)))
            V(dve.tensor_copy(flat(hdec), flat(hB).rearrange("p (a b) -> p a b", b=16)[:, :, 15]))
            V(dve.tensor_tensor(flat(hQ), flat(hQ), flat(hB), ALU.mult))
            dve.wait_ge(sem("hK"), at("hK", l))
            dve.wait_ge(sem("expb"), at("expb", (l, 1)))
            V(dve.tensor_tensor(flat(hKT), flat(hKT), flat(hK), ALU.mult))
            dve.wait_ge(sem("expb"), at("expb", (l, 2)))
            dve.tensor_tensor(flat(hKS), flat(hKS), flat(hK), ALU.mult)\
                .then_inc(sem("h_factors"), mark("h_factors", l))
            dve.wait_ge(sem("h_factors"), latest("h_factors"))
            dve.wait_ge(sem("hV"), at("hV", ("read", 5, (l, "hi", 1))))
            for hh in range(8):
                for t in range(NT):
                    if hh:
                        dve.wait_ge(bank_full(2 * t + 1), filled_at(2 * t + 1, (l, "U", hh - 1)))
                    v = bc(hV[:, t, hh * P:(hh + 1) * P], 1, [P, 8, P])
                    dve.tensor_tensor(hvx[t][:, :, :], v, bc(cst("block"), 2, [P, 8, P]), ALU.mult)\
                        .then_inc(sem("vx"), mark("vx", (l, hh, t)))
                dve.wait_ge(bank_full(7), filled_at(7, (l, "AT", hh)))
                if hh:
                    dve.wait_ge(bank_full(4 + (hh - 1) % 2), filled_at(4 + (hh - 1) % 2, (l, "ho", hh - 1)))
                dve.tensor_tensor(hAT[:, :, :], split(bank(7)[:, 0:T], 2),
                                            bc(cst("blockcausal"), 1, [P, 2, P]), ALU.mult)\
                                                .then_inc(sem("AT"), mark("AT", (l, hh)))
                was_read(7, (l, "AT", hh), "AT")
                for j in range(1, 16):
                    dve.wait_ge(bank_full((j - 1) // 4), filled_at((j - 1) // 4, (l, "U", hh)))
                    U = bank((j - 1) // 4)[:, ((j - 1) % 4) * P:((j - 1) % 4 + 1) * P]
                    if j == 1:
                        m = dve.tensor_copy(hstate[:, j, :], U)
                    else:
                        m = dve.scalar_tensor_tensor(out=hstate[:, j, :], in0=hstate[:, j - 1, :],
                                                     scalar=hdec[:, hh, j - 1:j], in1=U, op0=ALU.mult, op1=ALU.add)
                    m.then_inc(sem("hstate"), mark("hstate", (l, hh, j)))
                    if j % 4 == 0 or j == 15:
                        was_read((j - 1) // 4, (l, "U", hh), "hstate")
                    dve.wait_ge(sem("hstate"), latest("hstate"))
            for b in range(4):
                dve.wait_ge(bank_full(b), filled_at(b, (l, "hsum")))
                dve.tensor_scalar(flat(hKT)[:, b * 512:(b + 1) * 512], bank(b), 1.0 / 128, 1e-6,
                                            ALU.mult, ALU.add).then_inc(sem("hvar"), mark("hvar", (l, b)))
                was_read(b, (l, "hsum"), "hvar")
            dve.wait_ge(sem("hroot"), at("hroot", l))
            V(dve.reciprocal(flat(hKT), flat(hKT)))
            V(dve.tensor_tensor(flat(hQ), flat(hQ), flat(hKT), ALU.mult))
            dve.wait_ge(sem("hG"), at("hG", ("read", 5, (l, "hg", 1))))
            dve.scalar_tensor_tensor(out=flat(cF), in0=flat(hQ), scalar=pcol("hgrn_norm_g_2", l),
                                               in1=flat(hG), op0=ALU.mult, op1=ALU.mult)\
                                                   .then_inc(sem("hgrn_out"), mark("hgrn_out", l))
            dve_merge(l, "gb", gB, (l, "yb"))

        wq, wk = view(4096, 8, T), view(6144, 4, T)
        wv = view(7168, NT, 256)
        wS = [view(7680 + 1024 * i, 1024) for i in range(2)]
        wP = [view(9728 + 1024 * i, 1024) for i in range(2)]
        wo = view(11776, NT, D)
        gC = view(13824, NT, D)
        HEAD_AT = (0, 2, 1, 3)
        UNITS_W = [(j, qt) for j in range(4) for qt in range(NT)]

        def pe_swa(l):
            for i in range(2):
                pe_cols_fm(u, (l, "sq", i))
            slot = arrived().rearrange("p (t n) -> p t n", n=COLS)
            for b in range(2):
                claim(4 + b)
                for c in range(2):
                    j = 2 * b + c
                    for rep in range(2):
                        for k in range(KC):
                            m = pe.matmul(bank(4 + b)[64 * rep:64 * rep + 64, c * T:(c + 1) * T],
                                          slot[:, k, j * 64:(j + 1) * 64], u[:, k, :],
                                          start=(k == 0), stop=(k == KC - 1))
                m.then_inc(bank_full(4 + b), fill(4 + b, (l, "sk")))
            claim(6)
            for t in range(NT):
                for k in range(KC):
                    m = pe.matmul(bank(6)[:, t * 256:(t + 1) * 256], u[:, k, t * P:(t + 1) * P],
                                  slot[:, k, 256:512], start=(k == 0), stop=(k == KC - 1))
            m.then_inc(bank_full(6), fill(6, (l, "sv")))
            released_last("bank_full6")
            pe_gate(l, "gc")
            pe.wait_ge(sem("w_ready"), at("w_ready", ("read", 6, (l, "sv"))))

            def scores(n):
                j, qt = UNITS_W[n]
                nk, b0 = (qt + 1) * P, 2 * (n % 2)
                claim(b0, b0 + 1)
                for r in range(4):
                    lo = 64 * (r % 2)
                    c0 = 256 * (r // 2)
                    m = pe.matmul(acc[:, b0 + r % 2, c0:c0 + nk],
                                  wq[lo:lo + 64, 2 * j + r // 2, qt * P:(qt + 1) * P],
                                  wk[lo:lo + 64, j, 0:nk], start=True, stop=True)
                m.then_inc(bank_full(b0), fill(b0, (l, "ws", n)))

            def values(n):
                j, qt = UNITS_W[n]
                b0, blocks = 2 * (n % 2), 4 * (qt + 1)
                tb = (duo, aux)[n % 2]
                pe.wait_ge(sem("w_probs"), at("w_probs", (l, n, 3)))
                claim(4 + 2 * (n % 2), 5 + 2 * (n % 2))
                for i in range(blocks):
                    m = pe.transpose(pair(tb[:, :, :], 1024)[:, i * P:(i + 1) * P], wS[n % 2][:, i * P:(i + 1) * P],
                                     cst("ident"))
                m.then_inc(bank_full(4 + 2 * (n % 2)), fill(4 + 2 * (n % 2), (l, "wt", n)))
                pe.wait_ge(sem("w_probsT"), at("w_probsT", (l, n)))
                for i in range(blocks):
                    r, kt = HEAD_AT[i // (qt + 1)], i % (qt + 1)
                    m = pe.matmul(acc[:, b0 + 1, r * 64:(r + 1) * 64], wP[n % 2][:, i * P:(i + 1) * P],
                                  wv[:, kt, j * 64:(j + 1) * 64], start=(kt == 0), stop=(kt == qt))
                m.then_inc(bank_full(b0 + 1), fill(b0 + 1, (l, "wo", n)))

            scores(0)
            for n in range(len(UNITS_W)):
                if n + 1 < len(UNITS_W):
                    scores(n + 1)
                values(n)
            pe.wait_ge(sem("wo_ready"), at("wo_ready", (l, len(UNITS_W) - 1)))
            pe_to_fm(wo, KC, (l, "wo"))
            pe_fm_wait((l, "wo"), KC)
            pe_rows_acc(cF, KC, (l, "yc"))
            pe.wait_ge(sem("merged"), at("merged", (l, "gc", 1)))
            pe_to_fm(merged, KC, (l, "merged"))
            pe_fm_wait((l, "merged"), KC)
            pe_rows_acc(cF, KC, ("mix", l))

        def act_swa(l):
            act.wait_ge(sem("merged"), at("merged", (l, "gb", 1)))
            for i in range(2):
                for b in range(2):
                    act.wait_ge(bank_full(4 + b), filled_at(4 + b, (l, "sq", i)))
                    act.activation(wq[:, 4 * i + 2 * b:4 * i + 2 * b + 2, :], split(bank(4 + b), 2), ACT.Copy)\
                        .then_inc(sem("w_ready"), mark_read("w_ready", 4 + b, (l, "sq", i)))
            for b in range(2):
                act.wait_ge(bank_full(4 + b), filled_at(4 + b, (l, "sk")))
                act.activation(wk[:, 2 * b:2 * b + 2, :], split(bank(4 + b), 2), ACT.Copy)\
                    .then_inc(sem("w_ready"), mark_read("w_ready", 4 + b, (l, "sk")))
            act.wait_ge(bank_full(6), filled_at(6, (l, "sv")))
            act.activation(wv[:, :, :], split(bank(6), 2), ACT.Copy)\
                .then_inc(sem("w_ready"), mark_read("w_ready", 6, (l, "sv")))
            act_gate(l, "gc", gC)
            for n, (j, qt) in enumerate(UNITS_W):
                nk, x = (qt + 1) * P, 4 * (n % 2)
                act.wait_ge(sem("w_negmax"), at("w_negmax", (l, n)))
                for r in range(4):
                    m = act.activation(wS[n % 2][:, r * nk:(r + 1) * nk], wS[n % 2][:, r * nk:(r + 1) * nk], ACT.Exp,
                                       bias=smax[:, 8 + x + r:9 + x + r], accum_out=ssum[:, x + r:x + r + 1])
                    m.then_inc(sem("w_probs"), mark("w_probs", (l, n, r)))
                act.wait_ge(sem("w_sink"), at("w_sink", (l, n)))
                act.activation(sinke[:, x:x + 4], sinke[:, x:x + 4], ACT.Exp)\
                    .then_inc(sem("w_sinke"), mark("w_sinke", (l, n)))
                b = 4 + 2 * (n % 2)
                act.wait_ge(bank_full(b), filled_at(b, (l, "wt", n)))
                act.activation(wP[n % 2][:, 0:4 * nk], pair((duo, aux)[n % 2][:, :, :], 4 * nk), ACT.Copy)\
                    .then_inc(sem("w_probsT"), mark("w_probsT", (l, n)))
                was_read(b, (l, "wt", n), "w_probsT")
            act_to_fm(cF, KC, (l, "wo"))
            act_to_fm(cF, KC, (l, "merged"))

        def dve_swa(l):
            def softmax(n):
                j, qt = UNITS_W[n]
                nk, b0, x = (qt + 1) * P, 2 * (n % 2), 4 * (n % 2)
                dve.wait_ge(bank_full(b0), filled_at(b0, (l, "ws", n)))
                if n >= 2:
                    dve.wait_ge(bank_full(4 + 2 * (n % 2)), filled_at(4 + 2 * (n % 2), (l, "wt", n - 2)))
                s4 = split(wS[n % 2][:, 0:4 * nk], 4)
                m = dve.scalar_tensor_tensor(out=s4, in0=split(pair(acc[:, b0:b0 + 2, :], 1024), 4)[:, :, 0:nk],
                                             scalar=0.125,
                                             in1=bc(cst(f"window{qt}"), 1, [P, 4, nk]), op0=ALU.mult, op1=ALU.add)
                m.then_inc(sem("w_biased"), mark_read("w_biased", b0, (l, "ws", n)))
                dve.wait_ge(sem("w_biased"), latest("w_biased"))
                V(dve.tensor_reduce(smax[:, x:x + 4], s4, AX.X, ALU.max))
                sk = sinks[:, 16 * l + 4 * j:16 * l + 4 * j + 4].rearrange("p (a b) -> p b a", a=2)
                V(dve.tensor_tensor(split(smax[:, x:x + 4], 2), split(smax[:, x:x + 4], 2), sk, ALU.max))
                dve.tensor_scalar(smax[:, 8 + x:12 + x], smax[:, x:x + 4], -1.0, None, ALU.mult)\
                    .then_inc(sem("w_negmax"), mark("w_negmax", (l, n)))
                dve.tensor_tensor(split(sinke[:, x:x + 4], 2), sk, split(smax[:, x:x + 4], 2), ALU.subtract)\
                    .then_inc(sem("w_sink"), mark("w_sink", (l, n)))

            def divide(n):
                j, qt = UNITS_W[n]
                x = 4 * (n % 2)
                dve.wait_ge(sem("w_sinke"), at("w_sinke", (l, n)))
                V(dve.tensor_tensor(ssum[:, x:x + 4], ssum[:, x:x + 4], sinke[:, x:x + 4], ALU.add))
                V(dve.reciprocal(ssum[:, x:x + 4], ssum[:, x:x + 4]))
                dve.wait_ge(bank_full(2 * (n % 2) + 1), filled_at(2 * (n % 2) + 1, (l, "wo", n)))
                def heads(v):
                    return v.rearrange("p (a b d) -> p a b d", a=2, b=2)
                m = dve.tensor_tensor(heads(wo[:, qt, j * 256:(j + 1) * 256]),
                                      heads(acc[:, 2 * (n % 2) + 1, 0:256]),
                                      bc(ssum[:, x:x + 4].rearrange("p (b a) -> p a b", a=2), 3, [P, 2, 2, 64]),
                                      ALU.mult)
                m.then_inc(sem("wo_ready"), mark("wo_ready", (l, n)))
                was_read(2 * (n % 2) + 1, (l, "wo", n), "wo_ready")

            softmax(0)
            for n in range(len(UNITS_W)):
                if n + 1 < len(UNITS_W):
                    softmax(n + 1)
                divide(n)
            dve_merge(l, "gc", gC, (l, "yc"))

        tmp1 = cols(1)
        chosen = cols(16)
        most = cols(1).bitcast(mybir.dt.int32)
        rtr = sb("rtr", [P, KC, NE])

        def pe_router():
            claim(4)
            for t in range(NT):
                for k in range(KC):
                    m = pe.matmul(bank(4)[:, t * NE:(t + 1) * NE], u[:, k, t * P:(t + 1) * P], rtr[:, k, :],
                                  start=(k == 0), stop=(k == KC - 1))
            m.then_inc(bank_full(4), fill(4, "router"))
            pe.wait_ge(sem("chosen"), at("chosen", 0))
            claim(5)
            c0, c1 = chosen[:, 0:NE], chosen[:, NE:2 * NE]
            pe.matmul(bank(5)[:, 0:NE], cst("upper"), c0, start=True, stop=True)
            pe.matmul(bank(5)[:, NE:2 * NE], cst("ones"), c0, start=True, stop=False)
            pe.matmul(bank(5)[:, NE:2 * NE], cst("upper"), c1, start=False, stop=True)
            pe.matmul(bank(5)[:, 2 * NE:3 * NE], cst("ones"), c0, start=True, stop=False)
            pe.matmul(bank(5)[:, 2 * NE:3 * NE], cst("ones"), c1, start=False, stop=True)\
              .then_inc(bank_full(5), fill(5, "places"))

        def act_router():
            act.wait_ge(sem("top_diff"), at("top_diff", 0))
            act.activation(prob[:, 0:2], prob[:, 0:2], ACT.Exp).then_inc(sem("top_exp"), mark("top_exp", 0))

        def dve_router():
            dve.wait_ge(bank_full(4), filled_at(4, "router"))
            dve.tensor_copy(logits, bank(4)[:, 0:16]).then_inc(sem("logits"), mark_read("logits", 4, "router"))
            dve.wait_ge(sem("logits"), latest("logits"))
            for t in range(NT):
                e = slice(8 * t, 8 * t + 8)
                V(dve.max(top[:, e], logits[:, e]))
                V(dve.max_index(topi[:, e], top[:, e], logits[:, e]))
            V(dve.tensor_copy(topf, topi))
            t2 = split(top, 2)
            dve.tensor_tensor(prob[:, 0:2], t2[:, :, 1], t2[:, :, 0], ALU.subtract)\
                .then_inc(sem("top_diff"), mark("top_diff", 0))
            dve.wait_ge(sem("top_exp"), at("top_exp", 0))
            V(dve.tensor_scalar(prob[:, 2:4], prob[:, 0:2], 1.0, None, ALU.add))
            V(dve.reciprocal(prob[:, 2:4], prob[:, 2:4]))
            V(dve.tensor_tensor(prob[:, 4:6], prob[:, 0:2], prob[:, 2:4], ALU.mult))
            for t in range(NT):
                e = slice(8 * t, 8 * t + 8)
                V(dve.tensor_scalar(top[:, e], cst("iota8"), topf[:, 8 * t:8 * t + 1], None, ALU.is_equal))
                V(dve.tensor_scalar(logits[:, e], cst("iota8"), topf[:, 8 * t + 1:8 * t + 2], None, ALU.is_equal))
            dve.tensor_tensor(chosen, top, logits, ALU.add).then_inc(sem("chosen"), mark("chosen", 0))
            for t in range(NT):
                e = slice(8 * t, 8 * t + 8)
                V(dve.tensor_scalar(gates[:, e], top[:, e], prob[:, 2 + t:3 + t], None, ALU.mult))
                V(dve.scalar_tensor_tensor(out=gates[:, e], in0=logits[:, e], scalar=prob[:, 4 + t:5 + t],
                                           in1=gates[:, e], op0=ALU.mult, op1=ALU.add))
            dve.wait_ge(bank_full(5), filled_at(5, "places"))
            V(dve.tensor_tensor(topf, bank(5)[:, 0:2 * NE], chosen, ALU.mult))
            V(dve.tensor_scalar(slot_of[:, :, :], split(topf, 2), -1.0, None, ALU.add))
            V(dve.tensor_copy(gate_of[:, :, :], split(gates, 2)))
            dve.tensor_reduce(tmp1, bank(5)[:, 2 * NE:3 * NE], AX.X, ALU.max)\
               .then_inc(sem("most"), mark_read("most", 5, "places"))
            dve.wait_ge(sem("most"), latest("most"))
            dve.tensor_copy(most, tmp1).then_inc(sem("most_tokens"), mark("most_tokens", 0))
            V(dve.scalar_tensor_tensor(out=split(gates, 2), in0=slot_of[:, :, :], scalar=float(SLOTS),
                                       in1=gate_of[:, :, :], op0=ALU.is_ge, op1=ALU.mult))
            if SLOTS < P:
                V(dve.tensor_tensor(gate_of[:, :, :], gate_of[:, :, :], split(gates, 2), ALU.subtract))

        stack = view(6144, STACKS, P)
        last_rows = STACK_ROWS - (STACKS - 1) * P

        def act_start():
            loads = [(dtb, a["ssm_dt_bias"][0].partition_broadcast(P)),
                     (alog, a["ssm_a_log"][0].partition_broadcast(P)),
                     (dskip, a["ssm_d"][0].partition_broadcast(P)),
                     (sinks, a["swa_sinks_2"].rearrange("l h -> (l h)").partition_broadcast(P)),
                     (rtr[:, :, :], a["moe_router_2"][0].rearrange("(t p) e -> p t e", p=P))]
            for name, n in STACK:
                v = a[name]
                v = v.rearrange({2: "a (c p) -> (a c) p", 3: "a b (c p) -> (a b c) p"}[len(v.shape)], p=P)
                row = 0
                while row < n:
                    pos = stack_at(name) + row
                    k = min(n - row, P - pos % P)
                    loads.append((stack[pos % P:pos % P + k, pos // P, :], v[row:row + k, :]))
                    row += k
            for dst, src in loads:
                act.dma_start(dst, src).then_inc(sem("start_loads"), 16)
            ev.seen[("start_loads", 0)] = 16 * (len(loads) + 2)
            act.wait_ge(sem("start_loads"), 16 * (len(loads) + 2))
            act.wait_ge(bank_full(6), filled_at(6, "stack"))
            act.activation(par[:, 0:STACK_ROWS], bank(6)[:, 0:STACK_ROWS], ACT.Copy)\
                .then_inc(sem("par"), mark("par", 0))
            was_read(6, "stack", "par")
            act.wait_ge(sem("par"), latest("par"))
            act.wait_ge(sem("lb_diff"), at("lb_diff", 0))
            A(act.activation(lb1[:, 0:8], lbd, ACT.Abs))
            A(act.activation(lb1[:, 0:8], lb1[:, 0:8], ACT.Exp, scale=-1.0))
            act.activation(lb1[:, 0:8], lb1[:, 0:8], ACT.Ln, bias=1.0).then_inc(sem("lb_soft"), mark("lb_soft", 0))

        def pe_start():
            pe.wait_ge(sem("start_loads"), at("start_loads", 0))
            for s in range(STACKS):
                k = P if s < STACKS - 1 else last_rows
                m = pe.transpose(bank(6)[:, s * P:s * P + k], stack[0:k, s, :], cst("ident")[0:k, 0:k])
            m.then_inc(bank_full(6), fill(6, "stack"))

        def dve_start():
            dve.wait_ge(sem("par"), at("par", 0))
            lb = stack_at("hgrn_lower_bounds_2")
            dve.tensor_tensor(lbd, par[:, lb + 8:lb + 16], par[:, lb:lb + 8], ALU.subtract)\
                .then_inc(sem("lb_diff"), mark("lb_diff", 0))
            dve.wait_ge(sem("lb_diff"), latest("lb_diff"))
            V(dve.tensor_scalar(lb2[:, 0:8], lbd, 0.0, None, ALU.min))
            V(dve.tensor_scalar(lb3[:, 0:8], lbd, -1.0, 0.0, ALU.mult, ALU.min))
            dve.wait_ge(sem("lb_soft"), at("lb_soft", 0))
            V(dve.tensor_tensor(lbA[:, 0:8], lb2[:, 0:8], lb1[:, 0:8], ALU.subtract))
            V(dve.tensor_tensor(lbC[:, 0:8], lb3[:, 0:8], lb1[:, 0:8], ALU.subtract))
            dve.wait_ge(sem("start_loads"), at("start_loads", 0))
            dve.tensor_copy(tmp1, lbA[:, 0:1]).then_inc(sem("h_ready"), mark("h_ready", ("ffn00", "pre")))

        FIRST = [("ffn00", 0, 0, 0.5), ("mixA", 0, 2, 1.0), ("ffn01", 0, 4, 0.5),
                 ("ffn10", 1, 0, 0.5), ("mixB", 1, 2, 1.0), ("ffn11", 1, 4, 0.5)]

        block = ctx.enter_context(nc.Block())

        def pe_h_to_fm(key):
            pe.wait_ge(sem("h_ready"), at("h_ready", key))
            pe_to_fm(h, KC, key)
            pe_fm_wait(key, KC)

        @block.tensor
        def _(_e):
            pe_start()
            for key, layer, g, _ in FIRST:
                if key == "mixA":
                    pe_prenorm((key, "pre"))
                    pe_mixer_a()
                elif key == "mixB":
                    pe_prenorm((key, "pre"))
                    pe_mixer_b()
                else:
                    pe.wait_ge(sem("normed"), at("normed", ((key, "pre"), 1)))
                    pe_to_fm(hn, KC, (key, "pre"))
                    pe_dense(key, (key, "pre"), FFB, 4)
            for l in range(2):
                pe_h_to_fm(("h", l))
                pe_retention(l)
                pe_hgrn(l)
                pe_swa(l)
                if l == 0:
                    pe.wait_ge(sem("h_ready"), at("h_ready", ("f", l)))
                    pe_to_fm(h, KC, ("f", l))
                    pe_dense(("ff", 0), ("f", l), FFB, 4)
                else:
                    pe_h_to_fm(("f", l))
                    pe_router()
                    pe_moe()
                    with pe.If(overflows(pe)):
                        pe_ffn("over", NE * MOEB, NE)

        @block.scalar
        def _(_e):
            act_start()
            for key, layer, g, _ in FIRST:
                if key == "mixA":
                    act_prenorm((key, "pre"), 6 * layer + g)
                    act_mixer_a()
                elif key == "mixB":
                    act_prenorm((key, "pre"), 6 * layer + g)
                    act_mixer_b()
                else:
                    act_dense_prenorm(key, 6 * layer + g)
                    act_dense(key, FFB, 4)
                act_postnorm(key)
            act_roots("ln_in", 2)
            for l in range(2):
                act_to_fm(u, KC, ("h", l))
                act_retention(l)
                act_hgrn(l)
                act_swa(l)
                act_roots(("mix", l), 2)
                if l == 0:
                    act_first_unit(("ff", 0))
                    act_to_fm_split(("f", l))
                    act_unit(("ff", 0), 1, 0, 0, 4)
                    act_dense(("ff", 0), FFB, 4)
                else:
                    act_to_fm(u, KC, ("f", l))
                    for x in range(3):
                        ev.start(f"unit_hi{x}", "moe")
                    act_unit("moe", 0, 0, 0, BODY)
                    act_unit("moe", 1, 0, 0, BODY)
                    act_router()
                    act_moe()
                    with act.If(overflows(act)):
                        act_ffn("over", NE * MOEB, NE)
                act_roots(("ff", l), 2)

        @block.vector
        def _(_e):
            dve_start()
            for n, (key, layer, g, factor) in enumerate(FIRST):
                if key == "mixA":
                    dve_prenorm((key, "pre"))
                    dve_mixer_a()
                elif key == "mixB":
                    dve_prenorm((key, "pre"))
                    dve_mixer_b()
                else:
                    dve_dense_prenorm(key, 6 * layer + g)
                    dve_dense(key, FFB, 4)
                dve_postnorm(key, factor, (FIRST[n + 1][0], "pre") if n + 1 < len(FIRST) else "ln_in")
            dve_layernorm("ln_in", False, ("h", 0))
            for l in range(2):
                dve_retention(l)
                dve_hgrn(l)
                dve_swa(l)
                dve_layernorm(("mix", l), True, ("f", l))
                if l == 0:
                    for x in range(3):
                        ev.start(f"unit_split{x}", ("ff", 0))
                    dve_unit(("ff", 0), 0, 0, 0, 4)
                    dve_to_fm_split(("f", 0))
                    dve_unit(("ff", 0), 1, 0, 0, 4)
                    dve_dense(("ff", 0), FFB, 4)
                    dve_layernorm(("ff", 0), True, ("h", 1))
                else:
                    for x in range(3):
                        ev.start(f"unit_split{x}", "moe")
                    dve_unit("moe", 0, 0, 0, BODY)
                    dve_unit("moe", 1, 0, 0, BODY)
                    dve_router()
                    dve_moe()
                    dve_layernorm(("ff", 1), "experts", ("h", 2))

        @block.gpsimd
        def _(_e):
            prev = None
            for n, (key, layer, g, _) in enumerate(FIRST):
                pool_rows(key, prev, a["norm_g"][layer, g + 1])
                prev = (FIRST[n + 1][0], "pre") if n + 1 < len(FIRST) else "ln_in"
            pool_rows("ln_in", prev, a["ln_in_g_2"], a["ln_in_b_2"])
            prev = ("h", 0)
            for l in range(2):
                pool_rows(("mix", l), prev, a["ln_mix_g_2"][l], a["ln_mix_b_2"][l])
                pool_rows(("ff", l), ("f", l), a["ln_ffn_g_2"][l], a["ln_ffn_b_2"][l])
                prev = ("h", l + 1)

        @block.sync
        def _(_e):
            sp.dma_start(con[:, :], consts).then_inc(sem("start_loads"), 16)
            sp.dma_start(h[:, :, :], a["x"][0].rearrange("(t p) d -> p t d", p=P)).then_inc(sem("start_loads"), 16)
            sp.wait_ge(sem("start_loads"), at("start_loads", 0))
            for key, layer, g, _ in FIRST:
                if key == "mixA":
                    w = a["hyb_w_in"][0]
                    sp.wait_ge(sem("h_ready"), at("h_ready", ("mixA", "pre")))
                    sp.dma_start(wdt[:, :, :], w[:, 4608:4624].rearrange("(t p) n -> p t n", p=P))\
                      .then_inc(sem("wdt_landed"), 16)
                    load(*[col_block(w, c) for _, _, c in KEYS_A])
                    load(*[col_block(w, 3072 + 512 * i) for i in range(3)])
                    load(*[col_block(w, 2048 + 512 * i) for i in range(2)])
                    load(*[row_block(a["hyb_w_out"][0], 512 * i) for i in range(4)])
                elif key == "mixB":
                    load(*[col_block(a["attn_w_qkv"][0], 512 * i) for i in range(9)])
                    load(row_block(a["attn_w_o"][0], 0))
                else:
                    w = a["ffn_w1"][layer, g // 4]
                    sp_dense(key, FFB, 4, *dense_sources(w[:, 0:FF], w[:, FF:2 * FF], a["ffn_w2"][layer, g // 4], 4))
            for l in range(2):
                w = a["w_in_2"][l]

                def wcols(*starts):
                    load(*[col_block(w, c) for c in starts])
                wcols(0, 512, 1024, 1536, 2048, 2560, 8704, 9216)
                load(*[row_block(a["ret_w_out_2"][l], 512 * i) for i in range(2)])
                wcols(3072, 3584, 4096, 4608, 5120, 5632, 6144, 6656, 9728, 10240)
                load(*[row_block(a["hgrn_w_out_2"][l], 512 * i) for i in range(2)])
                wcols(7168, 7680, 8192, 10752, 11264)
                load(*[row_block(a["swa_w_out_2"][l], 512 * i) for i in range(2)])
                load(*[row_block(a["w_o_2"][l], 512 * i) for i in range(2)])
                if l == 0:
                    sp_dense(("ff", l), FFB, 4, *dense_sources(a["ffn_w_gate_2"][0], a["ffn_w_up_2"][0],
                                                               a["ffn_w_down_2"][0], 4))
                else:
                    experts = a["moe_w_gate_2"][0], a["moe_w_up_2"][0], a["moe_w_down_2"][0]
                    sp_moe(*experts)
                    with sp.If(overflows(sp)):
                        sp_ffn("over", NE * MOEB, NE, *moe_sources(*experts))
            sp.wait_ge(sem("h_ready"), at("h_ready", ("h", 2)))
            sp.dma_start(out[0].rearrange("(t p) d -> p t d", p=P), h[:, :, :]).then_inc(sem("stored"), 16)
            sp.wait_ge(sem("stored"), 16)
    return ev.seen


INS = ["x", "norm_g", "ffn_w1", "ffn_w2", "hyb_w_in", "conv_dw_w", "conv_dw_b", "conv_ln_g", "conv_ln_b",
       "ssm_conv_w", "ssm_conv_b", "ssm_dt_bias", "ssm_a_log", "ssm_d", "ssm_norm_g", "hyb_w_out", "attn_w_qkv",
       "attn_w_o", "ln_in_g_2", "ln_in_b_2", "w_in_2", "ret_w_out_2", "hgrn_lower_bounds_2", "hgrn_norm_g_2",
       "hgrn_w_out_2", "swa_sinks_2", "swa_w_out_2", "w_o_2", "ln_mix_g_2", "ln_mix_b_2", "ffn_w_gate_2",
       "ffn_w_up_2", "ffn_w_down_2", "moe_router_2", "moe_w_gate_2", "moe_w_up_2", "moe_w_down_2", "ln_ffn_g_2",
       "ln_ffn_b_2"]


def program(nc, shapes, known):
    a = {n: nc.dram_tensor(f"in_{n}_dram", s, F32, kind="ExternalInput").ap() for n, s in shapes.items()}
    _, ccols = const_layout()
    consts = nc.dram_tensor("in_consts_dram", (P, ccols), F32, kind="ExternalInput").ap()
    out = nc.dram_tensor("out_0_dram", (1, T, D), F32, kind="ExternalOutput").ap()
    return build(nc, a, out, consts, known)


def kernel(**inputs):
    import concourse.bacc as bacc
    from concourse.bass_utils import run_bass_kernel_spmd

    arrays = {f"in_{n}_dram": np.ascontiguousarray(inputs[n]) for n in INS}
    shapes = {n: inputs[n].shape for n in INS}
    arrays["in_consts_dram"] = np.concatenate(list(shape_constants().values()), 1)
    counts = program(bacc.Bacc("TRN2", target_bir_lowering=False, num_devices=1), shapes, {})
    nc = bacc.Bacc("TRN2", target_bir_lowering=False, num_devices=1)
    program(nc, shapes, counts)
    r = run_bass_kernel_spmd(nc, [arrays], core_ids=[0])
    return r.results[0]["out_0_dram"]
```
